# Optimizing a Trainium2 kernel written in Bass

```python
import math
import jax, jax.numpy as jnp
from jax import lax
import numpy as np

D_MODEL = 1024
BATCH = 1
SEQ = 1024
DEPTH = 1
DEC_BATCH = 8
DEC_SEQ = 4
PAST_LEN = 4096
PAGE_SIZE = 128

N_MEM = 256
EPS = 1e-6
A_HEADS = 8
A_KV_HEADS = 2
A_GROUP = A_HEADS // A_KV_HEADS
A_HD = 64
WINDOW = 128
A_BLOCK = 128
N_BUCKETS = 32
MAX_DISTANCE = 128
B_HEADS = 4
B_DK = 64
B_DV = 128
B_RANK = 16
B_TAU = 16.0
B_CHUNK = 64
C_HEADS = 4
C_HD = 128
P_HEADS = 8
P_NKEYS = 128
P_DKEY = 256
P_TOPK = 16
P_EXPERTS = P_NKEYS * P_NKEYS
P_BLOCK = 256

A_W = A_HEADS * A_HD
A_KVW = A_KV_HEADS * A_HD
B_KW = B_HEADS * B_DK
B_VW = B_HEADS * B_DV
C_W = C_HEADS * C_HD
N_BRANCH = 3
IN_SIZES = (A_W, A_KVW, A_KVW, B_KW, B_KW, B_VW, B_RANK, B_VW, C_W, N_BRANCH * D_MODEL)
IN_OFFSETS = [int(o) for o in np.cumsum(IN_SIZES)[:-1]]
IN_WIDTH = int(sum(IN_SIZES))

kernel_name = 'hybrid_swa_gla_mem_peer_step'

def rmsnorm(x, g):
    xf = x.astype(jnp.float32)
    y = xf * lax.rsqrt(jnp.mean(xf * xf, axis=-1, keepdims=True) + EPS)
    return (y * g.astype(jnp.float32)).astype(x.dtype)

def t5_bucket(dist):
    n = jnp.maximum(dist, 0)
    max_exact = N_BUCKETS // 2
    nf = jnp.maximum(n, 1).astype(jnp.float32)
    large = max_exact + (jnp.log(nf / max_exact) / math.log(MAX_DISTANCE / max_exact)
                         * (N_BUCKETS - max_exact)).astype(jnp.int32)
    large = jnp.minimum(large, N_BUCKETS - 1)
    return jnp.where(n < max_exact, n, large)

def rel_bias_heads(rel_bias, dist):
    q, s = dist.shape
    b = rel_bias.astype(jnp.float32)[t5_bucket(dist)]
    return jnp.transpose(b, (2, 0, 1)).reshape(A_KV_HEADS, A_GROUP, q, s)

def sink_probs(scores, valid, sinks):
    scores = jnp.where(valid, scores, -jnp.inf)
    m = jnp.maximum(jnp.max(scores, axis=-1), sinks)
    p = jnp.exp(scores - m[..., None])
    return p / (jnp.sum(p, axis=-1) + jnp.exp(sinks - m))[..., None]

def window_attn_prompt(q, k, v, sinks, rel_bias):
    B, T = q.shape[:2]
    nb = T // A_BLOCK
    qb = q.reshape(B, nb, A_BLOCK, A_KV_HEADS, A_GROUP, A_HD)
    kc = k.reshape(B, nb, A_BLOCK, A_KV_HEADS, A_HD)
    vc = v.reshape(B, nb, A_BLOCK, A_KV_HEADS, A_HD)
    prev = lambda t: jnp.pad(t[:, :-1], ((0, 0), (1, 0), (0, 0), (0, 0), (0, 0)))
    kb = jnp.concatenate([prev(kc), kc], axis=2)
    vb = jnp.concatenate([prev(vc), vc], axis=2)
    qi = jnp.arange(A_BLOCK)[:, None]
    kj = jnp.arange(2 * A_BLOCK)[None, :]
    dist = qi + A_BLOCK - kj
    band = (dist >= 0) & (dist < WINDOW)
    bias = rel_bias_heads(rel_bias, dist)
    in_cur = kj >= A_BLOCK
    snk = sinks.astype(jnp.float32).reshape(A_KV_HEADS, A_GROUP, 1)
    scale = A_HD ** -0.5

    def one_block(args):
        qblk, kblk, vblk, idx = args
        valid = band & ((idx > 0) | in_cur)
        s = jnp.einsum('bqkgd,bskd->bkgqs', qblk, kblk, preferred_element_type=jnp.float32) * scale + bias
        p = sink_probs(s, valid, snk)
        return jnp.einsum('bkgqs,bskd->bqkgd', p.astype(vblk.dtype), vblk)

    out = lax.map(one_block, (qb.swapaxes(0, 1), kb.swapaxes(0, 1), vb.swapaxes(0, 1), jnp.arange(nb)))
    return out.swapaxes(0, 1).reshape(B, T, A_W)

def window_attn_sample(q, k, v, k_cache, v_cache, sinks, rel_bias):
    B, T = q.shape[:2]
    wc = k_cache.shape[1]
    kk = jnp.concatenate([k_cache.astype(k.dtype), k], axis=1)
    vv = jnp.concatenate([v_cache.astype(v.dtype), v], axis=1)
    dist = (wc + jnp.arange(T))[:, None] - jnp.arange(wc + T)[None, :]
    valid = (dist >= 0) & (dist < WINDOW)
    bias = rel_bias_heads(rel_bias, dist)
    snk = sinks.astype(jnp.float32).reshape(A_KV_HEADS, A_GROUP, 1)
    qg = q.reshape(B, T, A_KV_HEADS, A_GROUP, A_HD)
    s = jnp.einsum('bqkgd,bskd->bkgqs', qg, kk, preferred_element_type=jnp.float32) * A_HD ** -0.5 + bias
    p = sink_probs(s, valid, snk)
    o = jnp.einsum('bkgqs,bskd->bqkgd', p.astype(vv.dtype), vv).reshape(B, T, A_W)
    return o, kk[:, -wc:], vv[:, -wc:]

def gla_chunk(S, inp):
    q, k, v, g = inp
    C = q.shape[1]
    b = jnp.cumsum(g, axis=1)
    o_inter = jnp.einsum('bthk,bhkv->bthv', q * jnp.exp(b), S)
    causal = jnp.tril(jnp.ones((C, C), dtype=bool))[None, :, :, None, None]
    decay = jnp.exp(jnp.where(causal, b[:, :, None] - b[:, None, :], -jnp.inf))
    attn = jnp.einsum('bthk,bshk,btshk->bhts', q, k, decay)
    o_intra = jnp.einsum('bhts,bshv->bthv', attn, v)
    b_last = b[:, -1]
    S_new = jnp.exp(b_last)[..., None] * S + jnp.einsum('bshk,bshv->bhkv', k * jnp.exp(b_last[:, None] - b), v)
    return S_new, o_inter + o_intra

def gla_branch(xq, xk, xv, xlr, xr, S0, w2, gbias, gn_g):
    B, T = xq.shape[:2]
    f32 = jnp.float32
    q = xq.reshape(B, T, B_HEADS, B_DK).astype(f32) * B_DK ** -0.5
    k = xk.reshape(B, T, B_HEADS, B_DK).astype(f32)
    v = xv.reshape(B, T, B_HEADS, B_DV).astype(f32)
    g = (jax.nn.log_sigmoid((xlr @ w2 + gbias).astype(f32)) / B_TAU).reshape(B, T, B_HEADS, B_DK)
    C = math.gcd(T, B_CHUNK)
    nc = T // C
    chunks = lambda t: t.reshape(B, nc, C, *t.shape[2:]).swapaxes(0, 1)
    S, o = lax.scan(gla_chunk, S0.astype(f32), (chunks(q), chunks(k), chunks(v), chunks(g)))
    o = o.swapaxes(0, 1).reshape(B, T, B_HEADS, B_DV)
    o = rmsnorm(o, gn_g).reshape(B, T, B_VW).astype(xr.dtype) * jax.nn.silu(xr)
    return o, S

def memory_kv(mem, norm_g, w_kv, knorm_g):
    B, N, _ = mem.shape
    mk, mv = jnp.split(rmsnorm(mem, norm_g) @ w_kv, 2, axis=-1)
    return rmsnorm(mk.reshape(B, N, C_HEADS, C_HD), knorm_g), mv.reshape(B, N, C_HEADS, C_HD)

def memory_attn(q, mk, mv):
    s = jnp.einsum('bthd,bnhd->bhtn', q, mk.astype(q.dtype), preferred_element_type=jnp.float32) * C_HD ** -0.5
    p = jax.nn.softmax(s, axis=-1)
    return jnp.einsum('bhtn,bnhd->bthd', p.astype(q.dtype), mv.astype(q.dtype))

def peer_ffn(xn, wq, k1, k2, u_tab, v_tab):
    B, T, D = xn.shape
    n = B * T
    nblk = -(-n // P_BLOCK)
    xt = jnp.pad(xn.reshape(n, D), ((0, nblk * P_BLOCK - n), (0, 0))).reshape(nblk, P_BLOCK, D)
    half = P_DKEY // 2
    k1f = k1.astype(jnp.float32)
    k2f = k2.astype(jnp.float32)

    def one_block(xb):
        q = (xb @ wq).astype(jnp.float32).reshape(P_BLOCK, P_HEADS, 2, half)
        s1 = jnp.einsum('thd,nd->thn', q[:, :, 0], k1f)
        s2 = jnp.einsum('thd,nd->thn', q[:, :, 1], k2f)
        v1, i1 = lax.top_k(s1, P_TOPK)
        v2, i2 = lax.top_k(s2, P_TOPK)
        cand = (v1[..., :, None] + v2[..., None, :]).reshape(P_BLOCK, P_HEADS, P_TOPK * P_TOPK)
        cidx = (i1[..., :, None] * P_NKEYS + i2[..., None, :]).reshape(P_BLOCK, P_HEADS, P_TOPK * P_TOPK)
        sc, sel = lax.top_k(cand, P_TOPK)
        eidx = jnp.take_along_axis(cidx, sel, axis=-1)
        gate = jax.nn.softmax(sc, axis=-1)
        hid = jnp.einsum('thkd,td->thk', u_tab[eidx], xb, preferred_element_type=jnp.float32)
        act = (jax.nn.gelu(hid, approximate=False) * gate).astype(xb.dtype)
        return jnp.einsum('thk,thkd->td', act, v_tab[eidx])

    out = lax.map(one_block, xt).reshape(nblk * P_BLOCK, D)[:n]
    return out.reshape(B, T, D)

def decoder_layer(x, p, rel_bias, mem_k, mem_v, win_k, win_v, gla_state):
    B, T, _ = x.shape
    xn = rmsnorm(x, p['norm1_g'])
    aq, ak, av, bq, bk, bv, blr, br, cq, gl = jnp.split(xn @ p['w_in'], IN_OFFSETS, axis=-1)
    aq = rmsnorm(aq.reshape(B, T, A_HEADS, A_HD), p['a_qnorm_g'])
    ak = rmsnorm(ak.reshape(B, T, A_KV_HEADS, A_HD), p['a_knorm_g'])
    av = av.reshape(B, T, A_KV_HEADS, A_HD)
    if win_k is None:
        oa = window_attn_prompt(aq, ak, av, p['a_sinks'], rel_bias)
        new_wk, new_wv = ak[:, -WINDOW:], av[:, -WINDOW:]
        gla_state = jnp.zeros((B, B_HEADS, B_DK, B_DV), jnp.float32)
    else:
        oa, new_wk, new_wv = window_attn_sample(aq, ak, av, win_k, win_v, p['a_sinks'], rel_bias)
    ob, new_S = gla_branch(bq, bk, bv, blr, br, gla_state, p['b_gate_w2'], p['b_gate_b'], p['b_gn_g'])
    cq = rmsnorm(cq.reshape(B, T, C_HEADS, C_HD), p['c_qnorm_g'])
    oc = memory_attn(cq, mem_k, mem_v).reshape(B, T, C_W)
    ga, gb, gc = jnp.split(jax.nn.sigmoid((gl + p['b_gates']).astype(jnp.float32)).astype(x.dtype), N_BRANCH, axis=-1)
    merged = ga * (oa @ p['w_br_a']) + gb * (ob @ p['w_br_b']) + gc * (oc @ p['w_br_c'])
    h = x + merged @ p['w_out']
    y = h + peer_ffn(rmsnorm(h, p['norm2_g']), p['peer_wq'], p['peer_k1'], p['peer_k2'], p['peer_u'], p['peer_v'])
    return y, new_wk, new_wv, new_S.astype(x.dtype)

def setup_inputs(seed: int = 0) -> dict:
    key = jax.random.key(seed)
    keys = jax.random.split(key, 40)
    ctr = [0]

    def nrm(shape, scale):
        k = keys[ctr[0]]
        ctr[0] += 1
        return jax.random.normal(k, shape, jnp.float32) * scale

    def gain(shape):
        return 1.0 + nrm(shape, 0.02)

    wc = min(WINDOW, PAST_LEN)
    L = DEPTH
    D = D_MODEL
    return {
        'x_prompt': nrm((BATCH, SEQ, D), 1.0),
        'x_sample': nrm((DEC_BATCH, DEC_SEQ, D), 1.0),
        'mem_prompt': nrm((BATCH, N_MEM, D), 1.0),
        'cache_win_k': nrm((L, DEC_BATCH, wc, A_KV_HEADS, A_HD), 1.0),
        'cache_win_v': nrm((L, DEC_BATCH, wc, A_KV_HEADS, A_HD), 1.0),
        'state_gla': nrm((L, DEC_BATCH, B_HEADS, B_DK, B_DV), 0.5),
        'cache_mem_k': nrm((L, DEC_BATCH, N_MEM, C_HEADS, C_HD), 1.0),
        'cache_mem_v': nrm((L, DEC_BATCH, N_MEM, C_HEADS, C_HD), 1.0),
        'norm1_g': gain((L, D)),
        'w_in': nrm((L, D, IN_WIDTH), D ** -0.5),
        'b_gates': nrm((L, N_BRANCH * D), 0.01),
        'a_qnorm_g': gain((L, A_HD)),
        'a_knorm_g': gain((L, A_HD)),
        'a_sinks': nrm((L, A_HEADS), 0.5),
        'rel_bias': nrm((N_BUCKETS, A_HEADS), 0.1),
        'b_gate_w2': nrm((L, B_RANK, B_KW), B_RANK ** -0.5),
        'b_gate_b': nrm((L, B_KW), 0.1),
        'b_gn_g': gain((L, B_DV)),
        'c_qnorm_g': gain((L, C_HD)),
        'c_knorm_g': gain((L, C_HD)),
        'mem_norm_g': gain((L, D)),
        'w_mem_kv': nrm((L, D, 2 * C_W), D ** -0.5),
        'w_br_a': nrm((L, A_W, D), A_W ** -0.5),
        'w_br_b': nrm((L, B_VW, D), B_VW ** -0.5),
        'w_br_c': nrm((L, C_W, D), C_W ** -0.5),
        'w_out': nrm((L, D, D), D ** -0.5),
        'norm2_g': gain((L, D)),
        'peer_wq': nrm((L, D, P_HEADS * P_DKEY), D ** -0.5),
        'peer_k1': nrm((L, P_NKEYS, P_DKEY // 2), (P_DKEY // 2) ** -0.5),
        'peer_k2': nrm((L, P_NKEYS, P_DKEY // 2), (P_DKEY // 2) ** -0.5),
        'peer_u': nrm((L, P_EXPERTS, D), D ** -0.5),
        'peer_v': nrm((L, P_EXPERTS, D), 0.5),
    }

def reference(x_prompt, x_sample, mem_prompt, cache_win_k, cache_win_v, state_gla, cache_mem_k, cache_mem_v,
              norm1_g, w_in, b_gates, a_qnorm_g, a_knorm_g, a_sinks, rel_bias, b_gate_w2, b_gate_b, b_gn_g,
              c_qnorm_g, c_knorm_g, mem_norm_g, w_mem_kv, w_br_a, w_br_b, w_br_c, w_out, norm2_g,
              peer_wq, peer_k1, peer_k2, peer_u, peer_v):
    y_p, y_s = x_prompt, x_sample
    wk_p, wv_p, s_p, mk_p, mv_p, wk_s, wv_s, s_s = [], [], [], [], [], [], [], []
    for l in range(DEPTH):
        p = dict(norm1_g=norm1_g[l], w_in=w_in[l], b_gates=b_gates[l], a_qnorm_g=a_qnorm_g[l],
                 a_knorm_g=a_knorm_g[l], a_sinks=a_sinks[l], b_gate_w2=b_gate_w2[l], b_gate_b=b_gate_b[l],
                 b_gn_g=b_gn_g[l], c_qnorm_g=c_qnorm_g[l], w_br_a=w_br_a[l], w_br_b=w_br_b[l],
                 w_br_c=w_br_c[l], w_out=w_out[l], norm2_g=norm2_g[l], peer_wq=peer_wq[l],
                 peer_k1=peer_k1[l], peer_k2=peer_k2[l], peer_u=peer_u[l], peer_v=peer_v[l])
        mk, mv = memory_kv(mem_prompt, mem_norm_g[l], w_mem_kv[l], c_knorm_g[l])
        y_p, nk, nv, ns = decoder_layer(y_p, p, rel_bias, mk, mv, None, None, None)
        wk_p.append(nk); wv_p.append(nv); s_p.append(ns); mk_p.append(mk); mv_p.append(mv)
        y_s, nk, nv, ns = decoder_layer(y_s, p, rel_bias, cache_mem_k[l], cache_mem_v[l],
                                        cache_win_k[l], cache_win_v[l], state_gla[l])
        wk_s.append(nk); wv_s.append(nv); s_s.append(ns)
    new_win_k_prompt = jnp.stack(wk_p)
    new_win_v_prompt = jnp.stack(wv_p)
    new_gla_prompt = jnp.stack(s_p)
    new_mem_k_prompt = jnp.stack(mk_p)
    new_mem_v_prompt = jnp.stack(mv_p)
    new_win_k_sample = jnp.stack(wk_s)
    new_win_v_sample = jnp.stack(wv_s)
    new_gla_sample = jnp.stack(s_s)
    return (y_p, y_s, new_win_k_prompt, new_win_v_prompt, new_gla_prompt, new_mem_k_prompt, new_mem_v_prompt,
            new_win_k_sample, new_win_v_sample, new_gla_sample)


_drawn_inputs = setup_inputs


def setup_inputs(seed=0):
    import zlib

    import numpy as np

    out = dict(_drawn_inputs(seed))
    spreads = {}
    factors = {'b_gates': 4.919,
     'a_qnorm_g': 3.951,
     'a_knorm_g': 9.142,
     'a_sinks': 64.0,
     'b_gn_g': 2.815,
     'c_qnorm_g': 7.132,
     'c_knorm_g': 2.914,
     'mem_norm_g': 2.931,
     'rel_bias': 7.777}
    for name, (base, spread) in spreads.items():
        noise = np.random.default_rng([zlib.crc32(name.encode()), seed]).standard_normal(out[name].shape)
        drawn = base * np.exp(spread * noise) if base else spread * noise
        out[name] = __import__('jax').numpy.asarray(drawn.astype(out[name].dtype))
    for name, factor in factors.items():
        out[name] = (out[name] * factor).astype(out[name].dtype)
    return out
```

```python
from contextlib import ExitStack

import concourse.bass as bass
from concourse import mybir

F32 = mybir.dt.float32
F32R = mybir.dt.float32r
U32 = mybir.dt.uint32
ALU = mybir.AluOpType
ACT = mybir.ActivationFunctionType
AX = mybir.AxisListType.X

P = 128
D = 1024
KT = D // P
TP, NB, TS = 1024, 8, 4
T = TP + NB * TS
NMEM = 256
TM = T + NMEM
CH = T // 3
CHUNKS = [(c * CH, (c + 1) * CH) for c in range(3)]
BLK = TP // P
EPS = 1e-6
NEG = -1e30
QA, KA, QB, KB, RB, QC, NF = 0, 4, 5, 7, 9, 13, 17
WIN = 128
WK = WIN + TS
EXT = 384
GC = 64
HEADS, TOPK, NK = 8, 16, 128
NT = BLK + 1
TBG = 48

C_ID, C_BLK, C_IOTA, C_TRI, C_TRIS, C_OWN, C_SEL, C_HOT, C_END = 0, 128, 256, 384, 448, 480, 488, 496, 624


class Chain:

    def __init__(self, eng, sem, count=0):
        self.eng, self.sem, self.n = eng, sem, count

    def __call__(self, ins):
        ins.then_inc(self.sem, 1)
        self.n += 1
        self.eng.wait_ge(self.sem, self.n)


class Mem:
    pass


def tile_rows(t):
    return P if t < BLK else T - TP


def exact_product(pe, out, w, x, first, last):
    pe.matmul(out, w[0], x[0], start=first, stop=False)
    pe.matmul(out, w[0], x[1], start=False, stop=False)
    return pe.matmul(out, w[1], x[0], start=False, stop=last)


def load_small(nc, m, d, sem):
    loaded = sem("small_loaded")
    with nc.Block() as block:

        @block.sync
        def _(sp):
            n = 0

            def load(dst, src):
                nonlocal n
                sp.dma_start(dst, src).then_inc(loaded, 16)
                n += 16

            load(m.const[:], d["const"])
            load(m.norm1[:], d["norm1_g"])
            load(m.norm2[:], d["norm2_g"])
            load(m.memg[:], d["mem_norm_g"])
            for half in range(2):
                load(m.qg[64 * half:64 * half + 64, :], d["a_qnorm_g"])
                load(m.kg[64 * half:64 * half + 64, :], d["a_knorm_g"])
            load(m.cqg[:], d["c_qnorm_g"])
            load(m.ckg[:], d["c_knorm_g"])
            load(m.gng[:], d["b_gn_g"])
            load(m.gbias[:], d["b_gate_b"])
            load(m.gates_b[:], d["b_gates"])
            load(m.sink[:], d["a_sinks"].broadcast_to([P, 8]))
            for kv in range(2):
                src = bass.AP(tensor=d["a_sinks"].tensor, offset=4 * kv, ap=[[1, 4], [0, 32], [1, 1]])
                load(m.sink_s[:, kv:kv + 1], src)
            load(m.relb[:], d["rel_bias"])
            load(m.w2[:], d["b_gate_w2"])
            sp.wait_ge(loaded, n)

        @block.vector
        def _(dve):
            dve.memset(m.ones[:], 1.0)
            dve.memset(m.eps[:], EPS)
            dve.memset(m.one[:], 1.0)


def bias_by_distance(nc, m, d, sem):
    with ExitStack() as ctx:
        ext = ctx.enter_context(nc.sbuf_tensor("ext", [8, EXT], F32))
        cleared, picked, ready, out, back = (sem(f"bias_{x}") for x in ("cleared", "picked", "ready", "out", "back"))
        with nc.Block() as block:

            @block.tensor
            def _(pe):
                pe.matmul(m.ps[0:8, 0, 0:WIN], m.relb[:], m.const[0:32, C_HOT:C_HOT + WIN],
                          start=True, stop=True).then_inc(picked, 1)

            @block.vector
            def _(dve):
                dve.memset(ext[:], NEG).then_inc(cleared, 1)
                dve.wait_ge(cleared, 1)
                dve.wait_ge(picked, 1)
                dve.tensor_copy(ext[:, P:P + WIN], m.ps[0:8, 0, 0:WIN]).then_inc(ready, 1)

            @block.sync
            def _(sp):
                sp.wait_ge(ready, 1)
                sp.dma_start(d["skew"], ext[:].unsqueeze(1).broadcast_to([8, P, EXT])).then_inc(out, 16)
                sp.wait_ge(out, 16)
                for h in range(8):
                    src = bass.AP(tensor=d["skew"].tensor, offset=h * P * EXT + P - 1, ap=[[EXT - 1, P], [1, 2 * P]])
                    sp.dma_start(m.bias[:, h // 4, h % 4, :], src).then_inc(back, 16)
                    src = bass.AP(tensor=d["skew"].tensor, offset=h * P * EXT + P - 1,
                                  ap=[[0, NB], [EXT - 1, TS], [1, WK]])
                    g = h % 4
                    sp.dma_start(m.bias_s[32 * g:32 * g + 32, h // 4, :], src).then_inc(back, 16)
                sp.wait_ge(back, 16 * 16)


def norm_features(nc, m, sem, tag, src, dst, parts, loads):
    width = src.shape[2]
    spans = [(a, min(a + CH, width)) for a in range(0, width, CH)]
    with ExitStack() as ctx:
        sq = ctx.enter_context(nc.sbuf_tensor(f"{tag}_sq", [P, 2, width], F32))
        root = ctx.enter_context(nc.sbuf_tensor(f"{tag}_root", [P, width], F32))
        x_loaded = [sem(f"{tag}_loaded{k}") for k in range(KT)]
        squared, summed, rooted, inv = (sem(f"{tag}_{x}") for x in ("squared", "summed", "rooted", "inverted"))
        with nc.Block() as block:

            @block.sync
            def _(sp):
                for k in range(KT):
                    sp.dma_start(src[:, k, :], loads[:, k, :]).then_inc(x_loaded[k], 16)

            @block.scalar
            def _(act):
                for k in range(KT):
                    act.wait_ge(x_loaded[k], 16)
                    if k >= 2:
                        act.wait_ge(summed, k - 1)
                    act.activation(sq[:, k % 2, :], src[:, k, :], ACT.Square).then_inc(squared, 1)
                act.wait_ge(summed, KT)
                for b, (a, z) in enumerate(spans):
                    act.activation(root[:, a:z], m.ps[:, b, 0:z - a], ACT.Sqrt, bias=m.eps[:, 0:1],
                                   scale=1.0 / D).then_inc(rooted, 1)

            @block.tensor
            def _(pe):
                for k in range(KT):
                    pe.wait_ge(squared, k + 1)
                    for b, (a, z) in enumerate(spans):
                        mm = pe.matmul(m.ps[:, b, 0:z - a], m.ones[:], sq[:, k % 2, a:z],
                                       start=(k == 0), stop=(k == KT - 1))
                    mm.then_inc(summed, 1)

            @block.vector
            def _(dve):
                dve.wait_ge(rooted, len(spans))
                dve.reciprocal(root[:], root[:]).then_inc(inv, 1)
                dve.wait_ge(inv, 1)
                for k in range(KT):
                    for a, z, gain in parts:
                        dve.scalar_tensor_tensor(dst[:, k, a:z], src[:, k, a:z], gain[:, k:k + 1], root[:, a:z],
                                                 ALU.mult, ALU.mult)


def norm_and_split(nc, m, sem):
    spans = [(a, min(a + CH, T)) for a in range(0, T, CH)]
    with ExitStack() as ctx:
        sq = ctx.enter_context(nc.sbuf_tensor("n2_sq", [P, 2, T], F32))
        full = ctx.enter_context(nc.sbuf_tensor("n2_full", [P, 2, T], F32))
        root = ctx.enter_context(nc.sbuf_tensor("n2_root", [P, T], F32))
        squared, summed, rooted, inv, scaled, high, low = (
            sem(f"n2_{x}") for x in ("squared", "summed", "rooted", "inverted", "scaled", "high", "low"))
        with nc.Block() as block:

            @block.scalar
            def _(act):
                for k in range(KT):
                    if k >= 2:
                        act.wait_ge(summed, k - 1)
                    act.activation(sq[:, k % 2, :], m.x2[:, k, :], ACT.Square).then_inc(squared, 1)
                act.wait_ge(summed, KT)
                for b, (a, z) in enumerate(spans):
                    act.activation(root[:, a:z], m.ps[:, b, 0:z - a], ACT.Sqrt, bias=m.eps[:, 0:1],
                                   scale=1.0 / D).then_inc(rooted, 1)
                for k in range(KT):
                    act.wait_ge(scaled, k + 1)
                    act.copy(m.hn[0][:, k, :], full[:, k % 2, :]).then_inc(high, 1)

            @block.tensor
            def _(pe):
                for k in range(KT):
                    pe.wait_ge(squared, k + 1)
                    for b, (a, z) in enumerate(spans):
                        mm = pe.matmul(m.ps[:, b, 0:z - a], m.ones[:], sq[:, k % 2, a:z],
                                       start=(k == 0), stop=(k == KT - 1))
                    mm.then_inc(summed, 1)

            @block.vector
            def _(dve):
                for b, (a, z) in enumerate(spans):
                    dve.wait_ge(rooted, b + 1)
                    dve.reciprocal(root[:, a:z], root[:, a:z]).then_inc(inv, 1)
                dve.wait_ge(inv, len(spans))
                for k in range(KT + 1):
                    if k < KT:
                        if k >= 2:
                            dve.wait_ge(low, k - 1)
                        dve.scalar_tensor_tensor(full[:, k % 2, :], m.x2[:, k, :], m.norm2[:, k:k + 1], root[:],
                                                 ALU.mult, ALU.mult).then_inc(scaled, 1)
                    if k:
                        dve.wait_ge(high, k)
                        dve.tensor_tensor(m.hn[1][:, k - 1, :], full[:, (k - 1) % 2, :],
                                          m.hn[0][:, k - 1, :].bitcast(F32), ALU.subtract).then_inc(low, 1)


def project_memory(nc, m, d, sem):
    with ExitStack() as ctx:
        wk = ctx.enter_context(nc.sbuf_tensor("wmk", [P, 4, KT, P], F32))
        wv = ctx.enter_context(nc.sbuf_tensor("wmv", [P, KT, 512], F32))
        k_loaded, v_loaded, done, kept = (sem(f"mkv_{x}") for x in ("k_loaded", "v_loaded", "done", "kept"))
        with nc.Block() as block:

            @block.sync
            def _(sp):
                sp.dma_start(wk[:], d["w_mk"]).then_inc(k_loaded, 16)
                sp.dma_start(wv[:], d["w_mv"]).then_inc(v_loaded, 16)

            @block.tensor
            def _(pe):
                pe.wait_ge(k_loaded, 16)
                for h in range(4):
                    for k in range(KT):
                        mm = pe.matmul(m.ps[:, h, 0:NMEM], wk[:, h, k, :], m.xn[:, k, T:TM], start=(k == 0),
                                       stop=(k == KT - 1))
                    mm.then_inc(done, 1)
                pe.wait_ge(v_loaded, 16)
                for c in range(2):
                    for k in range(KT):
                        mm = pe.matmul(m.ps[:, 4 + c, :], m.xn[:, k, T + c * P:T + c * P + P], wv[:, k, :],
                                       start=(k == 0), stop=(k == KT - 1))
                    mm.then_inc(done, 1)

            @block.scalar
            def _(act):
                for h in range(4):
                    act.wait_ge(done, h + 1)
                    act.copy(m.mk[:, h, :], m.ps[:, h, 0:NMEM])
                for c in range(2):
                    act.wait_ge(done, 5 + c)
                    act.copy(m.mv[:, c, :], m.ps[:, 4 + c, :]).then_inc(kept, 1)
                act.wait_ge(kept, 2)
                act.dma_start(d["out_mv"].rearrange("(c n) e -> n c e", c=2), m.mv[:]).then_inc(m.stored, 16)


def project(nc, m, d, sem):
    with ExitStack() as ctx:
        w = ctx.enter_context(nc.sbuf_tensor("w_ring", [P, 2, KT, P], F32))
        wv = ctx.enter_context(nc.sbuf_tensor("wv", [P, KT, 640], F32))
        wlr = ctx.enter_context(nc.sbuf_tensor("wlr", [P, KT, 16], F32))
        w_loaded = [sem("w_loaded0"), sem("w_loaded1")]
        done, kept, wv_loaded, wlr_loaded = (sem(f"proj_{x}") for x in ("done", "kept", "wv_loaded", "wlr_loaded"))
        with nc.Block() as block:

            @block.sync
            def _(sp):
                for n in range(NF):
                    if n >= 2:
                        sp.wait_ge(done, 3 * (n - 1))
                    sp.dma_start(w[:, n % 2], d["w_f"][n]).then_inc(w_loaded[n % 2], 16)
                    if n == 2:
                        sp.dma_start(wlr[:], d["w_lr"]).then_inc(wlr_loaded, 16)
                        sp.dma_start(wv[:], d["w_v"]).then_inc(wv_loaded, 16)
                sp.dma_start(d["out_wvs"][:, 0:WIN - TS, :], d["win_v"][:, TS:WIN, :]).then_inc(m.stored, 16)

            @block.tensor
            def _(pe):
                unit = 0

                def product(rows, width, lhs, rhs):
                    nonlocal unit
                    if unit >= 8:
                        pe.wait_ge(kept, unit - 7)
                    for k in range(KT):
                        mm = pe.matmul(m.ps[0:rows, unit % 8, 0:width], lhs(k), rhs(k), start=(k == 0),
                                       stop=(k == KT - 1))
                    mm.then_inc(done, 1)
                    unit += 1

                for n in range(NF):
                    pe.wait_ge(w_loaded[n % 2], 16 * (n // 2 + 1))
                    for a, z in CHUNKS:
                        product(P, CH, lambda k: w[:, n % 2, k, :], lambda k: m.xn[:, k, a:z])
                pe.wait_ge(wlr_loaded, 16)
                for a, z in CHUNKS:
                    product(16, CH, lambda k: wlr[:, k, :], lambda k: m.xn[:, k, a:z])
                pe.wait_ge(wv_loaded, 16)
                for t in range(NT):
                    r = tile_rows(t)
                    product(r, P, lambda k: m.xn[:, k, t * P:t * P + r], lambda k: wv[:, k, 0:128])
                    product(r, 512, lambda k: m.xn[:, k, t * P:t * P + r], lambda k: wv[:, k, 128:640])

            @block.scalar
            def _(act):
                unit = 0

                def keep(dst, rows, width):
                    nonlocal unit
                    act.wait_ge(done, unit + 1)
                    act.copy(dst, m.ps[0:rows, unit % 8, 0:width]).then_inc(kept, 1)
                    unit += 1

                for n in range(NF):
                    for a, z in CHUNKS:
                        keep(m.f[:, n, a:z], P, CH)
                for a, z in CHUNKS:
                    keep(m.lr[:, a:z], 16, CH)
                for t in range(NT):
                    r = tile_rows(t)
                    keep(m.av[0:r, t, :], r, P)
                    keep(m.bv[0:r, t, :], r, 512)
                act.wait_ge(kept, unit)
                act.dma_start(d["out_wv"], m.av[:, BLK - 1, :]).then_inc(m.stored, 16)
                for b in range(NB):
                    act.dma_start(d["out_wvs"][b, WIN - TS:WIN, :], m.av[TS * b:TS * b + TS, BLK, :]).then_inc(m.stored, 16)


def norm_heads(nc, m, d, sem):
    blk, ones = m.const[:, C_BLK:C_BLK + P], m.ones[:]
    units = [(m.f[:, QA + t, a:z], blk, 64, m.qg) for t in range(4) for a, z in CHUNKS]
    units += [(m.f[:, KA, a:z], blk, 64, m.kg) for a, z in CHUNKS]
    units += [(m.f[:, QC + t, a:z], ones, P, m.cqg) for t in range(4) for a, z in CHUNKS]
    units += [(m.mk[:, h, :], ones, P, m.ckg) for h in range(4)]
    norm_units(nc, m, sem, "heads", units)
    with nc.Block() as block:

        @block.sync
        def _(sp):
            sp.dma_start(d["out_wk"], m.f[:, KA, TP - WIN:TP]).then_inc(m.stored, 16)
            sp.dma_start(d["out_mk"], m.mk[:]).then_inc(m.stored, 16)


def norm_units(nc, m, sem, tag, units):
    with ExitStack() as ctx:
        sq = ctx.enter_context(nc.sbuf_tensor(f"{tag}_sq", [P, 4, CH], F32))
        rt = ctx.enter_context(nc.sbuf_tensor(f"{tag}_rt", [P, 4, CH], F32))
        squared, summed, rooted, inverted, scaled = (
            sem(f"{tag}_{x}") for x in ("squared", "summed", "rooted", "inverted", "scaled"))
        with nc.Block() as block:

            @block.scalar
            def _(act):
                for u in range(len(units) + 2):
                    if u < len(units):
                        x = units[u][0]
                        if u >= 4:
                            act.wait_ge(summed, u - 3)
                        act.activation(sq[:, u % 4, 0:x.shape[1]], x, ACT.Square).then_inc(squared, 1)
                    v = u - 2
                    if v >= 0:
                        w = units[v][0].shape[1]
                        act.wait_ge(summed, v + 1)
                        if v >= 4:
                            act.wait_ge(scaled, v - 3)
                        act.activation(rt[:, v % 4, 0:w], m.ps[:, v % 8, 0:w], ACT.Sqrt, bias=m.eps[:, 0:1],
                                       scale=1.0 / units[v][2]).then_inc(rooted, 1)

            @block.tensor
            def _(pe):
                for u, (x, ones, _, _) in enumerate(units):
                    w = x.shape[1]
                    pe.wait_ge(squared, u + 1)
                    if u >= 8:
                        pe.wait_ge(rooted, u - 7)
                    pe.matmul(m.ps[:, u % 8, 0:w], ones, sq[:, u % 4, 0:w], start=True, stop=True).then_inc(summed, 1)

            @block.vector
            def _(dve):
                for u, (x, _, _, gain) in enumerate(units):
                    w = x.shape[1]
                    dve.wait_ge(rooted, u + 1)
                    dve.reciprocal(rt[:, u % 4, 0:w], rt[:, u % 4, 0:w]).then_inc(inverted, 1)
                    dve.wait_ge(inverted, u + 1)
                    dve.scalar_tensor_tensor(x, x, gain[:, 0:1], rt[:, u % 4, 0:w], ALU.mult,
                                             ALU.mult).then_inc(scaled, 1)


def attend_prompt(nc, m, sem, windowed):
    tag = "win" if windowed else "mem"
    units = [(n, kv) for n in range(BLK) for kv in range(2)] if windowed else [(n, 0) for n in range(BLK)]
    scale = 64 ** -0.5 if windowed else P ** -0.5
    ident = m.const[:, C_ID:C_ID + P]
    with ExitStack() as ctx:
        s = ctx.enter_context(nc.sbuf_tensor(f"{tag}_s", [P, 2, 4, 256], F32))
        pt = ctx.enter_context(nc.sbuf_tensor(f"{tag}_pt", [P, 2, 8, P], F32))
        st = ctx.enter_context(nc.sbuf_tensor(f"{tag}_stats", [P, 2, 6, 4], F32))
        scored, based, chained, maxed, expd, normed, turned, pt_kept, summed, kept = (
            sem(f"{tag}_{x}") for x in
            ("scored", "based", "chained", "maxed", "expd", "normed", "turned", "pt_kept", "summed", "kept"))
        MAXI, NMAX, SUM, SINK, INV = range(5)

        def lo(n):
            return P if windowed and n == 0 else 0

        with nc.Block() as block:

            @block.tensor
            def _(pe):
                for u in range(len(units) + 1):
                    if u < len(units):
                        n, kv = units[u]
                        if u >= 2:
                            pe.wait_ge(based if windowed else expd, u - 1)
                        for j in range(4):
                            out = m.ps[:, 2 * (u % 2) + j // 2, (j % 2) * 256 + lo(n):(j % 2) * 256 + 256]
                            if windowed:
                                rows = slice(64 * kv, 64 * kv + 64)
                                q = m.f[rows, QA + j, n * P:n * P + P]
                                k = m.f[rows, KA, n * P - P + lo(n):n * P + P]
                            else:
                                q, k = m.f[:, QC + j, n * P:n * P + P], m.mk[:, j, :]
                            mm = pe.matmul(out, q, k, start=True, stop=True)
                        mm.then_inc(scored, 1)
                    if u >= 1:
                        v = u - 1
                        n, kv = units[v]
                        pe.wait_ge(normed, v + 1)
                        if v >= 1:
                            pe.wait_ge(pt_kept, v)
                        for j in range(4):
                            for c in range(lo(n) // P, 2):
                                i = 2 * j + c
                                mm = pe.transpose(m.ps[:, 4 + i // 4, (i % 4) * P:(i % 4) * P + P],
                                                  s[:, v % 2, j, c * P:c * P + P], ident)
                        mm.then_inc(turned, 1)
                        pe.wait_ge(pt_kept, v + 1)
                        if v >= 2:
                            pe.wait_ge(kept, v - 1)
                        for j in range(4):
                            cs = range(lo(n) // P, 2)
                            for c in cs:
                                if windowed:
                                    out = m.ps[64 * kv:64 * kv + 64, 6 + v % 2, j * P:j * P + P]
                                    val = m.av[:, n - 1 + c, 64 * kv:64 * kv + 64]
                                else:
                                    out = m.ps[:, 6 + v % 2, j * P:j * P + P]
                                    val = m.mv[:, c, j * P:j * P + P]
                                mm = pe.matmul(out, val, pt[:, v % 2, 2 * j + c, :], start=(c == cs[0]), stop=(c == 1))
                        mm.then_inc(summed, 1)

            @block.vector
            def _(dve):
                chain = Chain(dve, chained)
                for u in range(len(units) + 1):
                    if u < len(units):
                        n, kv = units[u]
                        a = lo(n)
                        x, z = s[:, u % 2, :, a:256], st[:, u % 2]
                        raw = m.ps[:, 2 * (u % 2):2 * (u % 2) + 2, :].rearrange("p b (j k) -> p (b j) k", j=2)[:, :, a:256]
                        dve.wait_ge(scored, u + 1)
                        if u >= 2:
                            dve.wait_ge(turned, u - 1)
                        if windowed:
                            dve.scalar_tensor_tensor(x, raw, scale, m.bias[:, kv, :, a:256], ALU.mult,
                                                     ALU.add).then_inc(based, 1)
                            dve.wait_ge(based, u + 1)
                            chain(dve.tensor_reduce(z[:, MAXI, :], x, AX, ALU.max))
                            sink = m.sink[:, 4 * kv:4 * kv + 4]
                            chain(dve.tensor_tensor(z[:, MAXI, :], z[:, MAXI, :], sink, ALU.max))
                            chain(dve.tensor_scalar(z[:, NMAX, :], z[:, MAXI, :], -1.0, None, ALU.mult))
                            dve.tensor_tensor(z[:, SINK, :], sink, z[:, NMAX, :], ALU.add).then_inc(maxed, 1)
                        else:
                            chain(dve.tensor_reduce(z[:, MAXI, :], raw, AX, ALU.max))
                            dve.tensor_scalar(z[:, NMAX, :], z[:, MAXI, :], -scale, None, ALU.mult).then_inc(maxed, 1)
                    if u >= 1:
                        v = u - 1
                        a = lo(units[v][0])
                        x, z = s[:, v % 2, :, a:256], st[:, v % 2]
                        dve.wait_ge(expd, v + 1)
                        if windowed:
                            chain(dve.tensor_tensor(z[:, SUM, :], z[:, SUM, :], z[:, SINK, :], ALU.add))
                        chain(dve.reciprocal(z[:, INV, :], z[:, SUM, :]))
                        dve.tensor_tensor(x, x, z[:, INV, :].unsqueeze(2).broadcast_to([P, 4, 256 - a]),
                                          ALU.mult).then_inc(normed, 1)

            @block.scalar
            def _(act):
                for u in range(len(units) + 1):
                    if u < len(units):
                        n, kv = units[u]
                        a = lo(n)
                        z = st[:, u % 2]
                        act.wait_ge(maxed, u + 1)
                        for j in range(4):
                            x = s[:, u % 2, j, a:256]
                            raw = x if windowed else m.ps[:, 2 * (u % 2) + j // 2, (j % 2) * 256:(j % 2) * 256 + 256]
                            ins = act.activation(x, raw, ACT.Exp, bias=z[:, NMAX, j:j + 1],
                                                 scale=1.0 if windowed else scale, accum_out=z[:, SUM, j:j + 1])
                        if windowed:
                            ins = act.activation(z[:, SINK, :], z[:, SINK, :], ACT.Exp)
                        ins.then_inc(expd, 1)
                    if u >= 1:
                        v = u - 1
                        n, kv = units[v]
                        act.wait_ge(turned, v + 1)
                        if v >= 2:
                            act.wait_ge(summed, v - 1)
                        for b in range(2):
                            bank = m.ps[:, 4 + b, :].rearrange("p (j c q) -> p j c q", j=2, c=2)
                            dst = pt[:, v % 2, 4 * b:4 * b + 4, :].rearrange("p (j c) q -> p j c q", c=2)
                            c = lo(n) // P
                            ins = act.copy(dst[:, :, c:2, :], bank[:, :, c:2, :])
                        ins.then_inc(pt_kept, 1)
                        act.wait_ge(summed, v + 1)
                        rows = slice(64 * kv, 64 * kv + 64) if windowed else slice(0, P)
                        q0 = QA if windowed else QC
                        act.copy(m.f[rows, q0:q0 + 4, n * P:n * P + P],
                                 m.ps[rows, 6 + v % 2, :].rearrange("p (j q) -> p j q", j=4)).then_inc(kept, 1)


def attend_memory_samples(nc, m, d, sem):
    scale = P ** -0.5
    with ExitStack() as ctx:
        kc = ctx.enter_context(nc.sbuf_tensor("sm_k", [P, 2, NB * NMEM], F32))
        vc = ctx.enter_context(nc.sbuf_tensor("sm_v", [P, NB, 512], F32))
        s = ctx.enter_context(nc.sbuf_tensor("sm_s", [P, NB, NMEM], F32))
        pt = kc[:, 0, :].rearrange("p (b r) -> p b r", r=P)
        st = ctx.enter_context(nc.sbuf_tensor("sm_stats", [P, 4], F32))
        k_loaded = [sem(f"sm_k_loaded{h}") for h in range(4)]
        v_loaded, scored, chained, maxed, expd, normed, turned, pt_kept, summed = (
            sem(f"sm_{x}") for x in
            ("v_loaded", "scored", "chained", "maxed", "expd", "normed", "turned", "pt_kept", "summed"))
        with nc.Block() as block:

            @block.sync
            def _(sp):
                for h in range(4):
                    if h >= 2:
                        sp.wait_ge(scored, h - 1)
                    sp.dma_start(kc[:, h % 2, :], d["mem_k"][h]).then_inc(k_loaded[h], 16)
                for q in range(2):
                    if q:
                        sp.wait_ge(summed, 1)
                    for b in range(4):
                        sp.dma_start(vc[:, 2 * b:2 * b + 2, :], d["mem_v"][4 * q + b].rearrange("(c n) e -> n c e", c=2)
                                     ).then_inc(v_loaded, 16)
                sp.wait_ge(m.stored, m.stores - 32)

            @block.tensor
            def _(pe):
                for h in range(4):
                    pe.wait_ge(k_loaded[h], 16)
                    for b in range(4):
                        mm = pe.matmul(m.ps[32 * h:32 * h + 32, b, :], m.f[:, QC + h, TP:T],
                                       kc[:, h % 2, b * 512:b * 512 + 512], start=True, stop=True)
                    mm.then_inc(scored, 1)
                pe.wait_ge(normed, 1)
                x = s[:].rearrange("p b k -> p (b k)")
                for i in range(16):
                    mm = pe.transpose(m.ps[:, 4 + i // 4, (i % 4) * P:(i % 4) * P + P], x[:, i * P:i * P + P],
                                      m.const[:, C_ID:C_ID + P])
                mm.then_inc(turned, 1)
                pe.wait_ge(pt_kept, 1)
                for q in range(2):
                    pe.wait_ge(v_loaded, 64 * (q + 1))
                    for h in range(4):
                        for b in range(4 * q, 4 * q + 4):
                            for c in range(2):
                                col = 32 * h + TS * b
                                mm = pe.matmul(m.ps[:, 0, col:col + TS], vc[:, 2 * (b % 4) + c, h * P:h * P + P],
                                               pt[:, 2 * b + c, col:col + TS], start=(c == 0), stop=(c == 1))
                    mm.then_inc(summed, 1)

            @block.vector
            def _(dve):
                chain = Chain(dve, chained)
                dve.wait_ge(scored, 4)
                own = m.const[:, C_OWN:C_OWN + NB].unsqueeze(2).broadcast_to([P, NB, NMEM])
                for b in range(4):
                    ins = dve.scalar_tensor_tensor(s[:, 2 * b:2 * b + 2, :],
                                                   m.ps[:, b, :].rearrange("p (a k) -> p a k", a=2), 1.0,
                                                   own[:, 2 * b:2 * b + 2, :], ALU.mult, ALU.add)
                chain(ins)
                chain(dve.tensor_reduce(st[:, 0:1], s[:].rearrange("p b k -> p (b k)"), AX, ALU.max))
                dve.tensor_scalar(st[:, 1:2], st[:, 0:1], -scale, None, ALU.mult).then_inc(maxed, 1)
                dve.wait_ge(expd, 1)
                chain(dve.reciprocal(st[:, 3:4], st[:, 2:3]))
                dve.tensor_scalar(s[:], s[:], st[:, 3:4], None, ALU.mult).then_inc(normed, 1)

            @block.scalar
            def _(act):
                act.wait_ge(maxed, 1)
                act.activation(s[:], s[:], ACT.Exp, bias=st[:, 1:2], scale=scale, accum_out=st[:, 2:3]).then_inc(expd, 1)
                act.wait_ge(turned, 1)
                act.copy(pt, m.ps[:, 4:8, :].rearrange("p b (i r) -> p (b i) r", i=4)).then_inc(pt_kept, 1)
                act.wait_ge(summed, 2)
                act.copy(m.f[:, QC:QC + 4, TP:T], m.ps[:, 0, 0:P].rearrange("p (h r) -> p h r", h=4))


def attend_window_samples(nc, m, d, sem):
    scale = 64 ** -0.5
    with ExitStack() as ctx:
        kk = ctx.enter_context(nc.sbuf_tensor("sw_k", [P, NB, WK], F32))
        cv = ctx.enter_context(nc.sbuf_tensor("sw_v", [P, NB, P], F32))
        q = ctx.enter_context(nc.sbuf_tensor("sw_q", [P, 4, 32], F32))
        s = ctx.enter_context(nc.sbuf_tensor("sw_s", [P, 2, NB, WK], F32))
        new = ctx.enter_context(nc.sbuf_tensor("sw_new", [P, 2, 32], F32))
        pt = ctx.enter_context(nc.sbuf_tensor("sw_pt", [P, 2, NB + 1, P], F32))
        st = ctx.enter_context(nc.sbuf_tensor("sw_stats", [P, 2, 6], F32))
        loaded, keys, chained, scored, maxed, expd, normed, turned, pt_kept, summed = (
            sem(f"sw_{x}") for x in
            ("loaded", "keys", "chained", "scored", "maxed", "expd", "normed", "turned", "pt_kept", "summed"))
        with nc.Block() as block:

            @block.sync
            def _(sp):
                sp.dma_start(kk[:, :, 0:WIN], d["win_k"]).then_inc(loaded, 16)
                sp.dma_start(cv[:], d["win_v"].rearrange("b s c -> s b c")).then_inc(loaded, 16)
                sp.wait_ge(loaded, 32)
                sp.wait_ge(keys, 2)
                sp.dma_start(d["out_wks"], kk[:, :, TS:WK]).then_inc(m.stored, 16)
                sp.wait_ge(m.stored, m.stores - 16)

            @block.vector
            def _(dve):
                chain = Chain(dve, chained)
                dve.tensor_copy(kk[:, :, WIN:WK], m.f[:, KA, TP:T].rearrange("p (b s) -> p b s", b=NB)).then_inc(keys, 1)
                dve.tensor_copy(q[:], m.f[:, QA:QA + 4, TP:T]).then_inc(keys, 1)
                own = m.const[:, C_OWN:C_OWN + NB].unsqueeze(2).broadcast_to([P, NB, WK])
                for kv in range(2):
                    dve.wait_ge(scored, kv + 1)
                    for c in range(4):
                        bias = m.bias_s[:, kv, :].unsqueeze(1).broadcast_to([P, 2, WK])
                        ins = dve.scalar_tensor_tensor(s[:, kv, 2 * c:2 * c + 2, :],
                                                       m.ps[:, 4 * kv + c, 0:2 * WK].rearrange("p (b k) -> p b k", b=2),
                                                       scale, bias, ALU.mult, ALU.add)
                    chain(ins)
                    chain(dve.tensor_tensor(s[:, kv], s[:, kv], own, ALU.add))
                    chain(dve.tensor_reduce(st[:, kv, 0:1], s[:, kv].rearrange("p b k -> p (b k)"), AX, ALU.max))
                    chain(dve.tensor_tensor(st[:, kv, 0:1], st[:, kv, 0:1], m.sink_s[:, kv:kv + 1], ALU.max))
                    chain(dve.tensor_scalar(st[:, kv, 1:2], st[:, kv, 0:1], -1.0, None, ALU.mult))
                    dve.tensor_tensor(st[:, kv, 3:4], m.sink_s[:, kv:kv + 1], st[:, kv, 1:2], ALU.add).then_inc(maxed, 1)
                for kv in range(2):
                    dve.wait_ge(expd, kv + 1)
                    chain(dve.tensor_tensor(st[:, kv, 4:5], st[:, kv, 2:3], st[:, kv, 3:4], ALU.add))
                    chain(dve.reciprocal(st[:, kv, 5:6], st[:, kv, 4:5]))
                    chain(dve.tensor_scalar(s[:, kv], s[:, kv], st[:, kv, 5:6], None, ALU.mult))
                    dve.tensor_copy(new[:, kv].rearrange("p (b s) -> p b s", b=NB), s[:, kv, :, WIN:WK]).then_inc(normed, 1)

            @block.tensor
            def _(pe):
                pe.wait_ge(loaded, 32)
                pe.wait_ge(keys, 2)
                ident = m.const[:, C_ID:C_ID + P]
                for kv in range(2):
                    rows = slice(64 * kv, 64 * kv + 64)
                    for c in range(4):
                        mm = pe.matmul(m.ps[:, 4 * kv + c, 0:2 * WK], q[rows].rearrange("p g t -> p (g t)"),
                                       kk[rows, 2 * c:2 * c + 2, :].rearrange("p b k -> p (b k)"), start=True, stop=True)
                    mm.then_inc(scored, 1)
                for kv in range(2):
                    rows = slice(64 * kv, 64 * kv + 64)
                    pe.wait_ge(normed, kv + 1)
                    if kv == 0:
                        pe.wait_ge(maxed, 2)
                    for b in range(NB):
                        pe.transpose(m.ps[:, 4 * kv + b // 4, (b % 4) * P:(b % 4) * P + P], s[:, kv, b, 0:WIN], ident)
                    pe.transpose(m.ps[0:32, 4 * kv + 2, 0:P], new[:, kv, :], ident).then_inc(turned, 1)
                    pe.wait_ge(pt_kept, kv + 1)
                    for b in range(NB):
                        pe.matmul(m.ps[rows, 4 * kv + 3, 0:P], cv[:, b, rows], pt[:, kv, b, :], start=(b == 0), stop=False)
                    pe.matmul(m.ps[rows, 4 * kv + 3, 0:P], m.av[0:32, BLK, rows], pt[0:32, kv, NB, :], start=False,
                              stop=True).then_inc(summed, 1)

            @block.scalar
            def _(act):
                for kv in range(2):
                    act.wait_ge(maxed, kv + 1)
                    act.activation(s[:, kv], s[:, kv], ACT.Exp, bias=st[:, kv, 1:2], accum_out=st[:, kv, 2:3])
                    act.activation(st[:, kv, 3:4], st[:, kv, 3:4], ACT.Exp).then_inc(expd, 1)
                for kv in range(2):
                    rows = slice(64 * kv, 64 * kv + 64)
                    act.wait_ge(turned, kv + 1)
                    act.copy(pt[:, kv, 0:NB, :],
                             m.ps[:, 4 * kv:4 * kv + 2, :].rearrange("p b (i r) -> p (b i) r", i=4))
                    act.copy(pt[0:32, kv, NB, :], m.ps[0:32, 4 * kv + 2, 0:P]).then_inc(pt_kept, 1)
                    act.wait_ge(summed, kv + 1)
                    act.copy(m.f[rows, QA:QA + 4, TP:T], m.ps[rows, 4 * kv + 3, 0:P].rearrange("p (g t) -> p g t", g=4))


def prepare_gla(nc, m, g, d, sem):
    zed, done, chained, a_done, b_done, x_done = (sem(f"gla_{x}") for x in ("zed", "done", "chained", "abs", "exp", "ln"))
    tmp_done = sem("gla_tmp")
    with ExitStack() as ctx:
        z = ctx.enter_context(nc.sbuf_tensor("gla_z", [P, 2, T], F32))
        l = ctx.enter_context(nc.sbuf_tensor("gla_l", [P, 2, T], F32))
        scan = ctx.enter_context(nc.sbuf_tensor("gla_scan", [P, T], F32))
        scan_loaded = sem("gla_scan_loaded")
        with nc.Block() as block:

            @block.sync
            def _(sp):
                sp.dma_start(scan[:], d["scan"].broadcast_to([P, T])).then_inc(scan_loaded, 16)

            @block.tensor
            def _(pe):
                for j in range(2):
                    for c, (a, e) in enumerate(CHUNKS):
                        pe.matmul(m.ps[:, 3 * j + c, 0:CH], m.w2[:, j * P:j * P + P], m.lr[:, a:e],
                                  start=True, stop=True).then_inc(zed, 1)

            @block.scalar
            def _(act):
                for j in range(2):
                    for c, (a, e) in enumerate(CHUNKS):
                        act.wait_ge(zed, 3 * j + c + 1)
                        act.activation(z[:, j, a:e], m.ps[:, 3 * j + c, 0:CH], ACT.Identity,
                                       bias=m.gbias[:, j:j + 1]).then_inc(done, 1)
                act.wait_ge(done, 6)
                act.activation(l[:], z[:], ACT.Abs).then_inc(a_done, 1)
                act.wait_ge(a_done, 1)
                act.activation(l[:], l[:], ACT.Exp, scale=-1.0).then_inc(b_done, 1)
                act.wait_ge(b_done, 1)
                act.activation(l[:], l[:], ACT.Ln, bias=m.one[:, 0:1]).then_inc(x_done, 1)

            @block.vector
            def _(dve):
                chain = Chain(dve, chained)
                dve.wait_ge(a_done, 1)
                chain(dve.tensor_scalar(z[:], z[:], 0.0, 1.0 / 16, ALU.min, ALU.mult))
                dve.wait_ge(x_done, 1)
                chain(dve.scalar_tensor_tensor(l[:], l[:], -1.0 / 16, z[:], ALU.mult, ALU.add))
                dve.wait_ge(scan_loaded, 16)
                for j in range(2):
                    dve.tensor_tensor_scan(g.b[:, j, :], scan[:], l[:, j, :], 0.0, ALU.mult, ALU.add)

        spans = [(0, TP // GC, GC, GC // 2 - 1), (TP, NB, TS, 1)]
        e, u = z, l
        grown, powered, times = sem("gla_grown"), sem("gla_powered"), sem("gla_times")
        with nc.Block() as block:

            @block.vector
            def _(dve):
                chain = Chain(dve, chained, 2)

                def minus(out, sign, at):
                    for j in range(2):
                        for c0, n, w, mid in spans:
                            x = g.b[:, j, c0:c0 + n * w].rearrange("p (c t) -> p c t", t=w)
                            y = out[:, j, c0:c0 + n * w].rearrange("p (c t) -> p c t", t=w)
                            k = mid if at == "mid" else w - 1
                            ref = x[:, :, k:k + 1].broadcast_to([P, n, w])
                            ins = dve.tensor_tensor(y, *((x, ref) if sign > 0 else (ref, x)), ALU.subtract)
                            if (j, c0) != (1, TP):
                                chain(ins)
                    return ins

                qb, kb = m.f[:, QB:QB + 2, :], m.f[:, KB:KB + 2, :]
                minus(u, -1, "last").then_inc(grown, 1)
                chain(minus(e, 1, "mid"))
                dve.tensor_scalar(e[:], e[:], 40.0, -40.0, ALU.min, ALU.max).then_inc(grown, 1)
                dve.wait_ge(powered, 1)
                chain(dve.scalar_tensor_tensor(g.aq[:], qb, 64 ** -0.5, g.aq[:], ALU.mult, ALU.mult))
                dve.wait_ge(powered, 2)
                dve.tensor_tensor(g.kl[:], kb, u[:], ALU.mult).then_inc(times, 1)
                dve.wait_ge(powered, 3)
                dve.scalar_tensor_tensor(qb, qb, 64 ** -0.5, u[:], ALU.mult, ALU.mult)
                dve.wait_ge(powered, 4)
                dve.wait_ge(times, 1)
                dve.tensor_tensor(kb, kb, e[:], ALU.mult)

            @block.scalar
            def _(act):
                act.activation(g.aq[:], g.b[:], ACT.Exp).then_inc(powered, 1)
                for c0, n, w, _ in spans:
                    for j in range(2):
                        last = g.b[:, j, c0:c0 + n * w].rearrange("p (c t) -> p c t", t=w)[:, :, w - 1]
                        first = 0 if c0 == 0 else TP // GC
                        act.activation(g.el[:, j, first:first + n], last, ACT.Exp)
                act.wait_ge(grown, 1)
                act.activation(u[:], u[:], ACT.Exp).then_inc(powered, 1)
                act.wait_ge(grown, 2)
                act.wait_ge(times, 1)
                act.activation(u[:], e[:], ACT.Exp).then_inc(powered, 1)
                act.wait_ge(powered, 3)
                act.activation(e[:], e[:], ACT.Exp, scale=-1.0).then_inc(powered, 1)


def turn_keys(nc, m, g, sem):
    turned, kept = sem("turn_turned"), sem("turn_kept")
    with nc.Block() as block:

        @block.tensor
        def _(pe):
            for t in range(NT):
                r = tile_rows(t)
                if t >= 8:
                    pe.wait_ge(kept, t - 7)
                for j in range(2):
                    mm = pe.transpose(m.ps[0:r, t % 8, j * P:j * P + P], g.kl[:, j, t * P:t * P + r],
                                      m.const[:, C_ID:C_ID + P])
                mm.then_inc(turned, 1)

        @block.scalar
        def _(act):
            for t in range(NT):
                r = tile_rows(t)
                act.wait_ge(turned, t + 1)
                act.copy(g.kt[0:r, t, :], m.ps[0:r, t % 8, 0:256]).then_inc(kept, 1)


def gla_prompt(nc, m, g, d, sem):
    with ExitStack() as ctx:
        state = ctx.enter_context(nc.sbuf_tensor("gla_state", [P, 3, 2, P], F32))
        at = ctx.enter_context(nc.sbuf_tensor("gla_at", [P, 2, 2, GC], F32))
        scored, masked, updated, advanced, inner, outer, copied, kept = (
            sem(f"glap_{x}") for x in
            ("scored", "masked", "updated", "advanced", "inner", "outer", "copied", "kept"))
        with nc.Block() as block:

            @block.tensor
            def _(pe):
                def scores(n):
                    if n >= 1:
                        pe.wait_ge(masked, n)
                    for e in range(2):
                        for half in range(2):
                            for j in range(2):
                                a = n * P + half * GC
                                rows = slice(64 * e, 64 * e + 64)
                                mm = pe.matmul(m.ps[64 * half:64 * half + 64, e, j * GC:j * GC + GC],
                                               m.f[rows, KB + j, a:a + GC], m.f[rows, QB + j, a:a + GC],
                                               start=True, stop=True)
                    mm.then_inc(scored, 1)

                def updates(n):
                    for half in range(2):
                        if n >= 1:
                            pe.wait_ge(advanced, 1 + 2 * (n - 1) + half + 1)
                        for j in range(2):
                            for e in range(2):
                                rows = slice(64 * half, 64 * half + 64)
                                h = 2 * j + e
                                mm = pe.matmul(m.ps[64 * e:64 * e + 64, 6 + half, j * P:j * P + P],
                                               g.kt[rows, n, h * 64:h * 64 + 64], m.bv[rows, n, h * P:h * P + P],
                                               start=True, stop=True)
                        mm.then_inc(updated, 1)

                scores(0)
                updates(0)
                for n in range(BLK):
                    if n + 1 < BLK:
                        scores(n + 1)
                        updates(n + 1)
                    pe.wait_ge(masked, n + 1)
                    if n >= 1:
                        pe.wait_ge(copied, n)
                    for half in range(2):
                        rows = slice(64 * half, 64 * half + 64)
                        for j in range(2):
                            for e in range(2):
                                mm = pe.matmul(m.ps[:, 2 + half, e * P + j * GC:e * P + j * GC + GC],
                                               m.bv[rows, n, (2 * j + e) * P:(2 * j + e) * P + P],
                                               at[rows, e, j, :], start=True, stop=True)
                    mm.then_inc(inner, 1)
                    if n >= 1:
                        pe.wait_ge(kept, n)
                    for half in range(2):
                        c = 2 * n + half
                        pe.wait_ge(advanced, c + 1)
                        for e in range(2):
                            rows = slice(64 * e, 64 * e + 64)
                            for j in range(2):
                                mm = pe.matmul(m.ps[:, 4 + e, j * P + half * GC:j * P + half * GC + GC],
                                               state[rows, c % 3, j, :], g.aq[rows, j, c * GC:c * GC + GC],
                                               start=True, stop=True)
                        mm.then_inc(outer, 1)

            @block.vector
            def _(dve):
                dve.memset(state[:, 0], 0.0).then_inc(advanced, 1)
                tri = m.const[:, C_TRI:C_TRI + GC].unsqueeze(1).broadcast_to([P, 2, GC])

                def mask(n):
                    dve.wait_ge(scored, n + 1)
                    if n >= 1:
                        dve.wait_ge(inner, n)
                    for e in range(2):
                        ins = dve.tensor_tensor(at[:, e], m.ps[:, e, 0:P].rearrange("p (j t) -> p j t", j=2), tri,
                                                ALU.mult)
                    ins.then_inc(masked, 1)

                mask(0)
                for n in range(BLK):
                    for half in range(2):
                        c = 2 * n + half
                        dve.wait_ge(updated, c + 1)
                        dve.wait_ge(advanced, c + 1)
                        if c >= 2:
                            dve.wait_ge(outer, c - 1)
                        for j in range(2):
                            ins = dve.scalar_tensor_tensor(state[:, (c + 1) % 3, j, :], state[:, c % 3, j, :],
                                                           g.el[:, j, c:c + 1], m.ps[:, 6 + half, j * P:j * P + P],
                                                           ALU.mult, ALU.add)
                        ins.then_inc(advanced, 1)
                    dve.wait_ge(copied, n + 1)
                    for e, dst in enumerate((g.aq, g.kl)):
                        x = dst[:, :, n * P:n * P + P]
                        ins = dve.tensor_tensor(x, x, m.ps[:, 4 + e, 0:256].rearrange("p (j t) -> p j t", j=2), ALU.add)
                    ins.then_inc(kept, 1)
                    if n + 1 < BLK:
                        mask(n + 1)

            @block.scalar
            def _(act):
                for n in range(BLK):
                    act.wait_ge(inner, n + 1)
                    act.wait_ge(outer, 2 * n + 2)
                    for half in range(2):
                        for e, dst in enumerate((g.aq, g.kl)):
                            a = n * P + half * GC
                            ins = act.copy(dst[:, :, a:a + GC],
                                           m.ps[:, 2 + half, e * P:e * P + P].rearrange("p (j t) -> p j t", j=2))
                    ins.then_inc(copied, 1)

            @block.sync
            def _(sp):
                sp.wait_ge(advanced, 1 + 2 * BLK)
                sp.dma_start(d["out_sp"], state[:, (2 * BLK) % 3]).then_inc(m.stored, 16)
                sp.wait_ge(m.stored, m.stores)


def gla_samples(nc, m, g, d, sem):
    with ExitStack() as ctx:
        s0 = ctx.enter_context(nc.sbuf_tensor("glas_s0", [P, 2, NB, P], F32))
        vm = ctx.enter_context(nc.sbuf_tensor("glas_vm", [32, NB, 512], F32))
        at = ctx.enter_context(nc.sbuf_tensor("glas_at", [32, 2, 2, 32], F32))
        loaded, scored, masked, inner, outer, copied, split, updated, advanced, out = (
            sem(f"glas_{x}") for x in
            ("loaded", "scored", "masked", "inner", "outer", "copied", "split", "updated", "advanced", "out"))
        cols = slice(TP, T)
        with nc.Block() as block:

            @block.sync
            def _(sp):
                for e in range(2):
                    for j in range(2):
                        sp.dma_start(s0[64 * e:64 * e + 64, j], d["state"][:, 2 * j + e].rearrange("b k v -> k b v")
                                     ).then_inc(loaded, 16)
                sp.wait_ge(advanced, 1)
                for e in range(2):
                    for j in range(2):
                        sp.dma_start(d["out_ss"][:, 2 * j + e].rearrange("b k v -> k b v"), s0[64 * e:64 * e + 64, j]
                                     ).then_inc(out, 16)
                sp.wait_ge(out, 64)

            @block.tensor
            def _(pe):
                for e in range(2):
                    rows = slice(64 * e, 64 * e + 64)
                    for j in range(2):
                        mm = pe.matmul(m.ps[0:32, e, j * 32:j * 32 + 32], m.f[rows, KB + j, cols], m.f[rows, QB + j, cols],
                                       start=True, stop=True)
                mm.then_inc(scored, 1)
                pe.wait_ge(masked, 1)
                for e in range(2):
                    for j in range(2):
                        mm = pe.matmul(m.ps[:, 2, e * 64 + j * 32:e * 64 + j * 32 + 32],
                                       m.bv[0:32, BLK, (2 * j + e) * P:(2 * j + e) * P + P], at[:, e, j, :],
                                       start=True, stop=True)
                mm.then_inc(inner, 1)
                pe.wait_ge(loaded, 64)
                for e in range(2):
                    rows = slice(64 * e, 64 * e + 64)
                    for j in range(2):
                        for b in range(NB):
                            c = j * 32 + TS * b
                            mm = pe.matmul(m.ps[:, 4 + e, c:c + TS], s0[rows, j, b, :],
                                           g.aq[rows, j, TP + TS * b:TP + TS * b + TS], start=True, stop=True)
                mm.then_inc(outer, 1)
                pe.wait_ge(split, 1)
                banks = [6, 7, 0, 3]
                for j in range(2):
                    for q in range(2):
                        for e in range(2):
                            h = 2 * j + e
                            mm = pe.matmul(m.ps[64 * e:64 * e + 64, banks[2 * j + q], :].rearrange("p (b v) -> p b v", b=4),
                                           g.kt[0:32, BLK, h * 64:h * 64 + 64],
                                           vm[:, 4 * q:4 * q + 4, h * P:h * P + P], start=True, stop=True)
                mm.then_inc(updated, 1)

            @block.vector
            def _(dve):
                own = m.const[0:32, C_SEL:C_SEL + NB].unsqueeze(2).broadcast_to([32, NB, 512])
                dve.wait_ge(scored, 1)
                tri = m.const[0:32, C_TRIS:C_TRIS + 32].unsqueeze(1).broadcast_to([32, 2, 32])
                for e in range(2):
                    ins = dve.tensor_tensor(at[:, e], m.ps[0:32, e, 0:64].rearrange("p (j t) -> p j t", j=2), tri, ALU.mult)
                ins.then_inc(masked, 1)
                dve.tensor_tensor(vm[:], m.bv[0:32, BLK, :].unsqueeze(1).broadcast_to([32, NB, 512]), own,
                                  ALU.mult).then_inc(split, 1)
                dve.wait_ge(copied, 1)
                dve.wait_ge(outer, 1)
                for e, dst in enumerate((g.aq, g.kl)):
                    x = dst[:, :, cols]
                    dve.tensor_tensor(x, x, m.ps[:, 4 + e, 0:64].rearrange("p (j t) -> p j t", j=2), ALU.add)
                dve.wait_ge(updated, 1)
                banks = [6, 7, 0, 3]
                for j in range(2):
                    for b in range(NB):
                        ins = dve.scalar_tensor_tensor(s0[:, j, b, :], s0[:, j, b, :],
                                                       g.el[:, j, TP // GC + b:TP // GC + b + 1],
                                                       m.ps[:, banks[2 * j + b // 4], (b % 4) * P:(b % 4) * P + P],
                                                       ALU.mult, ALU.add)
                ins.then_inc(advanced, 1)

            @block.scalar
            def _(act):
                act.wait_ge(inner, 1)
                act.wait_ge(outer, 1)
                for e, dst in enumerate((g.aq, g.kl)):
                    ins = act.copy(dst[:, :, cols], m.ps[:, 2, e * 64:e * 64 + 64].rearrange("p (j t) -> p j t", j=2))
                ins.then_inc(copied, 1)


def finish_gla(nc, m, g, d, sem):
    units = [((g.aq, g.kl)[h % 2][:, h // 2, a:z], m.ones[:], P, m.gng) for h in range(4) for a, z in CHUNKS]
    norm_units(nc, m, sem, "glan", units)
    sig, gated = sem("silu_sigmoid"), sem("silu_gated")
    with ExitStack() as ctx:
        x = ctx.enter_context(nc.sbuf_tensor("silu_x", [P, 2, T], F32))
        with nc.Block() as block:

            @block.scalar
            def _(act):
                for h in range(4):
                    if h >= 2:
                        act.wait_ge(gated, h - 1)
                    act.activation(x[:, h % 2], m.f[:, RB + h, :], ACT.Sigmoid).then_inc(sig, 1)

            @block.vector
            def _(dve):
                for h in range(4):
                    dve.wait_ge(sig, h + 1)
                    r = m.f[:, RB + h, :]
                    chain_in = dve.tensor_tensor(r, r, x[:, h % 2], ALU.mult)
                    chain_in.then_inc(gated, 1)
                    dve.wait_ge(gated, h + 1)
                    dve.tensor_tensor(r, r, (g.aq, g.kl)[h % 2][:, h // 2, :], ALU.mult)


def merge(nc, m, d, sem):
    first = (QA, RB, QC)
    with ExitStack() as ctx:
        w = ctx.enter_context(nc.sbuf_tensor("wm_ring", [P, 2, 36, P], F32))
        sg = ctx.enter_context(nc.sbuf_tensor("merge_sg", [P, 4, CH], F32))
        loaded = [sem("wm_loaded0"), sem("wm_loaded1")]
        done, gated, added, multiplied = (sem(f"merge_{x}") for x in ("done", "gated", "added", "multiplied"))
        units = [(j, c, r) for j in range(KT) for c in range(3) for r in range(3)]
        with nc.Block() as block:

            @block.sync
            def _(sp):
                for j in range(KT):
                    if j >= 2:
                        sp.wait_ge(done, 9 * (j - 1))
                    sp.dma_start(w[:, j % 2], d["w_m"][j]).then_inc(loaded[j % 2], 16)

            @block.tensor
            def _(pe):
                for u, (j, c, r) in enumerate(units):
                    a, z = CHUNKS[c]
                    if u % 9 == 0:
                        pe.wait_ge(loaded[j % 2], 16 * (j // 2 + 1))
                    if u >= 4:
                        pe.wait_ge(multiplied, u - 3)
                    for k in range(KT):
                        pe.matmul(m.ps[:, 2 * (u % 4), 0:CH], w[:, j % 2, 8 * r + k, :], m.xn[:, k, a:z],
                                  start=(k == 0), stop=(k == KT - 1))
                    for k in range(4):
                        mm = pe.matmul(m.ps[:, 2 * (u % 4) + 1, 0:CH], w[:, j % 2, 24 + 4 * r + k, :],
                                       m.f[:, first[r] + k, a:z], start=(k == 0), stop=(k == 3))
                    mm.then_inc(done, 1)

            def adds(v):
                return 2 * (v // 3) + v % 3

            @block.scalar
            def _(act):
                for u, (j, c, r) in enumerate(units):
                    act.wait_ge(done, u + 1)
                    if u >= 4:
                        act.wait_ge(multiplied, u - 3)
                        if adds(u - 4):
                            act.wait_ge(added, adds(u - 4))
                    act.activation(sg[:, u % 4], m.ps[:, 2 * (u % 4), 0:CH], ACT.Sigmoid,
                                   bias=m.gates_b[:, j, r:r + 1]).then_inc(gated, 1)

            @block.vector
            def _(dve):
                for u, (j, c, r) in enumerate(units):
                    a, z = CHUNKS[c]
                    dst = m.h[:, j, a:z]
                    dve.wait_ge(gated, u + 1)
                    x = dst if r == 0 else sg[:, u % 4]
                    dve.tensor_tensor(x, sg[:, u % 4], m.ps[:, 2 * (u % 4) + 1, 0:CH], ALU.mult).then_inc(multiplied, 1)
                    dve.wait_ge(multiplied, u + 1)
                    if r:
                        dve.tensor_tensor(dst, dst, x, ALU.add).then_inc(added, 1)
                        dve.wait_ge(added, adds(u))


def project_out(nc, m, d, sem):
    with ExitStack() as ctx:
        w = ctx.enter_context(nc.sbuf_tensor("wo_ring", [P, 2, KT, P], F32))
        x_loaded = sem("wo_x_loaded")
        loaded = [sem("wo_loaded0"), sem("wo_loaded1")]
        done, added = sem("wo_done"), sem("wo_added")
        with nc.Block() as block:

            @block.sync
            def _(sp):
                for n in range(KT):
                    if n >= 2:
                        sp.wait_ge(done, 3 * (n - 1))
                    sp.dma_start(w[:, n % 2], d["w_out"][n]).then_inc(loaded[n % 2], 16)
                    if n == 0:
                        sp.dma_start(m.x2[:], d["x"][:, :, 0:T]).then_inc(x_loaded, 16)

            @block.tensor
            def _(pe):
                for n in range(KT):
                    pe.wait_ge(loaded[n % 2], 16 * (n // 2 + 1))
                    for c, (a, z) in enumerate(CHUNKS):
                        u = 3 * n + c
                        if u >= 8:
                            pe.wait_ge(added, u - 7)
                        for k in range(KT):
                            mm = pe.matmul(m.ps[:, u % 8, 0:CH], w[:, n % 2, k, :], m.h[:, k, a:z], start=(k == 0),
                                           stop=(k == KT - 1))
                        mm.then_inc(done, 1)

            @block.vector
            def _(dve):
                dve.wait_ge(x_loaded, 16)
                for n in range(KT):
                    for c, (a, z) in enumerate(CHUNKS):
                        u = 3 * n + c
                        dve.wait_ge(done, u + 1)
                        dve.tensor_tensor(m.x2[:, n, a:z], m.x2[:, n, a:z], m.ps[:, u % 8, 0:CH], ALU.add).then_inc(added, 1)


def choose_experts(nc, m, d, sem):
    NEGK = -3e38
    with ExitStack() as ctx:
        def sb(name, shape, dt=F32):
            return ctx.enter_context(nc.sbuf_tensor(name, shape, dt))

        raw = sb("wq_raw", [P, KT, P])
        w = (sb("wq_high", [P, 2, KT, P], F32R), sb("wq_low", [P, 2, KT, P], F32R))
        keys = sb("keys", [P, 2, NK])
        q = sb("pq", [P, 2, T])
        sc = sb("psc", [P, 2, NT, NK])
        top = sb("ptop", [P, 2, NT, TOPK])
        idx = sb("pidx", [P, 2, NT, TOPK], U32)
        idf = sb("pidf", [P, 2, NT, TOPK])
        cand = sb("pcand", [P, NT, TOPK, TOPK])
        best = sb("pbest", [P, NT, TOPK])
        expo = sb("pexpo", [P, NT, TOPK])
        pos = sb("ppos", [P, NT, TOPK], U32)
        half = sb("phalf", [P, 2, NT, TOPK], U32)
        halff = sb("phalff", [P, 2, NT, TOPK])
        tot = sb("ptot", [P, NT])
        w_loaded, w_high, w_low, keys_loaded = (sem(f"wq_{x}") for x in ("loaded", "high", "low", "keys_loaded"))
        projected, q_kept, scored, sc_kept, sc_used, seq, centred, expd = (
            sem(f"peer_{x}") for x in
            ("projected", "q_kept", "scored", "sc_kept", "sc_used", "seq", "centred", "expd"))
        with nc.Block() as block:

            def exp_gates(act, h):
                act.wait_ge(centred, h + 1)
                act.activation(expo[:], expo[:], ACT.Exp).then_inc(expd, 1)

            def gate_sums(h, dve, step, after):
                step(dve.tensor_reduce(tot[:], expo[:], AX, ALU.add))
                after(0)
                step(dve.reciprocal(tot[:], tot[:]))
                after(0)
                step(dve.tensor_tensor(m.gate[:, :, h * TOPK:h * TOPK + TOPK], expo[:],
                                       tot[:].unsqueeze(2).broadcast_to([P, NT, TOPK]), ALU.mult))
                after(0)

            @block.sync
            def _(sp):
                sp.dma_start(keys[:], d["keys"]).then_inc(keys_loaded, 16)
                for n in range(2 * HEADS):
                    if n:
                        sp.wait_ge(w_low, n)
                    sp.dma_start(raw[:], d["w_q"][n]).then_inc(w_loaded, 16)

            @block.tensor
            def _(pe):
                def queries(n):
                    pe.wait_ge(w_low, n + 1)
                    if n >= 2:
                        pe.wait_ge(q_kept, n - 1)
                    for c, (a, z) in enumerate(CHUNKS):
                        for k in range(KT):
                            mm = exact_product(pe, m.ps[:, 3 * (n % 2) + c, 0:CH], [x[:, n % 2, k, :] for x in w],
                                               [x[:, k, a:z] for x in m.hn], k == 0, k == KT - 1)
                    mm.then_inc(projected, 1)

                def scores(n):
                    pe.wait_ge(q_kept, n + 1)
                    for g in range(3):
                        u = 3 * n + g
                        if u >= 2:
                            pe.wait_ge(sc_kept, u - 1)
                        for t in range(4 * g, min(4 * g + 4, NT)):
                            r = tile_rows(t)
                            mm = pe.matmul(m.ps[0:r, 6 + u % 2, (t % 4) * NK:(t % 4) * NK + NK],
                                           q[:, n % 2, t * P:t * P + r], keys[:, n % 2, :], start=True, stop=True)
                        mm.then_inc(scored, 1)

                queries(0)
                pe.wait_ge(keys_loaded, 16)
                for n in range(2 * HEADS):
                    if n + 1 < 2 * HEADS:
                        queries(n + 1)
                    scores(n)

            @block.gpsimd
            def _(pool):
                for n in range(2 * HEADS):
                    pool.wait_ge(w_high, n + 1)
                    pool.tensor_tensor(w[1][:, n % 2], raw[:], w[0][:, n % 2].bitcast(F32), ALU.subtract).then_inc(w_low, 1)

            @block.scalar
            def _(act):
                def round_weights(n):
                    if n < 2 * HEADS:
                        act.wait_ge(w_loaded, 16 * (n + 1))
                        if n >= 2:
                            act.wait_ge(projected, n - 1)
                        act.copy(w[0][:, n % 2], raw[:]).then_inc(w_high, 1)

                def keep_scores(n):
                    if n >= 2:
                        act.wait_ge(sc_used, n - 1)
                    for g in range(3):
                        u = 3 * n + g
                        act.wait_ge(scored, u + 1)
                        r, k = (P, 4) if g < 2 else (T - TP, 1)
                        act.copy(sc[0:r, n % 2, 4 * g:4 * g + k, :],
                                 m.ps[0:r, 6 + u % 2, 0:k * NK].rearrange("p (t k) -> p t k", k=NK)).then_inc(sc_kept, 1)

                def keep_queries(n):
                    act.wait_ge(projected, n + 1)
                    if n >= 2:
                        act.wait_ge(scored, 3 * (n - 1))
                    ins = act.copy(q[:, n % 2, :].rearrange("p (c t) -> p c t", c=3),
                                   m.ps[:, 3 * (n % 2):3 * (n % 2) + 3, 0:CH])
                    ins.then_inc(q_kept, 1)

                round_weights(0)
                round_weights(1)
                keep_queries(0)
                for n in range(2 * HEADS):
                    round_weights(n + 2)
                    if n + 1 < 2 * HEADS:
                        keep_queries(n + 1)
                    keep_scores(n)
                    if n % 2 and n >= 3:
                        exp_gates(act, n // 2 - 1)
                exp_gates(act, HEADS - 1)

            @block.vector
            def _(dve):
                n_seq = 0

                def step(ins):
                    nonlocal n_seq
                    ins.then_inc(seq, 1)
                    n_seq += 1

                def after(k):
                    dve.wait_ge(seq, n_seq - k)

                for x in (idx[:, :, BLK, :], best[:, BLK, :], pos[:, BLK, :]):
                    step(dve.memset(x, 0))
                after(0)

                def best16(values, out, where, tiles):
                    for t in tiles:
                        step(dve.max(out(t, 0), values(t)))
                    for t in tiles:
                        after(len(tiles) - 1)
                        step(dve.max_index(where(t, 0), out(t, 0), values(t)))
                    for t in tiles:
                        after(len(tiles) - 1)
                        step(dve.match_replace(values(t), out(t, 0), values(t), NEGK))
                    for t in tiles:
                        after(len(tiles) - 1)
                        step(dve.max(out(t, 1), values(t)))
                    for t in tiles:
                        after(len(tiles) - 1)
                        step(dve.max_index(where(t, 1), out(t, 1), values(t)))

                tiles = range(NT)
                for h in range(HEADS):
                    for s in range(2):
                        dve.wait_ge(sc_kept, 3 * (2 * h + s + 1))
                        best16(lambda t: sc[0:tile_rows(t), s, t, :],
                               lambda t, i: top[0:tile_rows(t), s, t, 8 * i:8 * i + 8],
                               lambda t, i: idx[0:tile_rows(t), s, t, 8 * i:8 * i + 8], tiles)
                        after(0)
                        dve.tensor_copy(idf[:, s], idx[:, s]).then_inc(sc_used, 1)
                    for t in tiles:
                        r = tile_rows(t)
                        step(dve.tensor_tensor(cand[0:r, t], top[0:r, 0, t, :].unsqueeze(2).broadcast_to([r, TOPK, TOPK]),
                                               top[0:r, 1, t, :].unsqueeze(1).broadcast_to([r, TOPK, TOPK]), ALU.add))
                    after(0)
                    if h >= 1:
                        dve.wait_ge(expd, h)
                        gate_sums(h - 1, dve, step, after)
                    best16(lambda t: cand[0:tile_rows(t), t].rearrange("p a b -> p (a b)"),
                           lambda t, i: best[0:tile_rows(t), t, 8 * i:8 * i + 8],
                           lambda t, i: pos[0:tile_rows(t), t, 8 * i:8 * i + 8], tiles)
                    after(0)
                    dve.tensor_tensor(expo[:], best[:], best[:, :, 0:1].broadcast_to([P, NT, TOPK]), ALU.subtract).then_inc(centred, 1)
                    step(dve.tensor_scalar(half[:, 0], pos[:], 4, None, ALU.logical_shift_right))
                    step(dve.tensor_scalar(half[:, 1], pos[:], 15, None, ALU.bitwise_and))
                    after(0)
                    step(dve.tensor_copy(halff[:], half[:]))
                    after(0)
                    iota = m.const[:, C_IOTA:C_IOTA + TOPK].unsqueeze(1).unsqueeze(1).broadcast_to([P, NT, TOPK, TOPK])
                    for s, dst in enumerate((m.e1, m.e2)):
                        step(dve.tensor_tensor(cand[:], halff[:, s].unsqueeze(3).broadcast_to([P, NT, TOPK, TOPK]), iota,
                                               ALU.is_equal))
                        after(0)
                        step(dve.tensor_tensor(cand[:], cand[:],
                                               idf[:, s].unsqueeze(2).broadcast_to([P, NT, TOPK, TOPK]), ALU.mult))
                        after(0)
                        step(dve.tensor_reduce(dst[:, :, h * TOPK:h * TOPK + TOPK], cand[:], AX, ALU.add))
                        after(0)
                dve.wait_ge(expd, HEADS)
                gate_sums(HEADS - 1, dve, step, after)


def build_gate_matrix(nc, m, d, sem):
    with ExitStack() as ctx:
        def sb(name, shape, dt=F32):
            return ctx.enter_context(nc.sbuf_tensor(name, shape, dt))

        turned_in = sb("gm_in", [P, 3, T])
        RING = 8
        hot = sb("gm_hot", [P, RING, P])
        wgt = sb("gm_wgt", [P, RING, P])
        out = sb("gm_out", [P, 2, NK, TBG])
        turned, t_kept, made, used, copied = (sem(f"gm_{x}") for x in ("turned", "kept", "made", "used", "copied"))
        stored = [sem("gm_stored0"), sem("gm_stored1")]
        srcs = (m.e1, m.e2, m.gate)
        iota = m.const[:, C_IOTA:C_IOTA + NK]
        with nc.Block() as block:

            @block.tensor
            def _(pe):
                for s in range(3):
                    for t in range(NT):
                        r, u = tile_rows(t), s * NT + t
                        if u >= 8:
                            pe.wait_ge(t_kept, u - 7)
                        pe.transpose(m.ps[:, u % 8, 0:r], srcs[s][0:r, t, :],
                                     m.const[0:r, C_ID:C_ID + r]).then_inc(turned, 1)

            @block.scalar
            def _(act):
                for s in range(3):
                    for t in range(NT):
                        r, u = tile_rows(t), s * NT + t
                        act.wait_ge(turned, u + 1)
                        act.copy(turned_in[:, s, t * P:t * P + r], m.ps[:, u % 8, 0:r]).then_inc(t_kept, 1)

        GROUPS = TBG // 4
        with nc.Block() as block:

            @block.vector
            def _(dve):
                def group(g, first, q):
                    if not first:
                        dve.wait_ge(used, g - 1)
                    for i in range(4):
                        t = 4 * g + i
                        col = bass.ds(t, 1) if not isinstance(t, int) else slice(t, t + 1)
                        dve.tensor_scalar(hot[:, 4 * q + i, :], iota, turned_in[:, 0, col], None, ALU.is_equal)
                        ins = dve.tensor_scalar(wgt[:, 4 * q + i, :], iota, turned_in[:, 1, col], turned_in[:, 2, col],
                                                ALU.is_equal, ALU.mult)
                    ins.then_inc(made, 1)

                group(0, True, 0)
                group(1, True, 1)
                with dve.Fori(1, T // 8) as i:
                    group(2 * i, False, 0)
                    group(2 * i + 1, False, 1)

            @block.tensor
            def _(pe):
                def group(g, first, q):
                    pe.wait_ge(made, g + 1)
                    if not first:
                        pe.wait_ge(copied, g - 1)
                    for i in range(4):
                        mm = pe.matmul(m.ps[:, q, i * P:i * P + P], hot[:, 4 * q + i, :], wgt[:, 4 * q + i, :],
                                       start=True, stop=True)
                    mm.then_inc(used, 1)

                group(0, True, 0)
                group(1, True, 1)
                with pe.Fori(1, T // 8) as i:
                    group(2 * i, False, 0)
                    group(2 * i + 1, False, 1)

            @block.scalar
            def _(act):
                for blk in range(T // TBG):
                    if blk >= 2:
                        act.wait_ge(stored[blk % 2], 16 * (blk // 2))
                    with act.Fori(0, GROUPS // 2) as i:
                        for q in range(2):
                            g = 2 * i + q
                            act.wait_ge(used, g + (blk * GROUPS + 1))
                            act.copy(out[:, blk % 2, :, bass.ds(4 * g, 4)].rearrange("p n t -> p t n"),
                                     m.ps[:, q, :].rearrange("p (t n) -> p t n", t=4)).then_inc(copied, 1)

            @block.sync
            def _(sp):
                for blk in range(T // TBG):
                    sp.wait_ge(copied, GROUPS * (blk + 1))
                    sp.dma_start(d["gates"][blk], out[:, blk % 2]).then_inc(stored[blk % 2], 16)
                for i in range(2):
                    sp.wait_ge(stored[i], 16 * (T // TBG // 2))


def run_experts(nc, m, d, sem):
    GR = 2
    LAST = NK // GR - 1
    with ExitStack() as ctx:
        def sb(name, shape, dt=F32):
            return ctx.enter_context(nc.sbuf_tensor(name, shape, dt))

        u_raw = sb("x_u", [P, KT, P])
        u = (sb("x_u_high", [P, GR, KT, P], F32R), sb("x_u_low", [P, GR, KT, P], F32R))
        v_raw = [m.xn[:, 4 * i:4 * i + 4, T:TM] for i in range(GR)]
        v = (sb("x_v_high", [P, GR, D], F32R), sb("x_v_low", [P, GR, D], F32R))
        gates = sb("x_g", [P, T // TBG, GR, TBG])
        act = sb("x_act", [P, GR, T])
        split = (sb("x_act_high", [P, 2, GR, T], F32R), sb("x_act_low", [P, 2, GR, T], F32R))
        u_loaded, g_loaded = sem("x_u_loaded"), sem("x_g_loaded")
        v_loaded = [sem(f"x_v_loaded{i}") for i in range(GR)]
        hidden, gelu_done, gated, act_high, act_low, u_high, u_low, v_high, v_low, multiplied, added = (
            sem(f"x_{x}") for x in ("hidden", "gelu", "gated", "act_high", "act_low", "u_high", "u_low", "v_high",
                                    "v_low", "multiplied", "added"))

        def all_groups(eng, group):
            group(0, 0, True, False, False)
            group(1, 1, False, True, False)
            with eng.Fori(1, LAST // 2) as i:
                group(2 * i, 0, False, False, False)
                group(2 * i + 1, 1, False, False, False)
            group(LAST - 1, 0, False, False, False)
            group(LAST, 1, False, False, True)

        with nc.Block() as block:

            @block.sync
            def _(sp):
                def load_v(n, i, early):
                    if not early:
                        sp.wait_ge(v_low, n - 1)
                    sp.dma_start(v_raw[i], d["v"][bass.ds(n, 1)].rearrange("o p (k e) -> p (o k) e", k=4)).then_inc(v_loaded[i], 16)

                def group(g, p, first, second, last):
                    for i in range(GR):
                        n = g * GR + i
                        if not (first and i == 0):
                            sp.wait_ge(u_low, n)
                        sp.dma_start(u_raw[:], d["u"][bass.ds(n, 1)].rearrange("o p k n -> p (o k) n")).then_inc(u_loaded, 16)
                        if i == 0:
                            if not first:
                                sp.wait_ge(gated, GR * g)
                            src = bass.AP(tensor=d["gates"].tensor, offset=g * (GR * TBG),
                                          ap=[[NK * TBG, P], [NK * NK * TBG, T // TBG], [1, GR * TBG]])
                            sp.dma_start(gates[:].rearrange("p b i t -> p b (i t)"), src).then_inc(g_loaded, 16)
                        if not (first and i == 0):
                            load_v(n - 1, 1 - i, first or (second and i == 0))

                all_groups(sp, group)
                load_v(NK - 1, 1, False)

            @block.tensor
            def _(pe):
                def hidden_products(g, first):
                    for i in range(GR):
                        n = g * GR + i
                        pe.wait_ge(u_low, n + 1)
                        if not first:
                            pe.wait_ge(gelu_done, 3 * (n - 1))
                        for c, (a, z) in enumerate(CHUNKS):
                            for k in range(KT):
                                mm = exact_product(pe, m.ps[:, 3 * i + c, 0:CH], [x[:, i, k, :] for x in u],
                                                   [x[:, k, a:z] for x in m.hn], k == 0, k == KT - 1)
                            mm.then_inc(hidden, 1)

                def output_products(g, p, first):
                    pe.wait_ge(v_low, GR * g + GR)
                    pe.wait_ge(act_low, GR * g + GR)
                    for x in range(24):
                        j, c = x // 3, x % 3
                        a, z = CHUNKS[c]
                        if not (first and x < 2):
                            pe.wait_ge(added, 24 * g + x - 1)
                        for i in range(GR):
                            mm = exact_product(pe, m.ps[:, 6 + x % 2, 0:CH], [y[:, i, j * P:j * P + P] for y in v],
                                               [y[:, p, i, a:z] for y in split], i == 0, i == GR - 1)
                        mm.then_inc(multiplied, 1)

                hidden_products(0, True)
                hidden_products(1, False)
                output_products(0, 0, True)
                with pe.Fori(1, NK // GR // 2) as i:
                    hidden_products(2 * i, False)
                    output_products(2 * i - 1, 1, False)
                    hidden_products(2 * i + 1, False)
                    output_products(2 * i, 0, False)
                output_products(LAST, 1, False)

            @block.scalar
            def _(sc):
                def round_u(n, i, first=False):
                    sc.wait_ge(u_loaded, 16 * (n + 1))
                    if not first:
                        sc.wait_ge(hidden, 3 * (n - 1))
                    sc.copy(u[0][:, i], u_raw[:]).then_inc(u_high, 1)

                def round_act(g, p, i, early):
                    sc.wait_ge(gated, GR * g + i + 1)
                    if not early:
                        sc.wait_ge(multiplied, 24 * (g - 1))
                    sc.copy(split[0][:, p, i], act[:, i]).then_inc(act_high, 1)

                def round_v(g, i, first):
                    sc.wait_ge(v_loaded[i], 16 * (g + 1))
                    if not first:
                        sc.wait_ge(multiplied, 24 * g)
                    sc.copy(v[0][:, i].rearrange("p (k e) -> p k e", k=4), v_raw[i]).then_inc(v_high, 1)

                def gelu(n, i, first):
                    if not first:
                        sc.wait_ge(act_low, n - 1)
                    for c, (a, z) in enumerate(CHUNKS):
                        sc.wait_ge(hidden, 3 * n + c + 1)
                        sc.activation(act[:, i, a:z], m.ps[:, 3 * i + c, 0:CH], ACT.Gelu).then_inc(gelu_done, 1)

                def group(g, p, first, second, last):
                    n = GR * g
                    round_u(n + 1, 1, first)
                    if not first:
                        round_act(g - 1, 1 - p, 1, second)
                        round_v(g - 1, 0, second)
                    gelu(n, 0, first)
                    if not last:
                        round_u(n + 2, 0)
                    round_act(g, p, 0, first or second)
                    if not first:
                        round_v(g - 1, 1, second)
                    gelu(n + 1, 1, first)

                round_u(0, 0, True)
                all_groups(sc, group)
                round_act(LAST, LAST % 2, 1, False)
                for i in range(GR):
                    round_v(LAST, i, False)

            @block.gpsimd
            def _(pool):
                def group(g):
                    pool.wait_ge(g_loaded, 16 * (g + 1))
                    for i in range(GR):
                        pool.wait_ge(gelu_done, 3 * (g * GR + i) + 3)
                        x = act[:, i].rearrange("p (b t) -> p b t", t=TBG)
                        pool.tensor_tensor(x, x, gates[:, :, i], ALU.mult).then_inc(gated, 1)

                with pool.Fori(0, NK // GR) as g:
                    group(g)

            @block.vector
            def _(dve):
                def rest_u(n, i):
                    dve.wait_ge(u_high, n + 1)
                    dve.tensor_tensor(u[1][:, i], u_raw[:], u[0][:, i].bitcast(F32), ALU.subtract).then_inc(u_low, 1)

                def rest_act(g, p, i):
                    dve.wait_ge(act_high, GR * g + i + 1)
                    dve.tensor_tensor(split[1][:, p, i], act[:, i], split[0][:, p, i].bitcast(F32),
                                      ALU.subtract).then_inc(act_low, 1)

                def rest_v(g, i):
                    dve.wait_ge(v_high, GR * g + i + 1)
                    dve.tensor_tensor(v[1][:, i].rearrange("p (k e) -> p k e", k=4), v_raw[i],
                                      v[0][:, i].bitcast(F32).rearrange("p (k e) -> p k e", k=4),
                                      ALU.subtract).then_inc(v_low, 1)

                def add_outputs(g):
                    for x in range(24):
                        j, c = x // 3, x % 3
                        a, z = CHUNKS[c]
                        dve.wait_ge(multiplied, 24 * g + x + 1)
                        dve.tensor_tensor(m.x2[:, j, a:z], m.x2[:, j, a:z], m.ps[:, 6 + x % 2, 0:CH], ALU.add).then_inc(added, 1)

                def group(g, p, first, second, last):
                    n = GR * g
                    rest_u(n + 1, 1)
                    if not first:
                        rest_act(g - 1, 1 - p, 1)
                        rest_v(g - 1, 0)
                    if not last:
                        rest_u(n + 2, 0)
                    rest_act(g, p, 0)
                    if not first:
                        rest_v(g - 1, 1)
                        add_outputs(g - 1)

                rest_u(0, 0)
                all_groups(dve, group)
                rest_act(LAST, LAST % 2, 1)
                for i in range(GR):
                    rest_v(LAST, i)
                add_outputs(LAST)


def store_output(nc, m, d, sem):
    out = sem("y_stored")
    with nc.Block() as block:

        @block.sync
        def _(sp):
            sp.dma_start(d["out_y"], m.x2[:]).then_inc(out, 16)
            sp.wait_ge(out, 16)
            sp.wait_ge(m.stored, m.stores)


def build(nc, d, until=99):
    with ExitStack() as ctx:
        m = Mem()
        signals, handles = ExitStack(), []

        def sem(name):
            handles.append(signals.enter_context(nc.semaphore(name)))
            return handles[-1]

        def clear_semaphores():
            with nc.Block() as block:

                @block.sync
                def _(sp):
                    for x in handles:
                        sp.sem_clear(x)

            signals.close()
            handles.clear()

        def sb(stack, name, shape, dt=F32):
            return stack.enter_context(nc.sbuf_tensor(name, shape, dt))

        m.ps = ctx.enter_context(nc.psum_tensor("ps", [P, 8, 512], F32))
        m.const, m.ones = sb(ctx, "const", [P, C_END]), sb(ctx, "ones", [P, P])
        m.norm2 = sb(ctx, "norm2", [P, KT])
        m.eps, m.one = sb(ctx, "eps", [P, 1]), sb(ctx, "one", [P, 1])
        m.xn = sb(ctx, "xn", [P, KT, TM])
        m.x2 = m.xn[:, :, 0:T]
        m.stored = ctx.enter_context(nc.semaphore("stored"))
        m.stores = 16 * (1 + 1 + NB + 1 + 2 + 1 + 1)
        with ExitStack() as mix:
            m.norm1, m.memg = sb(mix, "norm1", [P, KT]), sb(mix, "memg", [P, KT])
            m.qg, m.kg, m.cqg, m.ckg, m.gng = (sb(mix, x, [P, 1]) for x in ("qg", "kg", "cqg", "ckg", "gng"))
            m.gbias = sb(mix, "gbias", [P, 2])
            m.gates_b = sb(mix, "gates_b", [P, KT, 3])
            m.sink, m.sink_s = sb(mix, "sink", [P, 8]), sb(mix, "sink_s", [P, 2])
            m.relb, m.w2 = sb(mix, "relb", [32, 8]), sb(mix, "w2", [16, 256])
            m.f = sb(mix, "features", [P, NF, T])
            load_small(nc, m, d, sem)
            norm_features(nc, m, sem, "n1", m.xn, m.xn, [(0, T, m.norm1), (T, TM, m.memg)], d["x"])
            with ExitStack() as values:
                m.av, m.bv = sb(values, "av", [P, NT, P]), sb(values, "bv", [P, NT, 512])
                m.lr = sb(values, "lr", [16, T])
                with ExitStack() as memory:
                    m.mk, m.mv = sb(memory, "mk", [P, 4, NMEM]), sb(memory, "mv", [P, 2, 512])
                    project_memory(nc, m, d, sem)
                    project(nc, m, d, sem)
                    norm_heads(nc, m, d, sem)
                    if until == 3:
                        return m
                    attend_prompt(nc, m, sem, windowed=False)
                    attend_memory_samples(nc, m, d, sem)
                with ExitStack() as window:
                    m.bias = sb(window, "bias", [P, 2, 4, 256])
                    m.bias_s = sb(window, "bias_s", [P, 2, WK])
                    bias_by_distance(nc, m, d, sem)
                    attend_prompt(nc, m, sem, windowed=True)
                    attend_window_samples(nc, m, d, sem)
                with ExitStack() as gla:
                    g = Mem()
                    g.b, g.aq, g.kl = (sb(gla, x, [P, 2, T]) for x in ("gla_b", "gla_aq", "gla_kl"))
                    g.el = sb(gla, "gla_el", [P, 2, TP // GC + NB])
                    prepare_gla(nc, m, g, d, sem)
                    g.kt = sb(gla, "gla_kt", [P, NT, 256])
                    turn_keys(nc, m, g, sem)
                    gla_prompt(nc, m, g, d, sem)
                    gla_samples(nc, m, g, d, sem)
                    finish_gla(nc, m, g, d, sem)
            if until == 6:
                return m
            m.h = sb(mix, "merged", [P, KT, T])
            merge(nc, m, d, sem)
            project_out(nc, m, d, sem)
        clear_semaphores()
        if until == 7:
            return m
        with ExitStack() as peer:
            m.hn = (sb(peer, "hn_high", [P, KT, T], F32R), sb(peer, "hn_low", [P, KT, T], F32R))
            norm_and_split(nc, m, sem)
            with ExitStack() as chosen:
                m.e1, m.e2, m.gate = (sb(chosen, x, [P, NT, HEADS * TOPK]) for x in ("e1", "e2", "gate"))
                choose_experts(nc, m, d, sem)
                if until == 9:
                    return m
                build_gate_matrix(nc, m, d, sem)
            run_experts(nc, m, d, sem)
        store_output(nc, m, d, sem)
        signals.close()


def constants():
    import math

    import numpy as np

    c = np.zeros((P, C_END), np.float32)
    r = np.arange(P)
    c[:, C_ID:C_ID + P] = np.eye(P)
    c[:, C_BLK:C_BLK + P] = r[:, None] // 64 == r[None, :] // 64
    c[:, C_IOTA:C_IOTA + P] = r[None, :]
    c[:, C_TRI:C_TRI + GC] = r[:, None] % GC <= np.arange(GC)[None, :]
    i = np.arange(32)
    c[0:32, C_TRIS:C_TRIS + 32] = (i[:, None] // TS == i[None, :] // TS) & (i[:, None] <= i[None, :])
    own = (r[:, None] % 32) // TS == np.arange(NB)[None, :]
    c[:, C_OWN:C_OWN + NB] = np.where(own, 0.0, NEG)
    c[:, C_SEL:C_SEL + NB] = own
    dist = WIN - 1 - np.arange(WIN)
    exact = 16
    large = exact + (np.log(np.maximum(dist, 1).astype(np.float32) / np.float32(exact))
                     / np.float32(math.log(128 / exact)) * np.float32(32 - exact)).astype(np.int32)
    bucket = np.where(dist < exact, dist, np.minimum(large, 31))
    c[0:32, C_HOT:C_HOT + WIN] = np.arange(32)[:, None] == bucket[None, :]
    t = np.arange(T)
    scan = np.where(t < TP, t % GC != 0, (t - TP) % TS != 0).astype(np.float32)[None, :]
    return c, scan


def lay_out(x):
    import numpy as np

    c = np.ascontiguousarray
    a = {}
    rows = np.concatenate([x["x_prompt"][0], x["x_sample"].reshape(NB * TS, D), x["mem_prompt"][0]])
    a["x"] = c(rows.T.reshape(KT, P, TM).transpose(1, 0, 2))
    w = x["w_in"][0]
    sizes = [512, 128, 128, 256, 256, 512, 16, 512, 512, 3072]
    at = np.concatenate([[0], np.cumsum(sizes)])
    aq, ak, av, bq, bk, bv, lr, br, cq, gl = (w[:, at[i]:at[i + 1]] for i in range(10))
    pair = [0, 4, 1, 5, 2, 6, 3, 7]
    aq = aq.reshape(D, 8, 64)[:, pair].reshape(D, 512)

    def tiles(y):
        return y.reshape(y.shape[0] // P, P, y.shape[1] // P, P).transpose(2, 1, 0, 3)

    a["w_f"] = c(tiles(np.concatenate([aq, ak, bq, bk, br, cq], axis=1)))
    a["w_lr"] = c(lr.reshape(KT, P, 16).transpose(1, 0, 2))
    a["w_v"] = c(np.concatenate([av, bv], axis=1).reshape(KT, P, 640).transpose(1, 0, 2))
    mk, mv = x["w_mem_kv"][0][:, 0:512], x["w_mem_kv"][0][:, 512:1024]
    a["w_mk"] = c(tiles(mk).transpose(1, 0, 2, 3))
    a["w_mv"] = c(mv.reshape(KT, P, 512).transpose(1, 0, 2))
    wa = x["w_br_a"][0].reshape(8, 64, D)[pair].reshape(512, D)
    gates = gl.reshape(KT, P, 3, KT, P).transpose(3, 1, 2, 0, 4).reshape(KT, P, 24, P)
    br = np.stack([wa, x["w_br_b"][0], x["w_br_c"][0]])
    br = br.reshape(3, 4, P, KT, P).transpose(3, 2, 0, 1, 4).reshape(KT, P, 12, P)
    a["w_m"] = c(np.concatenate([gates, br], axis=2))
    a["w_out"] = c(tiles(x["w_out"][0]))
    a["w_q"] = c(tiles(x["peer_wq"][0]))
    a["keys"] = c(np.stack([x["peer_k1"][0].T, x["peer_k2"][0].T], axis=1))
    a["u"] = c(x["peer_u"][0].reshape(NK, NK, KT, P).transpose(1, 3, 2, 0))
    a["v"] = c(x["peer_v"][0].reshape(NK, NK, D).transpose(1, 0, 2))
    for name in ("norm1_g", "norm2_g", "mem_norm_g"):
        a[name] = c(x[name][0].reshape(KT, P).T)
    for name in ("a_qnorm_g", "a_knorm_g", "c_qnorm_g", "c_knorm_g", "b_gn_g"):
        a[name] = c(x[name][0][:, None])
    a["b_gate_b"] = c(x["b_gate_b"][0].reshape(2, P).T)
    a["b_gates"] = c(x["b_gates"][0].reshape(3, KT, P).transpose(2, 1, 0))
    a["a_sinks"] = c(x["a_sinks"])
    a["rel_bias"] = c(x["rel_bias"])
    a["b_gate_w2"] = c(x["b_gate_w2"][0])
    a["win_k"] = c(x["cache_win_k"][0].reshape(NB, WIN, P).transpose(2, 0, 1))
    a["win_v"] = c(x["cache_win_v"][0].reshape(NB, WIN, P))
    a["mem_k"] = c(x["cache_mem_k"][0].transpose(2, 3, 0, 1).reshape(4, P, NB * NMEM))
    a["mem_v"] = c(x["cache_mem_v"][0].reshape(NB, NMEM, 512))
    a["state"] = c(x["state_gla"][0])
    a["const"], a["scan"] = constants()
    return a


OUTS = {
    "out_y": (P, KT, T), "out_wk": (P, WIN), "out_wv": (WIN, P), "out_sp": (P, 2, P), "out_mk": (P, 4, NMEM),
    "out_mv": (NMEM, 512), "out_wks": (P, NB, WIN), "out_wvs": (NB, WIN, P), "out_ss": (NB, 4, 64, P),
}
SCRATCH = {"skew": (8, P, EXT), "gates": (T // TBG, NK, NK, TBG)}


def declare(nc, arrays):
    t = {name: nc.dram_tensor(f"in_{name}", x.shape, F32, kind="ExternalInput").ap() for name, x in arrays.items()}
    t.update({name: nc.dram_tensor(name, shape, F32, kind="ExternalOutput").ap() for name, shape in OUTS.items()})
    t.update({name: nc.dram_tensor(name, shape, F32).ap() for name, shape in SCRATCH.items()})
    return t


def kernel(**inputs):
    import numpy as np

    import concourse.bacc as bacc
    from concourse.bass_utils import run_bass_kernel_spmd

    arrays = lay_out({k: np.asarray(v) for k, v in inputs.items()})
    nc = bacc.Bacc("TRN2", target_bir_lowering=False, num_devices=1)
    build(nc, declare(nc, arrays))
    r = run_bass_kernel_spmd(nc, [{f"in_{k}": v for k, v in arrays.items()}], core_ids=[0]).results[0]
    y = np.asarray(r["out_y"]).transpose(2, 1, 0).reshape(T, D)
    kv = (2, 64)
    return (
        np.ascontiguousarray(y[0:TP])[None],
        np.ascontiguousarray(y[TP:T]).reshape(NB, TS, D),
        np.ascontiguousarray(r["out_wk"].T).reshape(1, 1, WIN, *kv),
        r["out_wv"].reshape(1, 1, WIN, *kv),
        np.ascontiguousarray(r["out_sp"].reshape(2, 64, 2, P).transpose(2, 0, 1, 3)).reshape(1, 1, 4, 64, P),
        np.ascontiguousarray(r["out_mk"].transpose(2, 1, 0)).reshape(1, 1, NMEM, 4, P),
        r["out_mv"].reshape(1, 1, NMEM, 4, P),
        np.ascontiguousarray(r["out_wks"].transpose(1, 2, 0)).reshape(1, NB, WIN, *kv),
        r["out_wvs"].reshape(1, NB, WIN, *kv),
        r["out_ss"][None],
    )
```

```python
from contextlib import ExitStack

import concourse.bass as bass
from concourse import mybir

F32 = mybir.dt.float32
F32R = mybir.dt.float32r
BF16 = mybir.dt.bfloat16
U32 = mybir.dt.uint32
ALU = mybir.AluOpType
ACT = mybir.ActivationFunctionType
AX = mybir.AxisListType.X

P = 128
D = 1024
KT = D // P
TP, NB, TS = 1024, 8, 4
T = TP + NB * TS
NMEM = 256
TM = T + NMEM
CH = T // 3
CHUNKS = [(c * CH, (c + 1) * CH) for c in range(3)]
BLK = TP // P
EPS = 1e-6
NEG = -1e30
QA, KA, QB, KB, RB, QC, NF = 0, 4, 5, 7, 9, 13, 17
WIN = 128
WK = WIN + TS
EXT = 384
GC = 64
HEADS, TOPK, NK = 8, 16, 128
HTILES, HROWS = 13, 18
NT = BLK + 1
G8 = 8
KEPT = 24
GR = 2
TBG = 48

C_ID, C_BLK, C_IOTA, C_TRI, C_TRIS, C_OWN, C_SEL, C_HOT, C_END = 0, 128, 256, 384, 448, 480, 488, 496, 624


class Chain:

    def __init__(self, eng, sem, count=0):
        self.eng, self.sem, self.n = eng, sem, count

    def __call__(self, ins):
        ins.then_inc(self.sem, 1)
        self.n += 1
        self.eng.wait_ge(self.sem, self.n)


class Mem:
    pass


def tile_rows(t):
    return P if t < BLK else T - TP


def exact_product(pe, out, w, x, first, last):
    pe.matmul(out, w[0], x[0], start=first, stop=False)
    pe.matmul(out, w[0], x[1], start=False, stop=False)
    return pe.matmul(out, w[1], x[0], start=False, stop=last)


def load_small(nc, m, d, sem):
    loaded = sem("small_loaded")
    with nc.Block() as block:

        @block.sync
        def _(sp):
            n = 0

            def load(dst, src):
                nonlocal n
                sp.dma_start(dst, src).then_inc(loaded, 16)
                n += 16

            load(m.const[:], d["const"])
            load(m.norm1[:], d["norm1_g"])
            load(m.norm2[:], d["norm2_g"])
            load(m.memg[:], d["mem_norm_g"])
            for half in range(2):
                load(m.qg[64 * half:64 * half + 64, :], d["a_qnorm_g"])
                load(m.kg[64 * half:64 * half + 64, :], d["a_knorm_g"])
            load(m.cqg[:], d["c_qnorm_g"])
            load(m.ckg[:], d["c_knorm_g"])
            load(m.gng[:], d["b_gn_g"])
            load(m.gbias[:], d["b_gate_b"])
            load(m.gates_b[:], d["b_gates"])
            load(m.sink[:], d["a_sinks"].broadcast_to([P, 8]))
            for kv in range(2):
                src = bass.AP(tensor=d["a_sinks"].tensor, offset=4 * kv, ap=[[1, 4], [0, 32], [1, 1]])
                load(m.sink_s[:, kv:kv + 1], src)
            load(m.relb[:], d["rel_bias"])
            load(m.w2[:], d["b_gate_w2"])
            sp.wait_ge(loaded, n)

        @block.vector
        def _(dve):
            dve.memset(m.ones[:], 1.0)
            dve.memset(m.eps[:], EPS)
            dve.memset(m.one[:], 1.0)


def bias_by_distance(nc, m, d, sem):
    with ExitStack() as ctx:
        ext = ctx.enter_context(nc.sbuf_tensor("ext", [8, EXT], F32))
        cleared, picked, ready, out, back = (sem(f"bias_{x}") for x in ("cleared", "picked", "ready", "out", "back"))
        with nc.Block() as block:

            @block.tensor
            def _(pe):
                pe.matmul(m.ps[0:8, 0, 0:WIN], m.relb[:], m.const[0:32, C_HOT:C_HOT + WIN],
                          start=True, stop=True).then_inc(picked, 1)

            @block.vector
            def _(dve):
                dve.memset(ext[:], NEG).then_inc(cleared, 1)
                dve.wait_ge(cleared, 1)
                dve.wait_ge(picked, 1)
                dve.tensor_copy(ext[:, P:P + WIN], m.ps[0:8, 0, 0:WIN]).then_inc(ready, 1)

            @block.sync
            def _(sp):
                sp.wait_ge(ready, 1)
                sp.dma_start(d["skew"], ext[:].unsqueeze(1).broadcast_to([8, P, EXT])).then_inc(out, 16)
                sp.wait_ge(out, 16)
                for h in range(8):
                    src = bass.AP(tensor=d["skew"].tensor, offset=h * P * EXT + P - 1, ap=[[EXT - 1, P], [1, 2 * P]])
                    sp.dma_start(m.bias[:, h // 4, h % 4, :], src).then_inc(back, 16)
                    src = bass.AP(tensor=d["skew"].tensor, offset=h * P * EXT + P - 1,
                                  ap=[[0, NB], [EXT - 1, TS], [1, WK]])
                    g = h % 4
                    sp.dma_start(m.bias_s[32 * g:32 * g + 32, h // 4, :], src).then_inc(back, 16)
                sp.wait_ge(back, 16 * 16)


def norm_features(nc, m, d, sem):
    spare = m.f[:].rearrange("p n t -> p (n t)")
    m.w_memory = (spare[:, 0:4 * D].rearrange("p (h k e) -> p h k e", h=4, k=KT),
                  spare[:, 4 * D:8 * D].rearrange("p (k e) -> p k e", k=KT))
    m.w_memory_loaded = sem("mkv_k_loaded"), sem("mkv_v_loaded")
    spans = [(a, min(a + CH, TM)) for a in range(0, TM, CH)]
    x = m.xn
    with ExitStack() as ctx:
        sq = ctx.enter_context(nc.sbuf_tensor("n1_sq", [P, 2, TM], F32))
        root = ctx.enter_context(nc.sbuf_tensor("n1_root", [P, TM], F32))
        x_loaded = [sem(f"n1_loaded{k}") for k in range(KT)]
        squared, summed, rooted, inv, scaled, high = (
            sem(f"n1_{x}") for x in ("squared", "summed", "rooted", "inverted", "scaled", "high"))

        def split_tile(eng, k):
            eng.wait_ge(scaled, k + 1)
            eng.wait_ge(high, k + 1)
            eng.tensor_tensor(m.x_low[:, k, :], x[:, k, 0:T], m.x_high[:, k, :].bitcast(F32), ALU.subtract)

        with nc.Block() as block:

            @block.sync
            def _(sp):
                for k in range(KT):
                    sp.dma_start(x[:, k, :], d["x"][:, k, :]).then_inc(x_loaded[k], 16)
                for w, name, loaded in zip(m.w_memory, ("w_mk", "w_mv"), m.w_memory_loaded):
                    sp.dma_start(w, d[name]).then_inc(loaded, 16)

            @block.scalar
            def _(act):
                for k in range(KT):
                    act.wait_ge(x_loaded[k], 16)
                    if k >= 2:
                        act.wait_ge(summed, k - 1)
                    act.activation(sq[:, k % 2, :], x[:, k, :], ACT.Square).then_inc(squared, 1)
                act.wait_ge(summed, KT)
                for b, (a, z) in enumerate(spans):
                    act.activation(root[:, a:z], m.ps[:, b, 0:z - a], ACT.Sqrt, bias=m.eps[:, 0:1],
                                   scale=1.0 / D).then_inc(rooted, 1)
                for k in range(KT):
                    act.wait_ge(scaled, k + 1)
                    act.copy(m.x_high[:, k, :], x[:, k, 0:T]).then_inc(high, 1)

            @block.tensor
            def _(pe):
                for k in range(KT):
                    pe.wait_ge(squared, k + 1)
                    for b, (a, z) in enumerate(spans):
                        mm = pe.matmul(m.ps[:, b, 0:z - a], m.ones[:], sq[:, k % 2, a:z],
                                       start=(k == 0), stop=(k == KT - 1))
                    mm.then_inc(summed, 1)

            @block.vector
            def _(dve):
                for b, (a, z) in enumerate(spans):
                    dve.wait_ge(rooted, b + 1)
                    dve.reciprocal(root[:, a:z], root[:, a:z]).then_inc(inv, 1)
                dve.wait_ge(inv, len(spans))
                for k in range(KT):
                    dve.scalar_tensor_tensor(x[:, k, T:TM], x[:, k, T:TM], m.memg[:, k:k + 1], root[:, T:TM],
                                             ALU.mult, ALU.mult)
                    dve.scalar_tensor_tensor(x[:, k, 0:T], x[:, k, 0:T], m.norm1[:, k:k + 1], root[:, 0:T],
                                             ALU.mult, ALU.mult).then_inc(scaled, 1)
                    if k % 2:
                        split_tile(dve, k - 1)

            @block.gpsimd
            def _(pool):
                for k in range(1, KT, 2):
                    split_tile(pool, k)


def norm_and_split(nc, m, sem):
    spans = [(a, min(a + CH, T)) for a in range(0, T, CH)]
    with ExitStack() as ctx:
        sq = ctx.enter_context(nc.sbuf_tensor("n2_sq", [P, 2, T], F32))
        full = ctx.enter_context(nc.sbuf_tensor("n2_full", [P, KT, T], F32))
        root = ctx.enter_context(nc.sbuf_tensor("n2_root", [P, T], F32))
        squared, summed, rooted, inv, scaled, high = (
            sem(f"n2_{x}") for x in ("squared", "summed", "rooted", "inverted", "scaled", "high"))

        def split_tile(eng, k):
            eng.wait_ge(high, k + 1)
            eng.tensor_tensor(m.hn[1][:, k, :], full[:, k, :], m.hn[0][:, k, :].bitcast(F32), ALU.subtract)

        with nc.Block() as block:

            @block.scalar
            def _(act):
                for k in range(KT):
                    if k >= 2:
                        act.wait_ge(summed, k - 1)
                    act.activation(sq[:, k % 2, :], m.x2[:, k, :], ACT.Square).then_inc(squared, 1)
                act.wait_ge(summed, KT)
                for b, (a, z) in enumerate(spans):
                    act.activation(root[:, a:z], m.ps[:, b, 0:z - a], ACT.Sqrt, bias=m.eps[:, 0:1],
                                   scale=1.0 / D).then_inc(rooted, 1)
                for k in range(KT):
                    act.wait_ge(scaled, k + 1)
                    act.copy(m.hn[0][:, k, :], full[:, k, :]).then_inc(high, 1)

            @block.tensor
            def _(pe):
                for k in range(KT):
                    pe.wait_ge(squared, k + 1)
                    for b, (a, z) in enumerate(spans):
                        mm = pe.matmul(m.ps[:, b, 0:z - a], m.ones[:], sq[:, k % 2, a:z],
                                       start=(k == 0), stop=(k == KT - 1))
                    mm.then_inc(summed, 1)

            @block.vector
            def _(dve):
                for b, (a, z) in enumerate(spans):
                    dve.wait_ge(rooted, b + 1)
                    dve.reciprocal(root[:, a:z], root[:, a:z]).then_inc(inv, 1)
                dve.wait_ge(inv, len(spans))
                for k in range(KT):
                    dve.scalar_tensor_tensor(full[:, k, :], m.x2[:, k, :], m.norm2[:, k:k + 1], root[:],
                                             ALU.mult, ALU.mult).then_inc(scaled, 1)
                    if k % 2:
                        split_tile(dve, k - 1)

            @block.gpsimd
            def _(pool):
                for k in range(1, KT, 2):
                    split_tile(pool, k)


def project_memory(nc, m, d, sem):
    wk, wv = m.w_memory
    k_loaded, v_loaded = m.w_memory_loaded
    done, kept = sem("mkv_done"), sem("mkv_kept")
    with nc.Block() as block:

        @block.tensor
        def _(pe):
            pe.wait_ge(k_loaded, 16)
            for h in range(4):
                for k in range(KT):
                    mm = pe.matmul(m.ps[:, h, 0:NMEM], wk[:, h, k, :], m.xn[:, k, T:TM], start=(k == 0),
                                   stop=(k == KT - 1))
                mm.then_inc(done, 1)
            pe.wait_ge(v_loaded, 16)
            for c in range(2):
                for k in range(KT):
                    mm = pe.matmul(m.ps[:, 4 + c, :], m.xn[:, k, T + c * P:T + c * P + P], wv[:, k, :],
                                   start=(k == 0), stop=(k == KT - 1))
                mm.then_inc(done, 1)

        @block.scalar
        def _(act):
            for h in range(4):
                act.wait_ge(done, h + 1)
                act.copy(m.mk[:, h, :], m.ps[:, h, 0:NMEM])
            for c in range(2):
                act.wait_ge(done, 5 + c)
                act.copy(m.mv[:, c, :], m.ps[:, 4 + c, :]).then_inc(kept, 1)
            act.wait_ge(kept, 2)
            act.dma_start(d["out_mv"].rearrange("(c n) e -> n c e", c=2), m.mv[:]).then_inc(m.stored, 16)


def project(nc, m, d, sem):
    wb = m.wb_spare
    pieces = [("f", 0), ("f", 1), ("b", 0), ("b", 1), ("f", 2), ("b", 2), ("b", 3), ("a", 0)]
    pieces += [("f", n) for n in range(3, NF + 1)]
    ring = [x for x in pieces if x[0] != "b"]
    units_to = [0]
    for kind, _ in ring:
        units_to.append(units_to[-1] + (3 if kind == "f" else 2 * NT))
    with ExitStack() as ctx:
        raw = ctx.enter_context(nc.sbuf_tensor("w_raw", [P, KT, P], F32))
        w = [ctx.enter_context(nc.sbuf_tensor(f"w_{x}", [P, 2, KT, P], F32R)) for x in ("high", "low")]
        loaded, high, low, done, kept = (sem(f"proj_{x}") for x in ("loaded", "high", "low", "done", "kept"))

        def source(i):
            kind, n = pieces[i]
            if kind == "f":
                return d["w_f"][n] if n < NF else d["w_lr"]
            return d["w_bv"][n] if kind == "b" else d["w_av"]

        def place(part, i):
            kind, n = pieces[i]
            if kind == "b":
                return wb[part][:, 2 * n:2 * n + 2, :].rearrange("p k (h e) -> p (k h) e", h=4)
            return w[part][:, ring.index(pieces[i]) % 2]

        with nc.Block() as block:

            @block.sync
            def _(sp):
                for i in range(len(pieces)):
                    if i:
                        sp.wait_ge(low, i)
                    sp.dma_start(raw[:], source(i)).then_inc(loaded, 16)
                sp.dma_start(d["out_wvs"][:, 0:WIN - TS, :], d["win_v"][:, TS:WIN, :]).then_inc(m.stored, 16)

            @block.tensor
            def _(pe):
                unit = 0

                def product(width, lhs, rhs):
                    nonlocal unit
                    if unit >= 8:
                        pe.wait_ge(kept, unit - 7)
                    for k in range(KT):
                        mm = exact_product(pe, m.ps[:, unit % 8, 0:width], lhs(k), rhs(k), k == 0, k == KT - 1)
                    mm.then_inc(done, 1)
                    unit += 1

                for r, (kind, n) in enumerate(ring):
                    pe.wait_ge(low, pieces.index((kind, n)) + 1)
                    if kind == "f":
                        for a, z in CHUNKS:
                            product(CH, lambda k: [y[:, r % 2, k, :] for y in w],
                                    lambda k: (m.x_high[:, k, a:z], m.x_low[:, k, a:z]))
                        continue
                    for t in range(NT):
                        a = min(t * P, T - P)
                        product(P, lambda k: (m.x_high[:, k, a:a + P], m.x_low[:, k, a:a + P]),
                                lambda k: [y[:, r % 2, k, :] for y in w])
                        product(512, lambda k: (m.x_high[:, k, a:a + P], m.x_low[:, k, a:a + P]),
                                lambda k: [y[:, k, :] for y in wb])

            @block.vector
            def _(dve):
                for i in range(len(pieces)):
                    dve.wait_ge(high, i + 1)
                    dve.tensor_tensor(place(1, i), raw[:], place(0, i).bitcast(F32), ALU.subtract).then_inc(low, 1)

            @block.scalar
            def _(act):
                unit = 0

                def round_piece(i):
                    act.wait_ge(loaded, 16 * (i + 1))
                    if pieces[i][0] != "b":
                        r = ring.index(pieces[i])
                        if r >= 2:
                            act.wait_ge(done, units_to[r - 1])
                    act.copy(place(0, i), raw[:]).then_inc(high, 1)

                def keep(dst, first, rows, width):
                    nonlocal unit
                    act.wait_ge(done, unit + 1)
                    act.copy(dst, m.ps[first:first + rows, unit % 8, 0:width]).then_inc(kept, 1)
                    unit += 1

                ahead = 0
                for r, (kind, n) in enumerate(ring):
                    upto = pieces.index(ring[r + 1]) + 1 if r + 1 < len(ring) else len(pieces)
                    while ahead < upto:
                        round_piece(ahead)
                        ahead += 1
                    if kind == "a":
                        for t in range(NT):
                            rows = tile_rows(t)
                            keep(m.av[0:rows, t, :], P - rows, rows, P)
                            keep(m.bv[0:rows, t, :], P - rows, rows, 512)
                        continue
                    for a, z in CHUNKS:
                        if n < NF:
                            keep(m.f[:, n, a:z], 0, P, CH)
                        else:
                            keep(m.lr[:, a:z], 0, 16, CH)
                act.wait_ge(kept, unit)
                act.dma_start(d["out_wv"], m.av[:, BLK - 1, :]).then_inc(m.stored, 16)
                for b in range(NB):
                    act.dma_start(d["out_wvs"][b, WIN - TS:WIN, :], m.av[TS * b:TS * b + TS, BLK, :]).then_inc(m.stored, 16)


def norm_heads(nc, m, d, sem):
    tiles = [(m.f[:, QA + t], m.qg) for t in range(4)] + [(m.f[:, KA], m.kg)] + [(m.f[:, QC + t], m.cqg) for t in range(4)]
    parts = [[(x[:, a:z], gain, s) for s, (x, gain) in enumerate(tiles)] for a, z in CHUNKS]
    parts.append([(m.mk[:, h, :], m.ckg, len(tiles) + h) for h in range(4)])
    widths = [CH, CH, CH, NMEM]
    first = [0, 9, 18, 27]
    with ExitStack() as ctx:
        sq = ctx.enter_context(nc.sbuf_tensor("heads_sq", [P, 4, CH], F32))
        rt = ctx.enter_context(nc.sbuf_tensor("heads_rt", [HROWS, 4, CH], F32))
        gather = ctx.enter_context(nc.sbuf_tensor("heads_gather", [P, HTILES, HROWS], F32))
        spread = ctx.enter_context(nc.sbuf_tensor("heads_spread", [HROWS, HTILES, P], F32))
        picks_loaded, squared, summed, rooted, inverted, spread_out, scaled = (
            sem(f"heads_{x}") for x in
            ("picks_loaded", "squared", "summed", "rooted", "inverted", "spread_out", "scaled"))
        with nc.Block() as block:

            @block.sync
            def _(sp):
                sp.dma_start(gather[:], d["gather"]).then_inc(picks_loaded, 16)
                sp.dma_start(spread[:], d["spread"]).then_inc(picks_loaded, 16)

            @block.scalar
            def _(act):
                u = 0
                for c, part in enumerate(parts):
                    w = widths[c]
                    for x, _, _ in part:
                        if u >= 4:
                            act.wait_ge(summed, u - 3)
                        act.activation(sq[:, u % 4, 0:w], x, ACT.Square).then_inc(squared, 1)
                        u += 1
                    act.wait_ge(summed, u)
                    act.activation(rt[:, c, 0:w], m.ps[0:HROWS, c, 0:w], ACT.Sqrt, bias=m.eps[0:HROWS, 0:1]).then_inc(rooted, 1)

            @block.tensor
            def _(pe):
                def sums(c):
                    part, w = parts[c], widths[c]
                    for n, (_, _, s) in enumerate(part):
                        u = first[c] + n
                        pe.wait_ge(squared, u + 1)
                        pe.matmul(m.ps[0:HROWS, c, 0:w], gather[:, s, :], sq[:, u % 4, 0:w], start=(n == 0),
                                  stop=(n == len(part) - 1)).then_inc(summed, 1)

                def spreads(c):
                    pe.wait_ge(inverted, c + 1)
                    for n, (_, _, s) in enumerate(parts[c]):
                        u = first[c] + n
                        if u >= 4:
                            pe.wait_ge(scaled, u - 3)
                        pe.matmul(m.ps[:, 4 + u % 4, 0:widths[c]], spread[:, s, :], rt[:, c, 0:widths[c]], start=True,
                                  stop=True).then_inc(spread_out, 1)

                pe.wait_ge(picks_loaded, 32)
                sums(0)
                for c in range(4):
                    if c + 1 < 4:
                        sums(c + 1)
                    spreads(c)

            @block.vector
            def _(dve):
                def invert(c):
                    dve.wait_ge(rooted, c + 1)
                    dve.reciprocal(rt[:, c, 0:widths[c]], rt[:, c, 0:widths[c]]).then_inc(inverted, 1)

                invert(0)
                for c, part in enumerate(parts):
                    if c + 1 < 4:
                        invert(c + 1)
                    for n, (x, gain, _) in enumerate(part):
                        u = first[c] + n
                        dve.wait_ge(spread_out, u + 1)
                        dve.scalar_tensor_tensor(x, x, gain[:, 0:1], m.ps[:, 4 + u % 4, 0:widths[c]], ALU.mult,
                                                 ALU.mult).then_inc(scaled, 1)

            @block.gpsimd
            def _(pool):
                for k in range(KT):
                    pool.tensor_tensor(m.x2[:, k, :], m.x_high[:, k, :].bitcast(F32), m.x_low[:, k, :].bitcast(F32), ALU.add)

        with nc.Block() as block:

            @block.sync
            def _(sp):
                sp.dma_start(d["out_wk"], m.f[:, KA, TP - WIN:TP]).then_inc(m.stored, 16)
                sp.dma_start(d["out_mk"], m.mk[:]).then_inc(m.stored, 16)


def norm_units(nc, m, sem, tag, units):
    with ExitStack() as ctx:
        sq = ctx.enter_context(nc.sbuf_tensor(f"{tag}_sq", [P, 4, CH], F32))
        rt = ctx.enter_context(nc.sbuf_tensor(f"{tag}_rt", [P, 4, CH], F32))
        squared, summed, rooted, inverted, scaled = (
            sem(f"{tag}_{x}") for x in ("squared", "summed", "rooted", "inverted", "scaled"))
        with nc.Block() as block:

            @block.scalar
            def _(act):
                for u in range(len(units) + 2):
                    if u < len(units):
                        x = units[u][0]
                        if u >= 4:
                            act.wait_ge(summed, u - 3)
                        act.activation(sq[:, u % 4, 0:x.shape[1]], x, ACT.Square).then_inc(squared, 1)
                    v = u - 2
                    if v >= 0:
                        w = units[v][0].shape[1]
                        act.wait_ge(summed, v + 1)
                        if v >= 4:
                            act.wait_ge(scaled, v - 3)
                        act.activation(rt[:, v % 4, 0:w], m.ps[:, v % 8, 0:w], ACT.Sqrt, bias=m.eps[:, 0:1],
                                       scale=1.0 / units[v][2]).then_inc(rooted, 1)

            @block.tensor
            def _(pe):
                for u, (x, ones, _, _) in enumerate(units):
                    w = x.shape[1]
                    pe.wait_ge(squared, u + 1)
                    if u >= 8:
                        pe.wait_ge(rooted, u - 7)
                    pe.matmul(m.ps[:, u % 8, 0:w], ones, sq[:, u % 4, 0:w], start=True, stop=True).then_inc(summed, 1)

            @block.vector
            def _(dve):
                for u, (x, _, _, gain) in enumerate(units):
                    w = x.shape[1]
                    dve.wait_ge(rooted, u + 1)
                    dve.reciprocal(rt[:, u % 4, 0:w], rt[:, u % 4, 0:w]).then_inc(inverted, 1)
                    dve.wait_ge(inverted, u + 1)
                    dve.scalar_tensor_tensor(x, x, gain[:, 0:1], rt[:, u % 4, 0:w], ALU.mult,
                                             ALU.mult).then_inc(scaled, 1)


def attend_prompt(nc, m, sem, windowed):
    tag = "win" if windowed else "mem"
    units = [(n, kv) for n in range(BLK) for kv in range(2)] if windowed else [(n, 0) for n in range(BLK)]
    scale = 64 ** -0.5 if windowed else P ** -0.5
    ident = m.const[:, C_ID:C_ID + P]
    with ExitStack() as ctx:
        s = ctx.enter_context(nc.sbuf_tensor(f"{tag}_s", [P, 2, 4, 256], F32))
        pt = ctx.enter_context(nc.sbuf_tensor(f"{tag}_pt", [P, 2, 8, P], F32))
        st = ctx.enter_context(nc.sbuf_tensor(f"{tag}_stats", [P, 2, 6, 4], F32))
        scored, based, chained, maxed, expd, normed, turned, pt_kept, summed, kept = (
            sem(f"{tag}_{x}") for x in
            ("scored", "based", "chained", "maxed", "expd", "normed", "turned", "pt_kept", "summed", "kept"))
        MAXI, NMAX, SUM, SINK, INV = range(5)

        def lo(n):
            return P if windowed and n == 0 else 0

        with nc.Block() as block:

            @block.tensor
            def _(pe):
                def scores(u):
                    n, kv = units[u]
                    if u >= 2:
                        pe.wait_ge(based if windowed else expd, u - 1)
                    for j in range(4):
                        out = m.ps[:, 2 * (u % 2) + j // 2, (j % 2) * 256 + lo(n):(j % 2) * 256 + 256]
                        if windowed:
                            rows = slice(64 * kv, 64 * kv + 64)
                            q = m.f[rows, QA + j, n * P:n * P + P]
                            k = m.f[rows, KA, n * P - P + lo(n):n * P + P]
                        else:
                            q, k = m.f[:, QC + j, n * P:n * P + P], m.mk[:, j, :]
                        mm = pe.matmul(out, q, k, start=True, stop=True)
                    mm.then_inc(scored, 1)

                scores(0)
                for u in range(len(units) + 2):
                    if u + 1 < len(units):
                        scores(u + 1)
                    if u >= 2:
                        v = u - 2
                        n, kv = units[v]
                        pe.wait_ge(pt_kept, v + 1)
                        if v >= 2:
                            pe.wait_ge(kept, v - 1)
                        for j in range(4):
                            cs = range(lo(n) // P, 2)
                            for c in cs:
                                if windowed:
                                    out = m.ps[64 * kv:64 * kv + 64, 6 + v % 2, j * P:j * P + P]
                                    val = m.av[:, n - 1 + c, 64 * kv:64 * kv + 64]
                                else:
                                    out = m.ps[:, 6 + v % 2, j * P:j * P + P]
                                    val = m.mv[:, c, j * P:j * P + P]
                                mm = pe.matmul(out, val, pt[:, v % 2, 2 * j + c, :], start=(c == cs[0]), stop=(c == 1))
                        mm.then_inc(summed, 1)
                    if 1 <= u <= len(units):
                        v = u - 1
                        n, kv = units[v]
                        pe.wait_ge(normed, v + 1)
                        if v >= 1:
                            pe.wait_ge(pt_kept, v)
                        for j in range(4):
                            for c in range(lo(n) // P, 2):
                                i = 2 * j + c
                                mm = pe.transpose(m.ps[:, 4 + i // 4, (i % 4) * P:(i % 4) * P + P],
                                                  s[:, v % 2, j, c * P:c * P + P], ident)
                        mm.then_inc(turned, 1)

            @block.vector
            def _(dve):
                chain = Chain(dve, chained)
                for u in range(len(units) + 1):
                    if u < len(units):
                        n, kv = units[u]
                        a = lo(n)
                        x, z = s[:, u % 2, :, a:256], st[:, u % 2]
                        raw = m.ps[:, 2 * (u % 2):2 * (u % 2) + 2, :].rearrange("p b (j k) -> p (b j) k", j=2)[:, :, a:256]
                        dve.wait_ge(scored, u + 1)
                        if u >= 2:
                            dve.wait_ge(turned, u - 1)
                        if windowed:
                            dve.scalar_tensor_tensor(x, raw, scale, m.bias[:, kv, :, a:256], ALU.mult,
                                                     ALU.add).then_inc(based, 1)
                            dve.wait_ge(based, u + 1)
                            chain(dve.tensor_reduce(z[:, MAXI, :], x, AX, ALU.max))
                            sink = m.sink[:, 4 * kv:4 * kv + 4]
                            chain(dve.tensor_tensor(z[:, MAXI, :], z[:, MAXI, :], sink, ALU.max))
                            chain(dve.tensor_scalar(z[:, NMAX, :], z[:, MAXI, :], -1.0, None, ALU.mult))
                            dve.tensor_tensor(z[:, SINK, :], sink, z[:, NMAX, :], ALU.add).then_inc(maxed, 1)
                        else:
                            chain(dve.tensor_reduce(z[:, MAXI, :], raw, AX, ALU.max))
                            dve.tensor_scalar(z[:, NMAX, :], z[:, MAXI, :], -scale, None, ALU.mult).then_inc(maxed, 1)
                    if u >= 1:
                        v = u - 1
                        a = lo(units[v][0])
                        x, z = s[:, v % 2, :, a:256], st[:, v % 2]
                        dve.wait_ge(expd, v + 1)
                        if windowed:
                            chain(dve.tensor_tensor(z[:, SUM, :], z[:, SUM, :], z[:, SINK, :], ALU.add))
                        chain(dve.reciprocal(z[:, INV, :], z[:, SUM, :]))
                        dve.tensor_tensor(x, x, z[:, INV, :].unsqueeze(2).broadcast_to([P, 4, 256 - a]),
                                          ALU.mult).then_inc(normed, 1)

            @block.scalar
            def _(act):
                for u in range(len(units) + 2):
                    if u < len(units):
                        n, kv = units[u]
                        a = lo(n)
                        z = st[:, u % 2]
                        act.wait_ge(maxed, u + 1)
                        for j in range(4):
                            x = s[:, u % 2, j, a:256]
                            raw = x if windowed else m.ps[:, 2 * (u % 2) + j // 2, (j % 2) * 256:(j % 2) * 256 + 256]
                            ins = act.activation(x, raw, ACT.Exp, bias=z[:, NMAX, j:j + 1],
                                                 scale=1.0 if windowed else scale, accum_out=z[:, SUM, j:j + 1])
                        if windowed:
                            ins = act.activation(z[:, SINK, :], z[:, SINK, :], ACT.Exp)
                        ins.then_inc(expd, 1)
                    if u >= 2:
                        v = u - 2
                        n, kv = units[v]
                        act.wait_ge(summed, v + 1)
                        rows = slice(64 * kv, 64 * kv + 64) if windowed else slice(0, P)
                        q0 = QA if windowed else QC
                        act.copy(m.f[rows, q0:q0 + 4, n * P:n * P + P],
                                 m.ps[rows, 6 + v % 2, :].rearrange("p (j q) -> p j q", j=4)).then_inc(kept, 1)
                    if 1 <= u <= len(units):
                        v = u - 1
                        n, kv = units[v]
                        act.wait_ge(turned, v + 1)
                        if v >= 2:
                            act.wait_ge(summed, v - 1)
                        for b in range(2):
                            bank = m.ps[:, 4 + b, :].rearrange("p (j c q) -> p j c q", j=2, c=2)
                            dst = pt[:, v % 2, 4 * b:4 * b + 4, :].rearrange("p (j c) q -> p j c q", c=2)
                            c = lo(n) // P
                            ins = act.copy(dst[:, :, c:2, :], bank[:, :, c:2, :])
                        ins.then_inc(pt_kept, 1)


def attend_memory_samples(nc, m, d, sem):
    scale = P ** -0.5
    with ExitStack() as ctx:
        kc = ctx.enter_context(nc.sbuf_tensor("sm_k", [P, 2, NB * NMEM], F32))
        vc = ctx.enter_context(nc.sbuf_tensor("sm_v", [P, 2 * NB, 512], F32))
        s = ctx.enter_context(nc.sbuf_tensor("sm_s", [P, NB, NMEM], F32))
        pt = kc[:, 0, :].rearrange("p (b r) -> p b r", r=P)
        st = ctx.enter_context(nc.sbuf_tensor("sm_stats", [P, 4], F32))
        k_loaded = [sem(f"sm_k_loaded{h}") for h in range(4)]
        v_loaded, scored, chained, maxed, expd, normed, turned, pt_kept, summed = (
            sem(f"sm_{x}") for x in
            ("v_loaded", "scored", "chained", "maxed", "expd", "normed", "turned", "pt_kept", "summed"))
        with nc.Block() as block:

            @block.sync
            def _(sp):
                for h in range(4):
                    if h >= 2:
                        sp.wait_ge(scored, h - 1)
                    sp.dma_start(kc[:, h % 2, :], d["mem_k"][h]).then_inc(k_loaded[h], 16)
                for b in range(NB):
                    sp.dma_start(vc[:, 2 * b:2 * b + 2, :], d["mem_v"][b].rearrange("(c n) e -> n c e", c=2)
                                 ).then_inc(v_loaded, 16)
                sp.wait_ge(m.stored, m.stores - 32)

            @block.tensor
            def _(pe):
                for h in range(4):
                    pe.wait_ge(k_loaded[h], 16)
                    for b in range(4):
                        mm = pe.matmul(m.ps[32 * h:32 * h + 32, b, :], m.f[:, QC + h, TP:T],
                                       kc[:, h % 2, b * 512:b * 512 + 512], start=True, stop=True)
                    mm.then_inc(scored, 1)
                pe.wait_ge(normed, 1)
                x = s[:].rearrange("p b k -> p (b k)")
                for i in range(16):
                    mm = pe.transpose(m.ps[:, 4 + i // 4, (i % 4) * P:(i % 4) * P + P], x[:, i * P:i * P + P],
                                      m.const[:, C_ID:C_ID + P])
                mm.then_inc(turned, 1)
                pe.wait_ge(pt_kept, 1)
                pe.wait_ge(v_loaded, 16 * NB)
                for h in range(4):
                    for b in range(NB):
                        for c in range(2):
                            col = 32 * h + TS * b
                            mm = pe.matmul(m.ps[:, 0, col:col + TS], vc[:, 2 * b + c, h * P:h * P + P],
                                           pt[:, 2 * b + c, col:col + TS], start=(c == 0), stop=(c == 1))
                mm.then_inc(summed, 1)

            @block.vector
            def _(dve):
                chain = Chain(dve, chained)
                dve.wait_ge(scored, 4)
                own = m.const[:, C_OWN:C_OWN + NB].unsqueeze(2).broadcast_to([P, NB, NMEM])
                for b in range(4):
                    ins = dve.scalar_tensor_tensor(s[:, 2 * b:2 * b + 2, :],
                                                   m.ps[:, b, :].rearrange("p (a k) -> p a k", a=2), 1.0,
                                                   own[:, 2 * b:2 * b + 2, :], ALU.mult, ALU.add)
                chain(ins)
                chain(dve.tensor_reduce(st[:, 0:1], s[:].rearrange("p b k -> p (b k)"), AX, ALU.max))
                dve.tensor_scalar(st[:, 1:2], st[:, 0:1], -scale, None, ALU.mult).then_inc(maxed, 1)
                dve.wait_ge(expd, 1)
                chain(dve.reciprocal(st[:, 3:4], st[:, 2:3]))
                dve.tensor_scalar(s[:], s[:], st[:, 3:4], None, ALU.mult).then_inc(normed, 1)

            @block.scalar
            def _(act):
                act.wait_ge(maxed, 1)
                act.activation(s[:], s[:], ACT.Exp, bias=st[:, 1:2], scale=scale, accum_out=st[:, 2:3]).then_inc(expd, 1)
                act.wait_ge(turned, 1)
                act.copy(pt, m.ps[:, 4:8, :].rearrange("p b (i r) -> p (b i) r", i=4)).then_inc(pt_kept, 1)
                act.wait_ge(summed, 1)
                act.copy(m.f[:, QC:QC + 4, TP:T], m.ps[:, 0, 0:P].rearrange("p (h r) -> p h r", h=4))


def attend_window_samples(nc, m, d, sem):
    scale = 64 ** -0.5
    with ExitStack() as ctx:
        kk = ctx.enter_context(nc.sbuf_tensor("sw_k", [P, NB, WK], F32))
        cv = ctx.enter_context(nc.sbuf_tensor("sw_v", [P, NB, P], F32))
        q = ctx.enter_context(nc.sbuf_tensor("sw_q", [P, 4, 32], F32))
        s = ctx.enter_context(nc.sbuf_tensor("sw_s", [P, 2, NB, WK], F32))
        new = ctx.enter_context(nc.sbuf_tensor("sw_new", [P, 2, 32], F32))
        pt = ctx.enter_context(nc.sbuf_tensor("sw_pt", [P, 2, NB + 1, P], F32))
        st = ctx.enter_context(nc.sbuf_tensor("sw_stats", [P, 2, 6], F32))
        loaded, keys, chained, scored, maxed, expd, normed, turned, pt_kept, summed = (
            sem(f"sw_{x}") for x in
            ("loaded", "keys", "chained", "scored", "maxed", "expd", "normed", "turned", "pt_kept", "summed"))
        with nc.Block() as block:

            @block.sync
            def _(sp):
                sp.dma_start(kk[:, :, 0:WIN], d["win_k"]).then_inc(loaded, 16)
                sp.dma_start(cv[:], d["win_v"].rearrange("b s c -> s b c")).then_inc(loaded, 16)
                sp.wait_ge(loaded, 32)
                sp.wait_ge(keys, 2)
                sp.dma_start(d["out_wks"], kk[:, :, TS:WK]).then_inc(m.stored, 16)
                sp.wait_ge(m.stored, m.stores - 16)

            @block.vector
            def _(dve):
                chain = Chain(dve, chained)
                dve.tensor_copy(kk[:, :, WIN:WK], m.f[:, KA, TP:T].rearrange("p (b s) -> p b s", b=NB)).then_inc(keys, 1)
                dve.tensor_copy(q[:], m.f[:, QA:QA + 4, TP:T]).then_inc(keys, 1)
                own = m.const[:, C_OWN:C_OWN + NB].unsqueeze(2).broadcast_to([P, NB, WK])
                for kv in range(2):
                    dve.wait_ge(scored, kv + 1)
                    for c in range(4):
                        bias = m.bias_s[:, kv, :].unsqueeze(1).broadcast_to([P, 2, WK])
                        ins = dve.scalar_tensor_tensor(s[:, kv, 2 * c:2 * c + 2, :],
                                                       m.ps[:, 4 * kv + c, 0:2 * WK].rearrange("p (b k) -> p b k", b=2),
                                                       scale, bias, ALU.mult, ALU.add)
                    chain(ins)
                    chain(dve.tensor_tensor(s[:, kv], s[:, kv], own, ALU.add))
                    chain(dve.tensor_reduce(st[:, kv, 0:1], s[:, kv].rearrange("p b k -> p (b k)"), AX, ALU.max))
                    chain(dve.tensor_tensor(st[:, kv, 0:1], st[:, kv, 0:1], m.sink_s[:, kv:kv + 1], ALU.max))
                    chain(dve.tensor_scalar(st[:, kv, 1:2], st[:, kv, 0:1], -1.0, None, ALU.mult))
                    dve.tensor_tensor(st[:, kv, 3:4], m.sink_s[:, kv:kv + 1], st[:, kv, 1:2], ALU.add).then_inc(maxed, 1)
                for kv in range(2):
                    dve.wait_ge(expd, kv + 1)
                    chain(dve.tensor_tensor(st[:, kv, 4:5], st[:, kv, 2:3], st[:, kv, 3:4], ALU.add))
                    chain(dve.reciprocal(st[:, kv, 5:6], st[:, kv, 4:5]))
                    chain(dve.tensor_scalar(s[:, kv], s[:, kv], st[:, kv, 5:6], None, ALU.mult))
                    dve.tensor_copy(new[:, kv].rearrange("p (b s) -> p b s", b=NB), s[:, kv, :, WIN:WK]).then_inc(normed, 1)

            @block.tensor
            def _(pe):
                pe.wait_ge(loaded, 32)
                pe.wait_ge(keys, 2)
                ident = m.const[:, C_ID:C_ID + P]
                for kv in range(2):
                    rows = slice(64 * kv, 64 * kv + 64)
                    for c in range(4):
                        mm = pe.matmul(m.ps[:, 4 * kv + c, 0:2 * WK], q[rows].rearrange("p g t -> p (g t)"),
                                       kk[rows, 2 * c:2 * c + 2, :].rearrange("p b k -> p (b k)"), start=True, stop=True)
                    mm.then_inc(scored, 1)
                for kv in range(2):
                    rows = slice(64 * kv, 64 * kv + 64)
                    pe.wait_ge(normed, kv + 1)
                    if kv == 0:
                        pe.wait_ge(maxed, 2)
                    for b in range(NB):
                        pe.transpose(m.ps[:, 4 * kv + b // 4, (b % 4) * P:(b % 4) * P + P], s[:, kv, b, 0:WIN], ident)
                    pe.transpose(m.ps[0:32, 4 * kv + 2, 0:P], new[:, kv, :], ident).then_inc(turned, 1)
                    pe.wait_ge(pt_kept, kv + 1)
                    for b in range(NB):
                        pe.matmul(m.ps[rows, 4 * kv + 3, 0:P], cv[:, b, rows], pt[:, kv, b, :], start=(b == 0), stop=False)
                    pe.matmul(m.ps[rows, 4 * kv + 3, 0:P], m.av[0:32, BLK, rows], pt[0:32, kv, NB, :], start=False,
                              stop=True).then_inc(summed, 1)

            @block.scalar
            def _(act):
                for kv in range(2):
                    act.wait_ge(maxed, kv + 1)
                    act.activation(s[:, kv], s[:, kv], ACT.Exp, bias=st[:, kv, 1:2], accum_out=st[:, kv, 2:3])
                    act.activation(st[:, kv, 3:4], st[:, kv, 3:4], ACT.Exp).then_inc(expd, 1)
                for kv in range(2):
                    rows = slice(64 * kv, 64 * kv + 64)
                    act.wait_ge(turned, kv + 1)
                    act.copy(pt[:, kv, 0:NB, :],
                             m.ps[:, 4 * kv:4 * kv + 2, :].rearrange("p b (i r) -> p (b i) r", i=4))
                    act.copy(pt[0:32, kv, NB, :], m.ps[0:32, 4 * kv + 2, 0:P]).then_inc(pt_kept, 1)
                    act.wait_ge(summed, kv + 1)
                    act.copy(m.f[rows, QA:QA + 4, TP:T], m.ps[rows, 4 * kv + 3, 0:P].rearrange("p (g t) -> p g t", g=4))


def prepare_gla(nc, m, g, d, sem):
    zed, done, chained, a_done, b_done, x_done = (sem(f"gla_{x}") for x in ("zed", "done", "chained", "abs", "exp", "ln"))
    tmp_done = sem("gla_tmp")
    with ExitStack() as ctx:
        z = ctx.enter_context(nc.sbuf_tensor("gla_z", [P, 2, T], F32))
        l = ctx.enter_context(nc.sbuf_tensor("gla_l", [P, 2, T], F32))
        scan = ctx.enter_context(nc.sbuf_tensor("gla_scan", [P, T], F32))
        scan_loaded = sem("gla_scan_loaded")
        with nc.Block() as block:

            @block.sync
            def _(sp):
                sp.dma_start(scan[:], d["scan"].broadcast_to([P, T])).then_inc(scan_loaded, 16)

            @block.tensor
            def _(pe):
                for j in range(2):
                    for c, (a, e) in enumerate(CHUNKS):
                        pe.matmul(m.ps[:, 3 * j + c, 0:CH], m.w2[:, j * P:j * P + P], m.lr[:, a:e],
                                  start=True, stop=True).then_inc(zed, 1)

            @block.scalar
            def _(act):
                for j in range(2):
                    for c, (a, e) in enumerate(CHUNKS):
                        act.wait_ge(zed, 3 * j + c + 1)
                        act.activation(z[:, j, a:e], m.ps[:, 3 * j + c, 0:CH], ACT.Identity,
                                       bias=m.gbias[:, j:j + 1]).then_inc(done, 1)
                act.wait_ge(done, 6)
                act.activation(l[:], z[:], ACT.Abs).then_inc(a_done, 1)
                act.wait_ge(a_done, 1)
                act.activation(l[:], l[:], ACT.Exp, scale=-1.0).then_inc(b_done, 1)
                act.wait_ge(b_done, 1)
                act.activation(l[:], l[:], ACT.Ln, bias=m.one[:, 0:1]).then_inc(x_done, 1)

            @block.vector
            def _(dve):
                chain = Chain(dve, chained)
                dve.wait_ge(a_done, 1)
                chain(dve.tensor_scalar(z[:], z[:], 0.0, 1.0 / 16, ALU.min, ALU.mult))
                dve.wait_ge(x_done, 1)
                chain(dve.scalar_tensor_tensor(l[:], l[:], -1.0 / 16, z[:], ALU.mult, ALU.add))
                dve.wait_ge(scan_loaded, 16)
                for j in range(2):
                    dve.tensor_tensor_scan(g.b[:, j, :], scan[:], l[:, j, :], 0.0, ALU.mult, ALU.add)

        spans = [(0, TP // GC, GC, GC // 2 - 1), (TP, NB, TS, 1)]
        e, u = z, l
        grown, powered, times = sem("gla_grown"), sem("gla_powered"), sem("gla_times")
        with nc.Block() as block:

            @block.vector
            def _(dve):
                chain = Chain(dve, chained, 2)

                def minus(out, sign, at):
                    for j in range(2):
                        for c0, n, w, mid in spans:
                            x = g.b[:, j, c0:c0 + n * w].rearrange("p (c t) -> p c t", t=w)
                            y = out[:, j, c0:c0 + n * w].rearrange("p (c t) -> p c t", t=w)
                            k = mid if at == "mid" else w - 1
                            ref = x[:, :, k:k + 1].broadcast_to([P, n, w])
                            ins = dve.tensor_tensor(y, *((x, ref) if sign > 0 else (ref, x)), ALU.subtract)
                            if (j, c0) != (1, TP):
                                chain(ins)
                    return ins

                qb, kb = m.f[:, QB:QB + 2, :], m.f[:, KB:KB + 2, :]
                minus(u, -1, "last").then_inc(grown, 1)
                chain(minus(e, 1, "mid"))
                dve.tensor_scalar(e[:], e[:], 40.0, -40.0, ALU.min, ALU.max).then_inc(grown, 1)
                dve.wait_ge(powered, 1)
                chain(dve.scalar_tensor_tensor(g.aq[:], qb, 64 ** -0.5, g.aq[:], ALU.mult, ALU.mult))
                dve.wait_ge(powered, 2)
                dve.tensor_tensor(g.kl[:], kb, u[:], ALU.mult).then_inc(times, 1)
                dve.wait_ge(powered, 3)
                dve.scalar_tensor_tensor(qb, qb, 64 ** -0.5, u[:], ALU.mult, ALU.mult)
                dve.wait_ge(powered, 4)
                dve.wait_ge(times, 1)
                dve.tensor_tensor(kb, kb, e[:], ALU.mult)

            @block.scalar
            def _(act):
                act.activation(g.aq[:], g.b[:], ACT.Exp).then_inc(powered, 1)
                for c0, n, w, _ in spans:
                    for j in range(2):
                        last = g.b[:, j, c0:c0 + n * w].rearrange("p (c t) -> p c t", t=w)[:, :, w - 1]
                        first = 0 if c0 == 0 else TP // GC
                        act.activation(g.el[:, j, first:first + n], last, ACT.Exp)
                act.wait_ge(grown, 1)
                act.activation(u[:], u[:], ACT.Exp).then_inc(powered, 1)
                act.wait_ge(grown, 2)
                act.wait_ge(times, 1)
                act.activation(u[:], e[:], ACT.Exp).then_inc(powered, 1)
                act.wait_ge(powered, 3)
                act.activation(e[:], e[:], ACT.Exp, scale=-1.0).then_inc(powered, 1)


def turn_keys(nc, m, g, sem):
    turned, kept = sem("turn_turned"), sem("turn_kept")
    with nc.Block() as block:

        @block.tensor
        def _(pe):
            for t in range(NT):
                r = tile_rows(t)
                if t >= 8:
                    pe.wait_ge(kept, t - 7)
                for j in range(2):
                    mm = pe.transpose(m.ps[0:r, t % 8, j * P:j * P + P], g.kl[:, j, t * P:t * P + r],
                                      m.const[:, C_ID:C_ID + P])
                mm.then_inc(turned, 1)

        @block.scalar
        def _(act):
            for t in range(NT):
                r = tile_rows(t)
                act.wait_ge(turned, t + 1)
                act.copy(g.kt[0:r, t, :], m.ps[0:r, t % 8, 0:256]).then_inc(kept, 1)


def gla_prompt(nc, m, g, d, sem):
    with ExitStack() as ctx:
        state = ctx.enter_context(nc.sbuf_tensor("gla_state", [P, 3, 2, P], F32))
        at = ctx.enter_context(nc.sbuf_tensor("gla_at", [P, 2, 2, GC], F32))
        sg = ctx.enter_context(nc.sbuf_tensor("silu_sg", [P, 2, T], F32))
        scored, masked, updated, advanced, inner, outer, copied, kept, sigmoid, gated = (
            sem(f"glap_{x}") for x in
            ("scored", "masked", "updated", "advanced", "inner", "outer", "copied", "kept", "sigmoid", "gated"))
        with nc.Block() as block:

            @block.tensor
            def _(pe):
                def scores(n):
                    if n >= 1:
                        pe.wait_ge(masked, n)
                    for e in range(2):
                        for half in range(2):
                            for j in range(2):
                                a = n * P + half * GC
                                rows = slice(64 * e, 64 * e + 64)
                                mm = pe.matmul(m.ps[64 * half:64 * half + 64, e, j * GC:j * GC + GC],
                                               m.f[rows, KB + j, a:a + GC], m.f[rows, QB + j, a:a + GC],
                                               start=True, stop=True)
                    mm.then_inc(scored, 1)

                def updates(n):
                    for half in range(2):
                        if n >= 1:
                            pe.wait_ge(advanced, 1 + 2 * (n - 1) + half + 1)
                        for j in range(2):
                            for e in range(2):
                                rows = slice(64 * half, 64 * half + 64)
                                h = 2 * j + e
                                mm = pe.matmul(m.ps[64 * e:64 * e + 64, 6 + half, j * P:j * P + P],
                                               g.kt[rows, n, h * 64:h * 64 + 64], m.bv[rows, n, h * P:h * P + P],
                                               start=True, stop=True)
                        mm.then_inc(updated, 1)

                scores(0)
                updates(0)
                for n in range(BLK):
                    if n + 1 < BLK:
                        scores(n + 1)
                        updates(n + 1)
                    pe.wait_ge(masked, n + 1)
                    if n >= 1:
                        pe.wait_ge(copied, n)
                    for half in range(2):
                        rows = slice(64 * half, 64 * half + 64)
                        for j in range(2):
                            for e in range(2):
                                mm = pe.matmul(m.ps[:, 2 + half, e * P + j * GC:e * P + j * GC + GC],
                                               m.bv[rows, n, (2 * j + e) * P:(2 * j + e) * P + P],
                                               at[rows, e, j, :], start=True, stop=True)
                    mm.then_inc(inner, 1)
                    if n >= 1:
                        pe.wait_ge(kept, n)
                    for half in range(2):
                        c = 2 * n + half
                        pe.wait_ge(advanced, c + 1)
                        for e in range(2):
                            rows = slice(64 * e, 64 * e + 64)
                            for j in range(2):
                                mm = pe.matmul(m.ps[:, 4 + e, j * P + half * GC:j * P + half * GC + GC],
                                               state[rows, c % 3, j, :], g.aq[rows, j, c * GC:c * GC + GC],
                                               start=True, stop=True)
                        mm.then_inc(outer, 1)

            @block.vector
            def _(dve):
                dve.memset(state[:, 0], 0.0).then_inc(advanced, 1)
                tri = m.const[:, C_TRI:C_TRI + GC].unsqueeze(1).broadcast_to([P, 2, GC])

                def mask(n):
                    dve.wait_ge(scored, n + 1)
                    if n >= 1:
                        dve.wait_ge(inner, n)
                    for e in range(2):
                        ins = dve.tensor_tensor(at[:, e], m.ps[:, e, 0:P].rearrange("p (j t) -> p j t", j=2), tri,
                                                ALU.mult)
                    ins.then_inc(masked, 1)

                def finish(n):
                    dve.wait_ge(copied, n + 1)
                    for e, dst in enumerate((g.aq, g.kl)):
                        x = dst[:, :, n * P:n * P + P]
                        ins = dve.tensor_tensor(x, x, m.ps[:, 4 + e, 0:256].rearrange("p (j t) -> p j t", j=2), ALU.add)
                    ins.then_inc(kept, 1)

                mask(0)
                for n in range(BLK):
                    for half in range(2):
                        c = 2 * n + half
                        dve.wait_ge(updated, c + 1)
                        dve.wait_ge(advanced, c + 1)
                        if c >= 2:
                            dve.wait_ge(outer, c - 1)
                        for j in range(2):
                            ins = dve.scalar_tensor_tensor(state[:, (c + 1) % 3, j, :], state[:, c % 3, j, :],
                                                           g.el[:, j, c:c + 1], m.ps[:, 6 + half, j * P:j * P + P],
                                                           ALU.mult, ALU.add)
                        ins.then_inc(advanced, 1)
                    if n + 1 < BLK:
                        mask(n + 1)
                    if n:
                        finish(n - 1)
                finish(BLK - 1)

            @block.gpsimd
            def _(pool):
                for h in range(4):
                    pool.wait_ge(sigmoid, h + 1)
                    r = m.f[:, RB + h, :]
                    pool.tensor_tensor(r, r, sg[:, h % 2], ALU.mult).then_inc(gated, 1)

            @block.scalar
            def _(act):
                for h in range(4):
                    if h >= 2:
                        act.wait_ge(gated, h - 1)
                    act.activation(sg[:, h % 2], m.f[:, RB + h, :], ACT.Sigmoid).then_inc(sigmoid, 1)
                for n in range(BLK):
                    act.wait_ge(inner, n + 1)
                    act.wait_ge(outer, 2 * n + 2)
                    for half in range(2):
                        for e, dst in enumerate((g.aq, g.kl)):
                            a = n * P + half * GC
                            ins = act.copy(dst[:, :, a:a + GC],
                                           m.ps[:, 2 + half, e * P:e * P + P].rearrange("p (j t) -> p j t", j=2))
                    ins.then_inc(copied, 1)

            @block.sync
            def _(sp):
                sp.wait_ge(advanced, 1 + 2 * BLK)
                sp.dma_start(d["out_sp"], state[:, (2 * BLK) % 3]).then_inc(m.stored, 16)
                sp.wait_ge(m.stored, m.stores)


def gla_samples(nc, m, g, d, sem):
    with ExitStack() as ctx:
        s0 = ctx.enter_context(nc.sbuf_tensor("glas_s0", [P, 2, NB, P], F32))
        vm = ctx.enter_context(nc.sbuf_tensor("glas_vm", [32, NB, 512], F32))
        at = ctx.enter_context(nc.sbuf_tensor("glas_at", [32, 2, 2, 32], F32))
        loaded, scored, masked, inner, outer, copied, split, updated, advanced, out = (
            sem(f"glas_{x}") for x in
            ("loaded", "scored", "masked", "inner", "outer", "copied", "split", "updated", "advanced", "out"))
        cols = slice(TP, T)
        with nc.Block() as block:

            @block.sync
            def _(sp):
                for e in range(2):
                    for j in range(2):
                        sp.dma_start(s0[64 * e:64 * e + 64, j], d["state"][:, 2 * j + e].rearrange("b k v -> k b v")
                                     ).then_inc(loaded, 16)
                sp.wait_ge(advanced, 1)
                for e in range(2):
                    for j in range(2):
                        sp.dma_start(d["out_ss"][:, 2 * j + e].rearrange("b k v -> k b v"), s0[64 * e:64 * e + 64, j]
                                     ).then_inc(out, 16)
                sp.wait_ge(out, 64)

            @block.tensor
            def _(pe):
                for e in range(2):
                    rows = slice(64 * e, 64 * e + 64)
                    for j in range(2):
                        mm = pe.matmul(m.ps[0:32, e, j * 32:j * 32 + 32], m.f[rows, KB + j, cols], m.f[rows, QB + j, cols],
                                       start=True, stop=True)
                mm.then_inc(scored, 1)
                pe.wait_ge(masked, 1)
                for e in range(2):
                    for j in range(2):
                        mm = pe.matmul(m.ps[:, 2, e * 64 + j * 32:e * 64 + j * 32 + 32],
                                       m.bv[0:32, BLK, (2 * j + e) * P:(2 * j + e) * P + P], at[:, e, j, :],
                                       start=True, stop=True)
                mm.then_inc(inner, 1)
                pe.wait_ge(loaded, 64)
                for e in range(2):
                    rows = slice(64 * e, 64 * e + 64)
                    for j in range(2):
                        for b in range(NB):
                            c = j * 32 + TS * b
                            mm = pe.matmul(m.ps[:, 4 + e, c:c + TS], s0[rows, j, b, :],
                                           g.aq[rows, j, TP + TS * b:TP + TS * b + TS], start=True, stop=True)
                mm.then_inc(outer, 1)
                pe.wait_ge(split, 1)
                banks = [6, 7, 0, 3]
                for j in range(2):
                    for q in range(2):
                        for e in range(2):
                            h = 2 * j + e
                            mm = pe.matmul(m.ps[64 * e:64 * e + 64, banks[2 * j + q], :].rearrange("p (b v) -> p b v", b=4),
                                           g.kt[0:32, BLK, h * 64:h * 64 + 64],
                                           vm[:, 4 * q:4 * q + 4, h * P:h * P + P], start=True, stop=True)
                mm.then_inc(updated, 1)

            @block.vector
            def _(dve):
                own = m.const[0:32, C_SEL:C_SEL + NB].unsqueeze(2).broadcast_to([32, NB, 512])
                dve.wait_ge(scored, 1)
                tri = m.const[0:32, C_TRIS:C_TRIS + 32].unsqueeze(1).broadcast_to([32, 2, 32])
                for e in range(2):
                    ins = dve.tensor_tensor(at[:, e], m.ps[0:32, e, 0:64].rearrange("p (j t) -> p j t", j=2), tri, ALU.mult)
                ins.then_inc(masked, 1)
                dve.tensor_tensor(vm[:], m.bv[0:32, BLK, :].unsqueeze(1).broadcast_to([32, NB, 512]), own,
                                  ALU.mult).then_inc(split, 1)
                dve.wait_ge(copied, 1)
                dve.wait_ge(outer, 1)
                for e, dst in enumerate((g.aq, g.kl)):
                    x = dst[:, :, cols]
                    dve.tensor_tensor(x, x, m.ps[:, 4 + e, 0:64].rearrange("p (j t) -> p j t", j=2), ALU.add)
                dve.wait_ge(updated, 1)
                banks = [6, 7, 0, 3]
                for j in range(2):
                    for b in range(NB):
                        ins = dve.scalar_tensor_tensor(s0[:, j, b, :], s0[:, j, b, :],
                                                       g.el[:, j, TP // GC + b:TP // GC + b + 1],
                                                       m.ps[:, banks[2 * j + b // 4], (b % 4) * P:(b % 4) * P + P],
                                                       ALU.mult, ALU.add)
                ins.then_inc(advanced, 1)

            @block.scalar
            def _(act):
                act.wait_ge(inner, 1)
                act.wait_ge(outer, 1)
                for e, dst in enumerate((g.aq, g.kl)):
                    ins = act.copy(dst[:, :, cols], m.ps[:, 2, e * 64:e * 64 + 64].rearrange("p (j t) -> p j t", j=2))
                ins.then_inc(copied, 1)


def finish_gla(nc, m, g, d, sem):
    units = [((g.aq, g.kl)[h % 2][:, h // 2, a:z], m.ones[:], P, m.gng) for h in range(4) for a, z in CHUNKS]
    norm_units(nc, m, sem, "glan", units)
    with nc.Block() as block:

        @block.vector
        def _(dve):
            for h in range(4):
                dve.tensor_tensor(m.f[:, RB + h, :], m.f[:, RB + h, :], (g.aq, g.kl)[h % 2][:, h // 2, :], ALU.mult)


def merge(nc, m, d, sem):
    first = (QA, RB, QC)
    w_high, w_low = m.w_spare
    with ExitStack() as ctx:
        raw = ctx.enter_context(nc.sbuf_tensor("wg_raw", [P, KT, P], F32))
        wb = ctx.enter_context(nc.sbuf_tensor("wb_ring", [P, 2, 4, P], F32))
        sg = ctx.enter_context(nc.sbuf_tensor("merge_sg", [P, 4, CH], F32))
        b_loaded = [sem("wb_loaded0"), sem("wb_loaded1")]
        loaded, high, low, x_rounded, x_split, done, gated, added, multiplied = (
            sem(f"merge_{x}") for x in
            ("loaded", "high", "low", "x_rounded", "x_split", "done", "gated", "added", "multiplied"))
        steps = [(j, r) for j in range(KT) for r in range(3)]
        units = [(j, r, c) for j, r in steps for c in range(3)]
        with nc.Block() as block:

            @block.sync
            def _(sp):
                for n, (j, r) in enumerate(steps):
                    if n:
                        sp.wait_ge(low, n)
                    sp.dma_start(raw[:], d["w_m"][j][:, 8 * r:8 * r + 8]).then_inc(loaded, 16)
                    if n >= 2:
                        sp.wait_ge(done, 3 * (n - 1))
                    sp.dma_start(wb[:, n % 2], d["w_m"][j][:, 24 + 4 * r:28 + 4 * r]).then_inc(b_loaded[n % 2], 16)

            @block.tensor
            def _(pe):
                for u, (j, r, c) in enumerate(units):
                    a, z = CHUNKS[c]
                    n = u // 3
                    if c == 0:
                        pe.wait_ge(low, n + 1)
                        pe.wait_ge(b_loaded[n % 2], 16 * (n // 2 + 1))
                    if u >= 4:
                        pe.wait_ge(multiplied, u - 3)
                    for k in range(KT):
                        if u == 0:
                            pe.wait_ge(x_split, k + 1)
                        exact_product(pe, m.ps[:, 2 * (u % 4), 0:CH], (w_high[:, n % 2, k, :], w_low[:, n % 2, k, :]),
                                      (m.x_high[:, k, a:z], m.x_low[:, k, a:z]), k == 0, k == KT - 1)
                    for k in range(4):
                        mm = pe.matmul(m.ps[:, 2 * (u % 4) + 1, 0:CH], wb[:, n % 2, k, :],
                                       m.f[:, first[r] + k, a:z], start=(k == 0), stop=(k == 3))
                    mm.then_inc(done, 1)

            def adds(v):
                return 6 * (v // 9) + max(0, v % 9 - 2)

            @block.scalar
            def _(act):
                def round_weights(n):
                    if n < len(steps):
                        act.wait_ge(loaded, 16 * (n + 1))
                        if n >= 2:
                            act.wait_ge(done, 3 * (n - 1))
                        act.copy(w_high[:, n % 2], raw[:]).then_inc(high, 1)

                round_weights(0)
                for k in range(KT):
                    act.copy(m.x_high[:, k, :], m.x2[:, k, :]).then_inc(x_rounded, 1)
                for u, (j, r, c) in enumerate(units):
                    if c == 0:
                        round_weights(u // 3 + 1)
                    act.wait_ge(done, u + 1)
                    if u >= 4:
                        act.wait_ge(multiplied, u - 3)
                        if adds(u - 4):
                            act.wait_ge(added, adds(u - 4))
                    act.activation(sg[:, u % 4], m.ps[:, 2 * (u % 4), 0:CH], ACT.Sigmoid,
                                   bias=m.gates_b[:, j, r:r + 1]).then_inc(gated, 1)

            @block.vector
            def _(dve):
                def split_weights(n):
                    if n < len(steps):
                        dve.wait_ge(high, n + 1)
                        dve.tensor_tensor(w_low[:, n % 2], raw[:], w_high[:, n % 2].bitcast(F32), ALU.subtract).then_inc(low, 1)

                split_weights(0)
                for k in range(KT):
                    dve.wait_ge(x_rounded, k + 1)
                    dve.tensor_tensor(m.x_low[:, k, :], m.x2[:, k, :], m.x_high[:, k, :].bitcast(F32),
                                      ALU.subtract).then_inc(x_split, 1)
                for u, (j, r, c) in enumerate(units):
                    if c == 0:
                        split_weights(u // 3 + 1)
                    a, z = CHUNKS[c]
                    dst = m.h[:, j, a:z]
                    dve.wait_ge(gated, u + 1)
                    x = dst if r == 0 else sg[:, u % 4]
                    dve.tensor_tensor(x, sg[:, u % 4], m.ps[:, 2 * (u % 4) + 1, 0:CH], ALU.mult).then_inc(multiplied, 1)
                    if r:
                        dve.wait_ge(multiplied, u + 1)
                        dve.tensor_tensor(dst, dst, x, ALU.add).then_inc(added, 1)
                        dve.wait_ge(added, adds(u))


def project_out(nc, m, d, sem):
    w_high, w_low = m.w_spare
    h_high, h_low = m.x_high, m.h_low
    with ExitStack() as ctx:
        raw = ctx.enter_context(nc.sbuf_tensor("wo_raw", [P, KT, P], F32))
        x_loaded = sem("wo_x_loaded")
        loaded, high, low, h_rounded, h_split, done, added = (
            sem(f"wo_{x}") for x in ("loaded", "high", "low", "h_rounded", "h_split", "done", "added"))
        with nc.Block() as block:

            @block.sync
            def _(sp):
                for n in range(KT):
                    if n:
                        sp.wait_ge(low, n)
                    sp.dma_start(raw[:], d["w_out"][n]).then_inc(loaded, 16)
                    if n == 0:
                        sp.dma_start(m.x2[:], d["x"][:, :, 0:T]).then_inc(x_loaded, 16)

            @block.tensor
            def _(pe):
                for n in range(KT):
                    pe.wait_ge(low, n + 1)
                    for k in range(KT):
                        if n == 0:
                            pe.wait_ge(h_split, k + 1)
                        for c, (a, z) in enumerate(CHUNKS):
                            u = 3 * n + c
                            if k == 0 and u >= 6:
                                pe.wait_ge(added, u - 5)
                            mm = exact_product(pe, m.ps[:, u % 6, 0:CH], (w_high[:, n % 2, k, :], w_low[:, n % 2, k, :]),
                                               (h_high[:, k, a:z], h_low[:, k, a:z]), k == 0, k == KT - 1)
                            if k == KT - 1:
                                mm.then_inc(done, 1)

            @block.scalar
            def _(act):
                def round_weights(n):
                    act.wait_ge(loaded, 16 * (n + 1))
                    if n >= 2:
                        act.wait_ge(done, 3 * (n - 1))
                    act.copy(w_high[:, n % 2], raw[:]).then_inc(high, 1)

                for k in range(KT):
                    act.copy(h_high[:, k, :], m.h[:, k, :]).then_inc(h_rounded, 1)
                    if k == 0:
                        round_weights(0)
                for n in range(1, KT):
                    round_weights(n)

            @block.vector
            def _(dve):
                def split_weights(n):
                    dve.wait_ge(high, n + 1)
                    dve.tensor_tensor(w_low[:, n % 2], raw[:], w_high[:, n % 2].bitcast(F32), ALU.subtract).then_inc(low, 1)

                for k in range(KT):
                    dve.wait_ge(h_rounded, k + 1)
                    dve.tensor_tensor(h_low[:, k, :], m.h[:, k, :], h_high[:, k, :].bitcast(F32),
                                      ALU.subtract).then_inc(h_split, 1)
                    if k == 0:
                        split_weights(0)
                split_weights(1)
                dve.wait_ge(x_loaded, 16)
                for n in range(KT):
                    if 1 <= n < KT - 1:
                        split_weights(n + 1)
                    for c, (a, z) in enumerate(CHUNKS):
                        u = 3 * n + c
                        dve.wait_ge(done, u + 1)
                        dve.tensor_tensor(m.x2[:, n, a:z], m.x2[:, n, a:z], m.ps[:, u % 6, 0:CH], ALU.add).then_inc(added, 1)


def choose_experts(nc, m, d, sem):
    NEGK = -3e38
    RING = 3
    AHEAD = 2
    TURNS = 2 * HEADS
    turns, e = [[("q", n + 1)] * (n + 1 < TURNS) for n in range(TURNS + 1)], 0
    for n in range(2, TURNS):
        for _ in range(1 + n % 2):
            turns[n].append(("u", e))
            e += 1
    turns[TURNS] = [("u", x) for x in range(e, KEPT)]
    jobs = [("q", 0)] + [job for turn in turns for job in turn]
    with ExitStack() as ctx:
        def sb(name, shape, dt=F32):
            return ctx.enter_context(nc.sbuf_tensor(name, shape, dt))

        raw = sb("wq_raw", [P, 2, KT, P])
        w = (sb("wq_high", [P, RING, KT, P], F32R), sb("wq_low", [P, RING, KT, P], F32R))
        hid = sb("kept_act", [P, 2, T])
        keys = sb("keys", [P, 2, NK])
        q = sb("pq", [P, 2, T])
        sc = sb("psc", [P, AHEAD, NT, NK])
        top = sb("ptop", [P, 2, NT, TOPK])
        idx = sb("pidx", [P, 2, NT, TOPK], U32)
        idf = sb("pidf", [P, 2, NT, TOPK], BF16)
        picked = sb("ppicked", [P, 2 * NT, TOPK, TOPK], BF16)
        iota = sb("piota", [P, TOPK], BF16)
        cand = sb("pcand", [P, NT, TOPK, TOPK])
        best = sb("pbest", [P, NT, TOPK])
        expo = sb("pexpo", [P, NT, TOPK])
        pos = sb("ppos", [P, NT, TOPK], U32)
        half = sb("phalf", [P, 2, NT, TOPK], U32)
        halff = sb("phalff", [P, 2, NT, TOPK], BF16)
        tot = sb("ptot", [P, NT])
        w_loaded = [sem("wq_loaded0"), sem("wq_loaded1")]
        kept_stored = [sem("kept_stored0"), sem("kept_stored1")]
        w_high, w_low, keys_loaded, hidden, gelu_done = (
            sem(f"wq_{x}") for x in ("high", "low", "keys_loaded", "hidden", "gelu"))
        projected, q_kept, scored, sc_kept, sc_used, seq, centred, expd = (
            sem(f"peer_{x}") for x in
            ("projected", "q_kept", "scored", "sc_kept", "sc_used", "seq", "centred", "expd"))
        with nc.Block() as block:

            def exp_gates(act, h):
                act.wait_ge(centred, h + 1)
                act.activation(expo[:], expo[:], ACT.Exp).then_inc(expd, 1)

            def gate_sums(h, dve, step, after):
                step(dve.tensor_reduce(tot[:], expo[:], AX, ALU.add))
                after(0)
                step(dve.reciprocal(tot[:], tot[:]))
                after(0)
                step(dve.tensor_tensor(m.gate[:, :, h * TOPK:h * TOPK + TOPK], expo[:],
                                       tot[:].unsqueeze(2).broadcast_to([P, NT, TOPK]), ALU.mult))
                after(0)

            @block.sync
            def _(sp):
                sp.dma_start(keys[:], d["keys"]).then_inc(keys_loaded, 16)
                for j, (kind, n) in enumerate(jobs):
                    if j >= 2:
                        sp.wait_ge(w_low, j - 1)
                    sp.dma_start(raw[:, j % 2], d["w_q" if kind == "q" else "u"][n]).then_inc(w_loaded[j % 2], 16)

            @block.tensor
            def _(pe):
                def product(j):
                    kind, n = jobs[j]
                    pe.wait_ge(w_low, j + 1)
                    if n and kind == "q":
                        pe.wait_ge(q_kept, n)
                    if n and kind == "u":
                        pe.wait_ge(gelu_done, 3 * n)
                    for c, (a, z) in enumerate(CHUNKS):
                        for k in range(KT):
                            mm = exact_product(pe, m.ps[:, (0 if kind == "q" else 3) + c, 0:CH],
                                               [x[:, j % RING, k, :] for x in w], [x[:, k, a:z] for x in m.hn],
                                               k == 0, k == KT - 1)
                        mm.then_inc(projected if kind == "q" else hidden, 1)

                def scores(n):
                    pe.wait_ge(q_kept, n + 1)
                    for g in range(3):
                        u = 3 * n + g
                        if u >= 2:
                            pe.wait_ge(sc_kept, u - 1)
                        for t in range(4 * g, min(4 * g + 4, NT)):
                            r = tile_rows(t)
                            mm = pe.matmul(m.ps[0:r, 6 + u % 2, (t % 4) * NK:(t % 4) * NK + NK],
                                           q[:, n % 2, t * P:t * P + r], keys[:, n % 2, :], start=True, stop=True)
                        mm.then_inc(scored, 1)

                product(0)
                j = 1
                pe.wait_ge(keys_loaded, 16)
                for n, turn in enumerate(turns):
                    for _ in turn:
                        product(j)
                        j += 1
                    if n < TURNS:
                        scores(n)

            @block.gpsimd
            def _(pool):
                for j in range(len(jobs)):
                    pool.wait_ge(w_high, j + 1)
                    pool.tensor_tensor(w[1][:, j % RING], raw[:, j % 2], w[0][:, j % RING].bitcast(F32),
                                       ALU.subtract).then_inc(w_low, 1)

            @block.scalar
            def _(act):
                def round_weights(j):
                    if j >= len(jobs):
                        return
                    act.wait_ge(w_loaded[j % 2], 16 * (j // 2 + 1))
                    if j >= RING:
                        kind, n = jobs[j - RING]
                        act.wait_ge(projected if kind == "q" else hidden, 3 * n + 3)
                    act.copy(w[0][:, j % RING], raw[:, j % 2]).then_inc(w_high, 1)

                def keep_hidden(e):
                    if e >= 2:
                        act.wait_ge(kept_stored[e % 2], 16 * (e // 2))
                    for c, (a, z) in enumerate(CHUNKS):
                        act.wait_ge(hidden, 3 * e + c + 1)
                        act.activation(hid[:, e % 2, a:z], m.ps[:, 3 + c, 0:CH], ACT.Gelu).then_inc(gelu_done, 1)
                    act.wait_ge(gelu_done, 3 * e + 3)
                    act.dma_start(d["kept"][e], hid[:, e % 2]).then_inc(kept_stored[e % 2], 16)

                def keep_scores(n):
                    if n >= AHEAD:
                        act.wait_ge(sc_used, n - AHEAD + 1)
                    for g in range(3):
                        u = 3 * n + g
                        act.wait_ge(scored, u + 1)
                        r, k = (P, 4) if g < 2 else (T - TP, 1)
                        act.copy(sc[0:r, n % AHEAD, 4 * g:4 * g + k, :],
                                 m.ps[0:r, 6 + u % 2, 0:k * NK].rearrange("p (t k) -> p t k", k=NK)).then_inc(sc_kept, 1)

                def keep_queries(n):
                    act.wait_ge(projected, 3 * n + 3)
                    if n >= 2:
                        act.wait_ge(scored, 3 * (n - 1))
                    act.copy(q[:, n % 2, :].rearrange("p (c t) -> p c t", c=3), m.ps[:, 0:3, 0:CH]).then_inc(q_kept, 1)

                for j in range(RING):
                    round_weights(j)
                keep_queries(0)
                round_weights(RING)
                j = 1
                for n, turn in enumerate(turns):
                    for kind, x in turn:
                        (keep_queries if kind == "q" else keep_hidden)(x)
                        round_weights(j + RING)
                        j += 1
                    if n < TURNS:
                        keep_scores(n)
                    if n % 2 and n >= 3:
                        exp_gates(act, n // 2 - 1)
                exp_gates(act, HEADS - 1)
                for x in kept_stored:
                    act.wait_ge(x, 16 * (KEPT // 2))

            @block.vector
            def _(dve):
                n_seq = 0

                def step(ins):
                    nonlocal n_seq
                    ins.then_inc(seq, 1)
                    n_seq += 1

                def after(k):
                    dve.wait_ge(seq, n_seq - k)

                for x in (idx[:, :, BLK, :], best[:, BLK, :], pos[:, BLK, :]):
                    step(dve.memset(x, 0))
                step(dve.tensor_copy(iota[:], m.const[:, C_IOTA:C_IOTA + TOPK]))
                after(0)

                def best16(values, out, where, tiles):
                    for t in tiles:
                        step(dve.max(out(t, 0), values(t)))
                    for t in tiles:
                        after(len(tiles) - 1)
                        step(dve.max_index(where(t, 0), out(t, 0), values(t)))
                    for t in tiles:
                        after(len(tiles) - 1)
                        step(dve.match_replace(values(t), out(t, 0), values(t), NEGK))
                    for t in tiles:
                        after(len(tiles) - 1)
                        step(dve.max(out(t, 1), values(t)))
                    for t in tiles:
                        after(len(tiles) - 1)
                        step(dve.max_index(where(t, 1), out(t, 1), values(t)))

                tiles = range(NT)
                for h in range(HEADS):
                    for s in range(2):
                        dve.wait_ge(sc_kept, 3 * (2 * h + s + 1))
                        best16(lambda t: sc[0:tile_rows(t), (2 * h + s) % AHEAD, t, :],
                               lambda t, i: top[0:tile_rows(t), s, t, 8 * i:8 * i + 8],
                               lambda t, i: idx[0:tile_rows(t), s, t, 8 * i:8 * i + 8], tiles)
                        after(0)
                        dve.tensor_copy(idf[:, s], idx[:, s]).then_inc(sc_used, 1)
                    for t in tiles:
                        r = tile_rows(t)
                        step(dve.tensor_tensor(cand[0:r, t], top[0:r, 0, t, :].unsqueeze(2).broadcast_to([r, TOPK, TOPK]),
                                               top[0:r, 1, t, :].unsqueeze(1).broadcast_to([r, TOPK, TOPK]), ALU.add))
                    after(0)
                    if h >= 1:
                        dve.wait_ge(expd, h)
                        gate_sums(h - 1, dve, step, after)
                    best16(lambda t: cand[0:tile_rows(t), t].rearrange("p a b -> p (a b)"),
                           lambda t, i: best[0:tile_rows(t), t, 8 * i:8 * i + 8],
                           lambda t, i: pos[0:tile_rows(t), t, 8 * i:8 * i + 8], tiles)
                    after(0)
                    dve.tensor_tensor(expo[:], best[:], best[:, :, 0:1].broadcast_to([P, NT, TOPK]), ALU.subtract).then_inc(centred, 1)
                    step(dve.tensor_scalar(half[:, 0], pos[:], 4, None, ALU.logical_shift_right))
                    step(dve.tensor_scalar(half[:, 1], pos[:], 15, None, ALU.bitwise_and))
                    after(0)
                    step(dve.tensor_copy(halff[:], half[:]))
                    after(0)
                    shape = [P, 2 * NT, TOPK, TOPK]
                    step(dve.tensor_tensor(picked[:], halff[:].rearrange("p s t k -> p (s t) k").unsqueeze(3).broadcast_to(shape),
                                           iota[:].unsqueeze(1).unsqueeze(1).broadcast_to(shape), ALU.is_equal))
                    after(0)
                    step(dve.tensor_tensor(picked[:], picked[:],
                                           idf[:].rearrange("p s t k -> p (s t) k").unsqueeze(2).broadcast_to(shape), ALU.mult))
                    after(0)
                    for s, dst in enumerate((m.e1, m.e2)):
                        step(dve.tensor_reduce(dst[:, :, h * TOPK:h * TOPK + TOPK], picked[:, s * NT:s * NT + NT], AX, ALU.add))
                    after(0)
                dve.wait_ge(expd, HEADS)
                gate_sums(HEADS - 1, dve, step, after)


def build_gate_matrix(nc, m, d, sem):
    with ExitStack() as ctx:
        def sb(name, shape, dt=F32):
            return ctx.enter_context(nc.sbuf_tensor(name, shape, dt))

        key1, key2, gate = sb("gm_key1", [P, T]), sb("gm_key2", [P, T], BF16), sb("gm_gate", [P, T])
        turned_in = (key1, key2, gate)
        iota2 = sb("gm_iota", [P, NK, G8], BF16)
        hot1, wgt = sb("gm_hot1", [P, 2, G8, NK]), sb("gm_wgt", [P, 2, G8, NK])
        hot2 = sb("gm_hot2", [P, 2, NK, G8], BF16)
        out = sb("gm_out", [P, 2, NK, TBG])
        turned, t_kept, hot1_made, hot2_made, weighted, last_weighted, used, copied = (
            sem(f"gm_{x}") for x in
            ("turned", "kept", "hot1_made", "hot2_made", "weighted", "last_weighted", "used", "copied"))
        stored = [sem("gm_stored0"), sem("gm_stored1")]
        srcs = (m.e1, m.e2, m.gate)
        iota = m.const[:, C_IOTA:C_IOTA + NK]
        with nc.Block() as block:

            @block.tensor
            def _(pe):
                for s in range(3):
                    for t in range(NT):
                        r, u = tile_rows(t), s * NT + t
                        if u >= 8:
                            pe.wait_ge(t_kept, u - 7)
                        pe.transpose(m.ps[:, u % 8, 0:r], srcs[s][0:r, t, :],
                                     m.const[0:r, C_ID:C_ID + r]).then_inc(turned, 1)

            @block.scalar
            def _(act):
                for s in range(3):
                    for t in range(NT):
                        r, u = tile_rows(t), s * NT + t
                        act.wait_ge(turned, u + 1)
                        act.copy(turned_in[s][:, t * P:t * P + r], m.ps[:, u % 8, 0:r]).then_inc(t_kept, 1)

            @block.vector
            def _(dve):
                dve.tensor_copy(iota2[:], iota.unsqueeze(2).broadcast_to([P, NK, G8]))

        GROUPS = TBG // G8
        with nc.Block() as block:

            def all_groups(eng, group):
                group(0, True, 0)
                group(1, True, 1)
                with eng.Fori(1, T // G8 // 2) as i:
                    group(2 * i, False, 0)
                    group(2 * i + 1, False, 1)

            @block.vector
            def _(dve):
                def group(g, first, q):
                    cols = bass.ds(G8 * g, G8)
                    if not first:
                        dve.wait_ge(weighted, g - 1)
                        dve.wait_ge(last_weighted, g - 1)
                    dve.tensor_tensor(hot2[:, q], iota2[:], key2[:, cols].unsqueeze(1).broadcast_to([P, NK, G8]),
                                      ALU.is_equal).then_inc(hot2_made, 1)
                    if not first:
                        dve.wait_ge(used, 2 * (g - 1))
                    dve.tensor_tensor(hot1[:, q], iota.unsqueeze(1).broadcast_to([P, G8, NK]),
                                      key1[:, cols].unsqueeze(2).broadcast_to([P, G8, NK]),
                                      ALU.is_equal).then_inc(hot1_made, 1)

                all_groups(dve, group)

            @block.gpsimd
            def _(pool):
                def group(g, first, q):
                    cols = bass.ds(G8 * g, G8 - 2)
                    pool.wait_ge(hot2_made, g + 1)
                    if not first:
                        pool.wait_ge(used, 2 * (g - 1))
                    pool.tensor_tensor(wgt[:, q, 0:G8 - 2], hot2[:, q, :, 0:G8 - 2].rearrange("p n t -> p t n"),
                                       gate[:, cols].unsqueeze(2).broadcast_to([P, G8 - 2, NK]),
                                       ALU.mult).then_inc(weighted, 1)

                all_groups(pool, group)

            @block.tensor
            def _(pe):
                def group(g, first, q):
                    pe.wait_ge(hot1_made, g + 1)
                    pe.wait_ge(weighted, g + 1)
                    pe.wait_ge(last_weighted, g + 1)
                    for b in range(2):
                        if not first:
                            pe.wait_ge(copied, 2 * (g - 2) + b + 1)
                        for i in range(4):
                            mm = pe.matmul(m.ps[:, 2 * q + b, i * P:i * P + P], hot1[:, q, 4 * b + i, :],
                                           wgt[:, q, 4 * b + i, :], start=True, stop=True)
                        mm.then_inc(used, 1)

                all_groups(pe, group)

            @block.scalar
            def _(act):
                def weigh(g, q):
                    act.wait_ge(hot2_made, g + 1)
                    for i in (G8 - 2, G8 - 1):
                        ins = act.activation(wgt[:, q, i], hot2[:, q, :, i], ACT.Copy,
                                             scale=gate[:, bass.ds(G8 * g + i, 1)])
                    ins.then_inc(last_weighted, 1)

                def copy_out(blk, i, q):
                    for bank in (2 * q, 2 * q + 1):
                        u = 4 * i + bank
                        act.wait_ge(used, u + (2 * blk * GROUPS + 1))
                        act.copy(out[:, blk % 2, :, bass.ds(4 * u, 4)].rearrange("p n t -> p t n"),
                                 m.ps[:, bank, :].rearrange("p (t n) -> p t n", t=4)).then_inc(copied, 1)

                weigh(0, 0)
                for blk in range(T // TBG):
                    if blk >= 2:
                        act.wait_ge(stored[blk % 2], 16 * (blk // 2))
                    last = blk == T // TBG - 1
                    with act.Fori(0, GROUPS // 2 - last) as i:
                        weigh(2 * i + (blk * GROUPS + 1), 1)
                        copy_out(blk, i, 0)
                        weigh(2 * i + (blk * GROUPS + 2), 0)
                        copy_out(blk, i, 1)
                    if last:
                        weigh(T // G8 - 1, 1)
                        for q in range(2):
                            copy_out(blk, GROUPS // 2 - 1, q)

            @block.sync
            def _(sp):
                for blk in range(T // TBG):
                    sp.wait_ge(copied, 2 * GROUPS * (blk + 1))
                    sp.dma_start(d["gates"][blk], out[:, blk % 2]).then_inc(stored[blk % 2], 16)
                for i in range(2):
                    sp.wait_ge(stored[i], 16 * (T // TBG // 2))


def run_kept_experts(nc, m, d, sem):
    GROUPS = KEPT // GR
    with ExitStack() as ctx:
        def sb(name, shape, dt=F32):
            return ctx.enter_context(nc.sbuf_tensor(name, shape, dt))

        v_raw = [m.xn[:, 4 * i:4 * i + 4, T:TM] for i in range(GR)]
        v = (sb("k_v_high", [P, 2, GR, D], F32R), sb("k_v_low", [P, 2, GR, D], F32R))
        gates = sb("k_g", [P, 2, T // TBG, GR, TBG])
        act = sb("k_act", [P, GR, T])
        split = (sb("k_act_high", [P, 2, GR, T], F32R), sb("k_act_low", [P, 2, GR, T], F32R))
        a_loaded, v_loaded, g_loaded = ([sem(f"k_{w}_loaded{i}") for i in range(2)] for w in "avg")
        gated, act_high, act_low, v_high, v_low, multiplied, added = (
            sem(f"k_{x}") for x in ("gated", "act_high", "act_low", "v_high", "v_low", "multiplied", "added"))
        with nc.Block() as block:

            @block.sync
            def _(sp):
                for g in range(GROUPS):
                    if g >= 2:
                        sp.wait_ge(gated, GR * (g - 1))
                    src = bass.AP(tensor=d["gates"].tensor, offset=g * GR * TBG,
                                  ap=[[NK * TBG, P], [NK * NK * TBG, T // TBG], [1, GR * TBG]])
                    sp.dma_start(gates[:, g % 2].rearrange("p b i t -> p b (i t)"), src).then_inc(g_loaded[g % 2], 16)
                    for i in range(GR):
                        n = GR * g + i
                        if n >= 2:
                            sp.wait_ge(act_low, n - 1)
                        sp.dma_start(act[:, i], d["kept"][n]).then_inc(a_loaded[i], 16)
                        if n >= 2:
                            sp.wait_ge(v_low, n - 1)
                        sp.dma_start(v_raw[i], d["v"][n].rearrange("p (k e) -> p k e", k=4)).then_inc(v_loaded[i], 16)

            @block.gpsimd
            def _(pool):
                for g in range(GROUPS):
                    pool.wait_ge(g_loaded[g % 2], 16 * (g // 2 + 1))
                    for i in range(GR):
                        pool.wait_ge(a_loaded[i], 16 * (g + 1))
                        x = act[:, i].rearrange("p (b t) -> p b t", t=TBG)
                        pool.tensor_tensor(x, x, gates[:, g % 2, :, i], ALU.mult).then_inc(gated, 1)

            @block.scalar
            def _(sc):
                for g in range(GROUPS):
                    if g >= 2:
                        sc.wait_ge(multiplied, 24 * (g - 1))
                    for i in range(GR):
                        sc.wait_ge(v_loaded[i], 16 * (g + 1))
                        sc.copy(v[0][:, g % 2, i].rearrange("p (k e) -> p k e", k=4), v_raw[i]).then_inc(v_high, 1)
                        sc.wait_ge(gated, GR * g + i + 1)
                        sc.copy(split[0][:, g % 2, i], act[:, i]).then_inc(act_high, 1)

            @block.tensor
            def _(pe):
                for g in range(GROUPS):
                    pe.wait_ge(v_low, GR * g + GR)
                    pe.wait_ge(act_low, GR * g + GR)
                    for x in range(24):
                        j, (a, z) = x // 3, CHUNKS[x % 3]
                        if 24 * g + x >= 8:
                            pe.wait_ge(added, 24 * g + x - 7)
                        for i in range(GR):
                            mm = exact_product(pe, m.ps[:, x % 8, 0:CH], [y[:, g % 2, i, j * P:j * P + P] for y in v],
                                               [y[:, g % 2, i, a:z] for y in split], i == 0, i == GR - 1)
                        mm.then_inc(multiplied, 1)

            @block.vector
            def _(dve):
                def rest(n):
                    p, i = n // GR % 2, n % GR
                    dve.wait_ge(v_high, n + 1)
                    dve.tensor_tensor(v[1][:, p, i].rearrange("p (k e) -> p k e", k=4), v_raw[i],
                                      v[0][:, p, i].bitcast(F32).rearrange("p (k e) -> p k e", k=4),
                                      ALU.subtract).then_inc(v_low, 1)
                    dve.wait_ge(act_high, n + 1)
                    dve.tensor_tensor(split[1][:, p, i], act[:, i], split[0][:, p, i].bitcast(F32),
                                      ALU.subtract).then_inc(act_low, 1)

                for n in range(GR):
                    rest(n)
                for g in range(GROUPS):
                    for x in range(24):
                        if g + 1 < GROUPS and x in (4, 12):
                            rest(GR * (g + 1) + x // 12)
                        j, (a, z) = x // 3, CHUNKS[x % 3]
                        dve.wait_ge(multiplied, 24 * g + x + 1)
                        dve.tensor_tensor(m.x2[:, j, a:z], m.x2[:, j, a:z], m.ps[:, x % 8, 0:CH], ALU.add).then_inc(added, 1)


def run_experts(nc, m, d, sem):
    START = KEPT // GR
    LAST = NK // GR - START - 1
    with ExitStack() as ctx:
        def sb(name, shape, dt=F32):
            return ctx.enter_context(nc.sbuf_tensor(name, shape, dt))

        u_raw = sb("x_u", [P, KT, P])
        u = (sb("x_u_high", [P, GR, KT, P], F32R), sb("x_u_low", [P, GR, KT, P], F32R))
        v_raw = [m.xn[:, 4 * i:4 * i + 4, T:TM] for i in range(GR)]
        v = (sb("x_v_high", [P, GR, D], F32R), sb("x_v_low", [P, GR, D], F32R))
        gates = sb("x_g", [P, T // TBG, GR, TBG])
        act = sb("x_act", [P, GR, T])
        split = (sb("x_act_high", [P, 2, GR, T], F32R), sb("x_act_low", [P, 2, GR, T], F32R))
        u_loaded, g_loaded = sem("x_u_loaded"), sem("x_g_loaded")
        v_loaded = [sem(f"x_v_loaded{i}") for i in range(GR)]
        hidden, gelu_done, gated, act_high, act_low, u_high, u_low, v_high, v_low, multiplied, added = (
            sem(f"x_{x}") for x in ("hidden", "gelu", "gated", "act_high", "act_low", "u_high", "u_low", "v_high",
                                    "v_low", "multiplied", "added"))

        def all_groups(eng, group):
            group(0, 0, True, False, False)
            group(1, 1, False, True, False)
            with eng.Fori(1, LAST // 2) as i:
                group(2 * i, 0, False, False, False)
                group(2 * i + 1, 1, False, False, False)
            group(LAST - 1, 0, False, False, False)
            group(LAST, 1, False, False, True)

        with nc.Block() as block:

            @block.sync
            def _(sp):
                def load_v(n, i, early):
                    if not early:
                        sp.wait_ge(v_low, n - 1)
                    sp.dma_start(v_raw[i], d["v"][bass.ds(n + KEPT, 1)].rearrange("o p (k e) -> p (o k) e", k=4)).then_inc(v_loaded[i], 16)

                def group(g, p, first, second, last):
                    for i in range(GR):
                        n = g * GR + i
                        if not (first and i == 0):
                            sp.wait_ge(u_low, n)
                        sp.dma_start(u_raw[:], d["u"][bass.ds(n + KEPT, 1)].rearrange("o p k n -> p (o k) n")).then_inc(u_loaded, 16)
                        if i == 0:
                            if not first:
                                sp.wait_ge(gated, GR * g)
                            src = bass.AP(tensor=d["gates"].tensor, offset=g * (GR * TBG) + KEPT * TBG,
                                          ap=[[NK * TBG, P], [NK * NK * TBG, T // TBG], [1, GR * TBG]])
                            sp.dma_start(gates[:].rearrange("p b i t -> p b (i t)"), src).then_inc(g_loaded, 16)
                        if not (first and i == 0):
                            load_v(n - 1, 1 - i, first or (second and i == 0))

                all_groups(sp, group)
                load_v(GR * LAST + 1, 1, False)

            @block.tensor
            def _(pe):
                def hidden_products(g, first):
                    for i in range(GR):
                        n = g * GR + i
                        pe.wait_ge(u_low, n + 1)
                        if not first:
                            pe.wait_ge(gelu_done, 3 * (n - 1))
                        for c, (a, z) in enumerate(CHUNKS):
                            for k in range(KT):
                                mm = exact_product(pe, m.ps[:, 3 * i + c, 0:CH], [x[:, i, k, :] for x in u],
                                                   [x[:, k, a:z] for x in m.hn], k == 0, k == KT - 1)
                            mm.then_inc(hidden, 1)

                def output_products(g, p, first):
                    pe.wait_ge(v_low, GR * g + GR)
                    pe.wait_ge(act_low, GR * g + GR)
                    for x in range(24):
                        j, c = x // 3, x % 3
                        a, z = CHUNKS[c]
                        if not (first and x < 2):
                            pe.wait_ge(added, 24 * g + x - 1)
                        for i in range(GR):
                            mm = exact_product(pe, m.ps[:, 6 + x % 2, 0:CH], [y[:, i, j * P:j * P + P] for y in v],
                                               [y[:, p, i, a:z] for y in split], i == 0, i == GR - 1)
                        mm.then_inc(multiplied, 1)

                hidden_products(0, True)
                hidden_products(1, False)
                output_products(0, 0, True)
                with pe.Fori(1, (LAST + 1) // 2) as i:
                    hidden_products(2 * i, False)
                    output_products(2 * i - 1, 1, False)
                    hidden_products(2 * i + 1, False)
                    output_products(2 * i, 0, False)
                output_products(LAST, 1, False)

            @block.scalar
            def _(sc):
                def round_u(n, i, first=False):
                    sc.wait_ge(u_loaded, 16 * (n + 1))
                    if not first:
                        sc.wait_ge(hidden, 3 * (n - 1))
                    sc.copy(u[0][:, i], u_raw[:]).then_inc(u_high, 1)

                def round_act(g, p, i, early):
                    sc.wait_ge(gated, GR * g + i + 1)
                    if not early:
                        sc.wait_ge(multiplied, 24 * (g - 1))
                    sc.copy(split[0][:, p, i], act[:, i]).then_inc(act_high, 1)

                def round_v(g, i, first):
                    sc.wait_ge(v_loaded[i], 16 * (g + 1))
                    if not first:
                        sc.wait_ge(multiplied, 24 * g)
                    sc.copy(v[0][:, i].rearrange("p (k e) -> p k e", k=4), v_raw[i]).then_inc(v_high, 1)

                def gelu(n, i, first):
                    if not first:
                        sc.wait_ge(act_low, n - 1)
                    for c, (a, z) in enumerate(CHUNKS):
                        sc.wait_ge(hidden, 3 * n + c + 1)
                        sc.activation(act[:, i, a:z], m.ps[:, 3 * i + c, 0:CH], ACT.Gelu).then_inc(gelu_done, 1)

                def group(g, p, first, second, last):
                    n = GR * g
                    round_u(n + 1, 1, first)
                    if not first:
                        round_act(g - 1, 1 - p, 1, second)
                        round_v(g - 1, 0, second)
                    gelu(n, 0, first)
                    if not last:
                        round_u(n + 2, 0)
                    round_act(g, p, 0, first or second)
                    if not first:
                        round_v(g - 1, 1, second)
                    gelu(n + 1, 1, first)

                round_u(0, 0, True)
                all_groups(sc, group)
                round_act(LAST, LAST % 2, 1, False)
                for i in range(GR):
                    round_v(LAST, i, False)

            @block.gpsimd
            def _(pool):
                def group(g):
                    pool.wait_ge(g_loaded, 16 * (g + 1))
                    for i in range(GR):
                        pool.wait_ge(gelu_done, 3 * (g * GR + i) + 3)
                        x = act[:, i].rearrange("p (b t) -> p b t", t=TBG)
                        pool.tensor_tensor(x, x, gates[:, :, i], ALU.mult).then_inc(gated, 1)

                with pool.Fori(0, LAST + 1) as g:
                    group(g)

            @block.vector
            def _(dve):
                def rest_u(n, i):
                    dve.wait_ge(u_high, n + 1)
                    dve.tensor_tensor(u[1][:, i], u_raw[:], u[0][:, i].bitcast(F32), ALU.subtract).then_inc(u_low, 1)

                def rest_act(g, p, i):
                    dve.wait_ge(act_high, GR * g + i + 1)
                    dve.tensor_tensor(split[1][:, p, i], act[:, i], split[0][:, p, i].bitcast(F32),
                                      ALU.subtract).then_inc(act_low, 1)

                def rest_v(g, i):
                    dve.wait_ge(v_high, GR * g + i + 1)
                    dve.tensor_tensor(v[1][:, i].rearrange("p (k e) -> p k e", k=4), v_raw[i],
                                      v[0][:, i].bitcast(F32).rearrange("p (k e) -> p k e", k=4),
                                      ALU.subtract).then_inc(v_low, 1)

                def add_outputs(g):
                    for x in range(24):
                        j, c = x // 3, x % 3
                        a, z = CHUNKS[c]
                        dve.wait_ge(multiplied, 24 * g + x + 1)
                        dve.tensor_tensor(m.x2[:, j, a:z], m.x2[:, j, a:z], m.ps[:, 6 + x % 2, 0:CH], ALU.add).then_inc(added, 1)

                def group(g, p, first, second, last):
                    n = GR * g
                    rest_u(n + 1, 1)
                    if not first:
                        rest_act(g - 1, 1 - p, 1)
                        rest_v(g - 1, 0)
                    if not last:
                        rest_u(n + 2, 0)
                    rest_act(g, p, 0)
                    if not first:
                        rest_v(g - 1, 1)
                        add_outputs(g - 1)

                rest_u(0, 0)
                all_groups(dve, group)
                rest_act(LAST, LAST % 2, 1)
                for i in range(GR):
                    rest_v(LAST, i)
                add_outputs(LAST)


def store_output(nc, m, d, sem):
    out = sem("y_stored")
    with nc.Block() as block:

        @block.sync
        def _(sp):
            sp.dma_start(d["out_y"], m.x2[:]).then_inc(out, 16)
            sp.wait_ge(out, 16)
            sp.wait_ge(m.stored, m.stores)


def build(nc, d, until=99):
    with ExitStack() as ctx:
        m = Mem()
        signals, handles = ExitStack(), []

        def sem(name):
            handles.append(signals.enter_context(nc.semaphore(name)))
            return handles[-1]

        def clear_semaphores():
            with nc.Block() as block:

                @block.sync
                def _(sp):
                    for x in handles:
                        sp.sem_clear(x)

            signals.close()
            handles.clear()

        def sb(stack, name, shape, dt=F32):
            return stack.enter_context(nc.sbuf_tensor(name, shape, dt))

        def next_place():
            return (nc.sbuf_base + 31) // 32 * 32

        def over(name, shape, first, skip=0):
            return nc.alloc_sbuf_tensor_at(name, shape, F32R, offset=first + skip)

        m.ps = ctx.enter_context(nc.psum_tensor("ps", [P, 8, 512], F32))
        m.const, m.ones = sb(ctx, "const", [P, C_END]), sb(ctx, "ones", [P, P])
        m.norm2 = sb(ctx, "norm2", [P, KT])
        m.eps, m.one = sb(ctx, "eps", [P, 1]), sb(ctx, "one", [P, 1])
        xn_at = next_place()
        m.xn = sb(ctx, "xn", [P, KT, TM])
        m.x2 = m.xn[:, :, 0:T]
        m.x_low = over("x_low", [P, KT, TM], xn_at)[:, :, 0:T]
        m.stored = ctx.enter_context(nc.semaphore("stored"))
        m.stores = 16 * (1 + 1 + NB + 1 + 2 + 1 + 1)
        with ExitStack() as mix:
            m.norm1, m.memg = sb(mix, "norm1", [P, KT]), sb(mix, "memg", [P, KT])
            m.qg, m.kg, m.cqg, m.ckg, m.gng = (sb(mix, x, [P, 1]) for x in ("qg", "kg", "cqg", "ckg", "gng"))
            m.gbias = sb(mix, "gbias", [P, 2])
            m.gates_b = sb(mix, "gates_b", [P, KT, 3])
            m.sink, m.sink_s = sb(mix, "sink", [P, 8]), sb(mix, "sink_s", [P, 2])
            m.relb, m.w2 = sb(mix, "relb", [32, 8]), sb(mix, "w2", [16, 256])
            f_at = next_place()
            m.f = sb(mix, "features", [P, NF, T])
            load_small(nc, m, d, sem)
            m.w_spare = [over(f"w_spare{i}", [P, 2, KT, P], f_at, 4 * (KA * T + 2 * D * i)) for i in range(2)]
            m.wb_spare = [over(f"wb_spare{i}", [P, KT, 512], f_at, 4 * (RB * T + 4 * D * i)) for i in range(2)]
            with ExitStack() as values:
                m.av, m.bv = sb(values, "av", [P, NT, P]), sb(values, "bv", [P, NT, 512])
                m.lr = sb(values, "lr", [16, T])
                with ExitStack() as memory:
                    m.mk, m.mv = sb(memory, "mk", [P, 4, NMEM]), sb(memory, "mv", [P, 2, 512])
                    with ExitStack() as halves:
                        m.x_high = sb(halves, "x_high", [P, KT, T], F32R)
                        norm_features(nc, m, d, sem)
                        project_memory(nc, m, d, sem)
                        project(nc, m, d, sem)
                        norm_heads(nc, m, d, sem)
                    if until == 3:
                        return m
                    attend_prompt(nc, m, sem, windowed=False)
                    attend_memory_samples(nc, m, d, sem)
                with ExitStack() as window:
                    m.bias = sb(window, "bias", [P, 2, 4, 256])
                    m.bias_s = sb(window, "bias_s", [P, 2, WK])
                    bias_by_distance(nc, m, d, sem)
                    attend_prompt(nc, m, sem, windowed=True)
                    attend_window_samples(nc, m, d, sem)
                with ExitStack() as gla:
                    g = Mem()
                    g.b, g.aq, g.kl = (sb(gla, x, [P, 2, T]) for x in ("gla_b", "gla_aq", "gla_kl"))
                    g.el = sb(gla, "gla_el", [P, 2, TP // GC + NB])
                    prepare_gla(nc, m, g, d, sem)
                    g.kt = sb(gla, "gla_kt", [P, NT, 256])
                    turn_keys(nc, m, g, sem)
                    gla_prompt(nc, m, g, d, sem)
                    gla_samples(nc, m, g, d, sem)
                    finish_gla(nc, m, g, d, sem)
            if until == 6:
                return m
            h_at = next_place()
            m.h = sb(mix, "merged", [P, KT, T])
            m.h_low = over("merged_low", [P, KT, T], h_at)
            m.x_high = sb(mix, "x_high_again", [P, KT, T], F32R)
            merge(nc, m, d, sem)
            project_out(nc, m, d, sem)
        clear_semaphores()
        if until == 7:
            return m
        with ExitStack() as peer:
            m.hn = (sb(peer, "hn_high", [P, KT, T], F32R), sb(peer, "hn_low", [P, KT, T], F32R))
            norm_and_split(nc, m, sem)
            with ExitStack() as chosen:
                m.e1, m.e2, m.gate = (sb(chosen, x, [P, NT, HEADS * TOPK]) for x in ("e1", "e2", "gate"))
                choose_experts(nc, m, d, sem)
                if until == 9:
                    return m
                build_gate_matrix(nc, m, d, sem)
            run_kept_experts(nc, m, d, sem)
            run_experts(nc, m, d, sem)
        store_output(nc, m, d, sem)
        signals.close()


def constants():
    import math

    import numpy as np

    c = np.zeros((P, C_END), np.float32)
    r = np.arange(P)
    c[:, C_ID:C_ID + P] = np.eye(P)
    c[:, C_BLK:C_BLK + P] = r[:, None] // 64 == r[None, :] // 64
    c[:, C_IOTA:C_IOTA + P] = r[None, :]
    c[:, C_TRI:C_TRI + GC] = r[:, None] % GC <= np.arange(GC)[None, :]
    i = np.arange(32)
    c[0:32, C_TRIS:C_TRIS + 32] = (i[:, None] // TS == i[None, :] // TS) & (i[:, None] <= i[None, :])
    own = (r[:, None] % 32) // TS == np.arange(NB)[None, :]
    c[:, C_OWN:C_OWN + NB] = np.where(own, 0.0, NEG)
    c[:, C_SEL:C_SEL + NB] = own
    dist = WIN - 1 - np.arange(WIN)
    exact = 16
    large = exact + (np.log(np.maximum(dist, 1).astype(np.float32) / np.float32(exact))
                     / np.float32(math.log(128 / exact)) * np.float32(32 - exact)).astype(np.int32)
    bucket = np.where(dist < exact, dist, np.minimum(large, 31))
    c[0:32, C_HOT:C_HOT + WIN] = np.arange(32)[:, None] == bucket[None, :]
    t = np.arange(T)
    scan = np.where(t < TP, t % GC != 0, (t - TP) % TS != 0).astype(np.float32)[None, :]
    return c, scan


def head_picks():
    import numpy as np

    gather = np.zeros((P, HTILES, HROWS), np.float32)
    head = 0
    for tile in range(HTILES):
        size = 64 if tile < 5 else P
        for a in range(0, P, size):
            gather[a:a + size, tile, head] = 1.0 / size
            head += 1
    return gather, np.ascontiguousarray((gather > 0).transpose(2, 1, 0).astype(np.float32))


def lay_out(x):
    import numpy as np

    c = np.ascontiguousarray
    a = {}
    rows = np.concatenate([x["x_prompt"][0], x["x_sample"].reshape(NB * TS, D), x["mem_prompt"][0]])
    a["x"] = c(rows.T.reshape(KT, P, TM).transpose(1, 0, 2))
    w = x["w_in"][0]
    sizes = [512, 128, 128, 256, 256, 512, 16, 512, 512, 3072]
    at = np.concatenate([[0], np.cumsum(sizes)])
    aq, ak, av, bq, bk, bv, lr, br, cq, gl = (w[:, at[i]:at[i + 1]] for i in range(10))
    pair = [0, 4, 1, 5, 2, 6, 3, 7]
    aq = aq.reshape(D, 8, 64)[:, pair].reshape(D, 512)

    def tiles(y):
        return y.reshape(y.shape[0] // P, P, y.shape[1] // P, P).transpose(2, 1, 0, 3)

    a["w_f"] = c(tiles(np.concatenate([aq, ak, bq, bk, br, cq], axis=1)))
    a["w_lr"] = np.zeros((P, KT, P), np.float32)
    a["w_lr"][:, :, 0:16] = lr.reshape(KT, P, 16).transpose(1, 0, 2)
    a["w_av"] = c(av.reshape(KT, P, P).transpose(1, 0, 2))
    a["w_bv"] = c(bv.reshape(4, 2, P, 4, P).transpose(0, 2, 1, 3, 4).reshape(4, P, KT, P))
    mk, mv = x["w_mem_kv"][0][:, 0:512], x["w_mem_kv"][0][:, 512:1024]
    a["w_mk"] = c(tiles(mk).transpose(1, 0, 2, 3))
    a["w_mv"] = c(mv.reshape(KT, P, 512).transpose(1, 0, 2))
    wa = x["w_br_a"][0].reshape(8, 64, D)[pair].reshape(512, D)
    gates = gl.reshape(KT, P, 3, KT, P).transpose(3, 1, 2, 0, 4).reshape(KT, P, 24, P)
    br = np.stack([wa, x["w_br_b"][0], x["w_br_c"][0]])
    br = br.reshape(3, 4, P, KT, P).transpose(3, 2, 0, 1, 4).reshape(KT, P, 12, P)
    a["w_m"] = c(np.concatenate([gates, br], axis=2))
    a["w_out"] = c(tiles(x["w_out"][0]))
    a["w_q"] = c(tiles(x["peer_wq"][0]))
    a["keys"] = c(np.stack([x["peer_k1"][0].T, x["peer_k2"][0].T], axis=1))
    a["u"] = c(x["peer_u"][0].reshape(NK, NK, KT, P).transpose(1, 3, 2, 0))
    a["v"] = c(x["peer_v"][0].reshape(NK, NK, D).transpose(1, 0, 2))
    for name in ("norm1_g", "norm2_g", "mem_norm_g"):
        a[name] = c(x[name][0].reshape(KT, P).T)
    for name in ("a_qnorm_g", "a_knorm_g", "c_qnorm_g", "c_knorm_g", "b_gn_g"):
        a[name] = c(x[name][0][:, None])
    a["b_gate_b"] = c(x["b_gate_b"][0].reshape(2, P).T)
    a["b_gates"] = c(x["b_gates"][0].reshape(3, KT, P).transpose(2, 1, 0))
    a["a_sinks"] = c(x["a_sinks"])
    a["rel_bias"] = c(x["rel_bias"])
    a["b_gate_w2"] = c(x["b_gate_w2"][0])
    a["win_k"] = c(x["cache_win_k"][0].reshape(NB, WIN, P).transpose(2, 0, 1))
    a["win_v"] = c(x["cache_win_v"][0].reshape(NB, WIN, P))
    a["mem_k"] = c(x["cache_mem_k"][0].transpose(2, 3, 0, 1).reshape(4, P, NB * NMEM))
    a["mem_v"] = c(x["cache_mem_v"][0].reshape(NB, NMEM, 512))
    a["state"] = c(x["state_gla"][0])
    a["const"], a["scan"] = constants()
    a["gather"], a["spread"] = head_picks()
    return a


OUTS = {
    "out_y": (P, KT, T), "out_wk": (P, WIN), "out_wv": (WIN, P), "out_sp": (P, 2, P), "out_mk": (P, 4, NMEM),
    "out_mv": (NMEM, 512), "out_wks": (P, NB, WIN), "out_wvs": (NB, WIN, P), "out_ss": (NB, 4, 64, P),
}
SCRATCH = {"skew": (8, P, EXT), "gates": (T // TBG, NK, NK, TBG), "kept": (KEPT, P, T)}


def declare(nc, arrays):
    t = {name: nc.dram_tensor(f"in_{name}", x.shape, F32, kind="ExternalInput").ap() for name, x in arrays.items()}
    t.update({name: nc.dram_tensor(name, shape, F32, kind="ExternalOutput").ap() for name, shape in OUTS.items()})
    t.update({name: nc.dram_tensor(name, shape, F32).ap() for name, shape in SCRATCH.items()})
    return t


def kernel(**inputs):
    import numpy as np

    import concourse.bacc as bacc
    from concourse.bass_utils import run_bass_kernel_spmd

    arrays = lay_out({k: np.asarray(v) for k, v in inputs.items()})
    nc = bacc.Bacc("TRN2", target_bir_lowering=False, num_devices=1)
    build(nc, declare(nc, arrays))
    r = run_bass_kernel_spmd(nc, [{f"in_{k}": v for k, v in arrays.items()}], core_ids=[0]).results[0]
    y = np.asarray(r["out_y"]).transpose(2, 1, 0).reshape(T, D)
    kv = (2, 64)
    return (
        np.ascontiguousarray(y[0:TP])[None],
        np.ascontiguousarray(y[TP:T]).reshape(NB, TS, D),
        np.ascontiguousarray(r["out_wk"].T).reshape(1, 1, WIN, *kv),
        r["out_wv"].reshape(1, 1, WIN, *kv),
        np.ascontiguousarray(r["out_sp"].reshape(2, 64, 2, P).transpose(2, 0, 1, 3)).reshape(1, 1, 4, 64, P),
        np.ascontiguousarray(r["out_mk"].transpose(2, 1, 0)).reshape(1, 1, NMEM, 4, P),
        r["out_mv"].reshape(1, 1, NMEM, 4, P),
        np.ascontiguousarray(r["out_wks"].transpose(1, 2, 0)).reshape(1, NB, WIN, *kv),
        r["out_wvs"].reshape(1, NB, WIN, *kv),
        r["out_ss"][None],
    )
```
